# Optimizing a Trainium2 kernel written in Bass

```python
import math
import jax, jax.numpy as jnp
from jax import lax
import numpy as np

D_MODEL = 1024
BATCH = 1
SEQ = 256
DEPTH = 1

GRID_W = 64
CTX_LEN = 256
N_MIXERS = 2
A_HEADS = 4
A_DK = 128
A_DV = 256
N_DIR = 2
CHUNK = 64
D_FF = 2816
EPS = 1e-6
A_PROJ = 2 * A_HEADS * A_DK + A_HEADS * A_DV + D_MODEL + 2 * N_DIR * A_HEADS
N_A = sum(1 for i in range(DEPTH) if i % N_MIXERS == 0)
N_B = DEPTH - N_A


def rmsnorm(x, g):
    xf = x.astype(jnp.float32)
    y = xf * lax.rsqrt(jnp.mean(xf * xf, axis=-1, keepdims=True) + EPS)
    return (y * g.astype(jnp.float32)).astype(x.dtype)

def modulate(x, g, shift, scale):
    return rmsnorm(x, g) * (1 + scale) + shift

def conv3(x, w, axis):
    pad = [(0, 0)] * x.ndim
    pad[axis] = (1, 1)
    xp = jnp.pad(x, pad)
    n = x.shape[axis]
    sl = lambda s: lax.slice_in_dim(xp, s, s + n, axis=axis)
    return sl(0) * w[0] + sl(1) * w[1] + sl(2) * w[2]

def mlstm_inputs(h, w_in, b_gate):
    bn, t, _ = h.shape
    p = h @ w_in
    o1 = A_HEADS * A_DK
    o2 = 2 * o1
    o3 = o2 + A_HEADS * A_DV
    o4 = o3 + D_MODEL
    heads = lambda a, d: a.reshape(bn, t, A_HEADS, d).transpose(0, 2, 1, 3).astype(jnp.float32)
    q = heads(p[..., :o1], A_DK)
    k = heads(p[..., o1:o2], A_DK) * (A_DK ** -0.5)
    v = heads(p[..., o2:o3], A_DV)
    o = p[..., o3:o4]
    gates = (p[..., o4:] + b_gate).astype(jnp.float32)
    gates = gates.reshape(bn, t, 2, N_DIR, A_HEADS).transpose(2, 3, 0, 4, 1)
    it = gates[0]
    lf = jax.nn.log_sigmoid(gates[1])
    return q, k, v, it, lf, o

def mlstm_chunk_scan(q, k, v, it, lf, state, emit):
    bn, nh, t, _ = q.shape
    nc = t // CHUNK
    chunks = lambda a: jnp.moveaxis(a.reshape(a.shape[:2] + (nc, CHUNK) + a.shape[3:]), 2, 0)
    xs = (chunks(q), chunks(k), chunks(v), chunks(it), chunks(lf))
    mask = jnp.tril(jnp.ones((CHUNK, CHUNK), dtype=bool))

    def body(carry, inp):
        cm, nv, m = carry
        qc, kc, vc, ic, fc = inp
        b = jnp.cumsum(fc, axis=-1)
        g = b[..., -1]
        a = g[..., None] - b + ic
        m_new = jnp.maximum(g + m, jnp.max(a, axis=-1))
        decay = jnp.exp(g + m - m_new)
        wa = jnp.exp(a - m_new[..., None])
        c_new = decay[..., None, None] * cm + jnp.einsum('bhsv,bhsd->bhvd', wa[..., None] * vc, kc)
        n_new = decay[..., None] * nv + jnp.einsum('bhs,bhsd->bhd', wa, kc)
        if not emit:
            return (c_new, n_new, m_new), None
        dmat = jnp.where(mask, b[..., :, None] - b[..., None, :] + ic[..., None, :], -jnp.inf)
        inter = b + m[..., None]
        m_t = jnp.maximum(inter, jnp.max(dmat, axis=-1))
        w = jnp.exp(dmat - m_t[..., None]) * jnp.einsum('bhtd,bhsd->bhts', qc, kc)
        wi = jnp.exp(inter - m_t)
        num = jnp.einsum('bhts,bhsv->bhtv', w, vc) + wi[..., None] * jnp.einsum('bhvd,bhtd->bhtv', cm, qc)
        den = jnp.sum(w, axis=-1) + wi * jnp.einsum('bhd,bhtd->bht', nv, qc)
        h = num / jnp.maximum(jnp.abs(den), jnp.exp(-m_t))[..., None]
        return (c_new, n_new, m_new), h

    state, hs = lax.scan(body, state, xs)
    if not emit:
        return None, state
    return jnp.moveaxis(hs, 0, 2).reshape(bn, nh, t, A_DV), state

def mlstm_readout(h, o, gain, w_out):
    bn, nh, t, dv = h.shape
    hn = h * lax.rsqrt(jnp.mean(h * h, axis=-1, keepdims=True) + EPS)
    hn = hn.transpose(0, 2, 1, 3).reshape(bn, t, nh * dv) * gain.astype(jnp.float32)
    y = hn * jax.nn.sigmoid(o.astype(jnp.float32))
    return y.astype(o.dtype) @ w_out

def mlstm_mixer(h_lat, h_ctx, w_in, b_gate, head_gain, w_out, emit_ctx):
    ql, kl, vl, il, fl, ol = mlstm_inputs(h_lat, w_in, b_gate)
    qc, kc, vc, ic, fc, oc = mlstm_inputs(h_ctx, w_in, b_gate)
    bn = h_lat.shape[0]
    s0 = (jnp.zeros((bn, A_HEADS, A_DV, A_DK), jnp.float32),
          jnp.zeros((bn, A_HEADS, A_DK), jnp.float32),
          jnp.zeros((bn, A_HEADS), jnp.float32))
    rq = lambda a: jnp.flip(a, axis=2)
    rg = lambda a: jnp.flip(a, axis=-1)
    hc_f, s_f = mlstm_chunk_scan(qc, kc, vc, ic[0], fc[0], s0, emit_ctx)
    hl_f, _ = mlstm_chunk_scan(ql, kl, vl, il[0], fl[0], s_f, True)
    hc_b, s_b = mlstm_chunk_scan(rq(qc), rq(kc), rq(vc), rg(ic[1]), rg(fc[1]), s0, emit_ctx)
    hl_b, _ = mlstm_chunk_scan(rq(ql), rq(kl), rq(vl), rg(il[1]), rg(fl[1]), s_b, True)
    y = mlstm_readout(hl_f + rq(hl_b), ol, head_gain, w_out)
    yc = mlstm_readout(hc_f + rq(hc_b), oc, head_gain, w_out) if emit_ctx else None
    return y, yc

def shortconv_mixer(h, w_in, w_conv, w_out, conv_fn):
    bg, cg, xv = jnp.split(h @ w_in, 3, axis=-1)
    return (bg * conv_fn(cg * xv, w_conv)) @ w_out

def conv_glu(h, w_up, w_conv, b_conv, w_down, conv_fn):
    gate, val = jnp.split(h @ w_up, 2, axis=-1)
    gate = conv_fn(gate, w_conv) + b_conv
    return (jax.nn.silu(gate) * val) @ w_down

def first_inputs(seed: int = 0) -> dict:
    key = jax.random.key(seed)
    ks = jax.random.split(key, 24)
    nrm = lambda k, s, sc: jax.random.normal(k, s, jnp.float32) * sc
    D = D_MODEL
    b_i = nrm(ks[10], (N_A, N_DIR, A_HEADS), 0.1)
    b_f = jnp.linspace(3.0, 6.0, A_HEADS, dtype=jnp.float32) + nrm(ks[11], (N_A, N_DIR, A_HEADS), 0.1)
    a_b_gate = jnp.stack([b_i, b_f], axis=1).reshape(N_A, 2 * N_DIR * A_HEADS)
    return {
        "x": nrm(ks[0], (BATCH, SEQ, D), 1.0),
        "c": nrm(ks[1], (BATCH, D), 1.0),
        "ctx": nrm(ks[2], (BATCH, CTX_LEN, D), 1.0),
        "c_ctx": nrm(ks[3], (D,), 1.0),
        "w_mod": nrm(ks[4], (DEPTH, D, 6 * D), 0.5 * D ** -0.5),
        "b_mod": nrm(ks[5], (DEPTH, 6 * D), 0.02),
        "g_mix": 1.0 + nrm(ks[6], (DEPTH, D), 0.05),
        "g_ffn": 1.0 + nrm(ks[7], (DEPTH, D), 0.05),
        "a_w_in": nrm(ks[8], (N_A, D, A_PROJ), D ** -0.5),
        "a_b_gate": a_b_gate,
        "a_head_gain": 1.0 + nrm(ks[9], (N_A, A_HEADS * A_DV), 0.05),
        "a_w_out": nrm(ks[12], (N_A, A_HEADS * A_DV, D), (A_HEADS * A_DV) ** -0.5),
        "b_w_in": nrm(ks[13], (N_B, D, 3 * D), D ** -0.5),
        "b_w_conv": nrm(ks[14], (N_B, 3, D), 3 ** -0.5),
        "b_w_out": nrm(ks[15], (N_B, D, D), D ** -0.5),
        "f_w_up": nrm(ks[16], (DEPTH, D, 2 * D_FF), D ** -0.5),
        "f_w_conv": nrm(ks[17], (DEPTH, 3, D_FF), 3 ** -0.5),
        "f_b_conv": nrm(ks[18], (DEPTH, D_FF), 0.02),
        "f_w_down": nrm(ks[19], (DEPTH, D_FF, D), D_FF ** -0.5),
        "g_final": 1.0 + nrm(ks[20], (D,), 0.05),
    }

def first_block(x, c, ctx, c_ctx, w_mod, b_mod, g_mix, g_ffn, a_w_in, a_b_gate, a_head_gain,
              a_w_out, b_w_in, b_w_conv, b_w_out, f_w_up, f_w_conv, f_b_conv, f_w_down, g_final):
    bn, t, d = x.shape
    rows = t // GRID_W
    lat_row_conv = lambda a, w: conv3(a.reshape(bn, rows, GRID_W, a.shape[-1]), w, 2).reshape(a.shape)
    lat_col_conv = lambda a, w: conv3(a.reshape(bn, rows, GRID_W, a.shape[-1]), w, 1).reshape(a.shape)
    seq_conv = lambda a, w: conv3(a, w, 1)
    rec_layers = [i for i in range(DEPTH) if i % N_MIXERS == 0]
    last_rec = max(rec_layers) if rec_layers else -1

    for i in range(DEPTH):
        j = i // N_MIXERS
        ctx_read = i <= last_rec
        ctx_live = i < last_rec
        mod = jax.nn.silu(c) @ w_mod[i] + b_mod[i]
        sh1, sc1, ga1, sh2, sc2, ga2 = [m[:, None, :] for m in jnp.split(mod, 6, axis=-1)]
        if ctx_read:
            mod_c = jax.nn.silu(c_ctx) @ w_mod[i] + b_mod[i]
            csh1, csc1, cga1, csh2, csc2, cga2 = jnp.split(mod_c, 6, axis=-1)
            hc = modulate(ctx, g_mix[i], csh1, csc1)
        hx = modulate(x, g_mix[i], sh1, sc1)
        if i % N_MIXERS == 0:
            y, yc = mlstm_mixer(hx, hc, a_w_in[j], a_b_gate[j], a_head_gain[j], a_w_out[j], ctx_live)
        else:
            y = shortconv_mixer(hx, b_w_in[j], b_w_conv[j], b_w_out[j], lat_row_conv)
            yc = shortconv_mixer(hc, b_w_in[j], b_w_conv[j], b_w_out[j], seq_conv) if ctx_live else None
        x = x + ga1 * y
        hx = modulate(x, g_ffn[i], sh2, sc2)
        x = x + ga2 * conv_glu(hx, f_w_up[i], f_w_conv[i], f_b_conv[i], f_w_down[i], lat_col_conv)
        if ctx_live:
            ctx = ctx + cga1 * yc
            hc = modulate(ctx, g_ffn[i], csh2, csc2)
            ctx = ctx + cga2 * conv_glu(hc, f_w_up[i], f_w_conv[i], f_b_conv[i], f_w_down[i], seq_conv)

    return rmsnorm(x, g_final)


DEPTH_2 = 2

N_A_LAYERS = DEPTH_2 // 2
N_B_LAYERS = DEPTH_2 - N_A_LAYERS
N_SUBLAYERS = 3
GLA_HEADS = 4
GLA_DK = D_MODEL // 2 // GLA_HEADS
GLA_DV = D_MODEL // GLA_HEADS
GLA_GATE_RANK = 16
GLA_TAU = 16.0
GLA_CHUNK = 64
MLA_HEADS = 8
QK_NOPE = 128
QK_ROPE = 64
V_HEAD = 128
KV_LORA = 256
Q_LORA = 384
ROPE_THETA = 10000.0
Q_BLOCK = 128
MAX_POS_OFFSET = 1024


def rmsnorm_2(x, g):
    xf = x.astype(jnp.float32)
    y = xf * lax.rsqrt(jnp.mean(xf * xf, axis=-1, keepdims=True) + EPS)
    return (y * g.astype(jnp.float32)).astype(x.dtype)

def swiglu(h, w_gu, w_down):
    gate, up = jnp.split(h @ w_gu, 2, axis=-1)
    return (jax.nn.silu(gate) * up) @ w_down

def sublayer(x, shift, scale, gate, g_pre, g_post, fn, res_weight):
    h = rmsnorm_2(x, g_pre) * (1 + scale[:, None, :]) + shift[:, None, :]
    return x + res_weight * gate[:, None, :] * rmsnorm_2(fn(h), g_post)

def rope_tables(positions):
    inv_freq = ROPE_THETA ** (-jnp.arange(0, QK_ROPE, 2, dtype=jnp.float32) / QK_ROPE)
    ang = positions.astype(jnp.float32)[..., None] * inv_freq
    return jnp.cos(ang), jnp.sin(ang)

def apply_rope(x, cos, sin):
    cos = cos.astype(x.dtype)
    sin = sin.astype(x.dtype)
    x1, x2 = jnp.split(x, 2, axis=-1)
    return jnp.concatenate([x1 * cos - x2 * sin, x1 * sin + x2 * cos], axis=-1)

def gla_chunked(q, k, v, log_a):
    B, S, H, DK = q.shape
    C = GLA_CHUNK
    N = S // C
    f32 = jnp.float32

    def chunks(t):
        return t.astype(f32).reshape(B, N, C, H, t.shape[-1]).transpose(0, 3, 1, 2, 4)

    q, k, v, log_a = chunks(q) * DK ** -0.5, chunks(k), chunks(v), chunks(log_a)
    b = jnp.cumsum(log_a, axis=3)
    b_last = b[:, :, :, -1:, :]
    q_dec = q * jnp.exp(b)
    k_dec = k * jnp.exp(-b)
    causal = jnp.tril(jnp.ones((C, C), dtype=bool))
    att = jnp.where(causal, jnp.einsum('bhnid,bhnjd->bhnij', q_dec, k_dec), 0.0)
    o_intra = jnp.einsum('bhnij,bhnjv->bhniv', att, v)
    upd = jnp.einsum('bhncd,bhncv->bhndv', k * jnp.exp(b_last - b), v)
    decay = jnp.exp(b_last[:, :, :, 0, :])

    def step(state, inp):
        dec, u = inp
        return dec[..., None] * state + u, state

    s0 = jnp.zeros((B, H, DK, v.shape[-1]), f32)
    _, states = lax.scan(step, s0, (jnp.moveaxis(decay, 2, 0), jnp.moveaxis(upd, 2, 0)))
    states = jnp.moveaxis(states, 0, 2)
    o = o_intra + jnp.einsum('bhncd,bhndv->bhncv', q_dec, states)
    return o.transpose(0, 2, 3, 1, 4).reshape(B, S, H, v.shape[-1])

def gla_mixer(h, w_in, w_gate_up, b_gate, g_out, w_out):
    B, S, _ = h.shape
    kd = GLA_HEADS * GLA_DK
    vd = GLA_HEADS * GLA_DV
    q, k, v, g_low, r = jnp.split(h @ w_in, [kd, 2 * kd, 2 * kd + vd, 2 * kd + vd + GLA_GATE_RANK], axis=-1)
    log_a = jax.nn.log_sigmoid((g_low @ w_gate_up + b_gate).astype(jnp.float32)) / GLA_TAU
    o = gla_chunked(q.reshape(B, S, GLA_HEADS, GLA_DK), k.reshape(B, S, GLA_HEADS, GLA_DK),
                    v.reshape(B, S, GLA_HEADS, GLA_DV), log_a.reshape(B, S, GLA_HEADS, GLA_DK))
    o = rmsnorm_2(o, g_out).astype(h.dtype).reshape(B, S, vd)
    return (o * jax.nn.silu(r)) @ w_out

def mla_shared_kv(h, w_kv_a, g_kv, w_kv_b, cos, sin):
    B, S, _ = h.shape
    c_kv, k_pe = jnp.split(h @ w_kv_a, [KV_LORA], axis=-1)
    c_kv = rmsnorm_2(c_kv, g_kv)
    k_rope = apply_rope(k_pe, cos, sin)
    kv = (c_kv @ w_kv_b).reshape(B, S, MLA_HEADS, QK_NOPE + V_HEAD)
    k_nope, v = jnp.split(kv, [QK_NOPE], axis=-1)
    return k_nope, k_rope, v

def mla_mixer(h, k_nope, k_rope, v, w_dq, g_q, w_uq, w_out, cos, sin):
    B, S, _ = h.shape
    c_q = rmsnorm_2(h @ w_dq, g_q)
    q = (c_q @ w_uq).reshape(B, S, MLA_HEADS, QK_NOPE + QK_ROPE)
    q_nope, q_rope = jnp.split(q, [QK_NOPE], axis=-1)
    q_rope = apply_rope(q_rope, cos[:, :, None, :], sin[:, :, None, :])
    scale = (QK_NOPE + QK_ROPE) ** -0.5
    nb = S // Q_BLOCK
    qn_blocks = q_nope.reshape(B, nb, Q_BLOCK, MLA_HEADS, QK_NOPE).transpose(1, 0, 2, 3, 4)
    qr_blocks = q_rope.reshape(B, nb, Q_BLOCK, MLA_HEADS, QK_ROPE).transpose(1, 0, 2, 3, 4)
    key_pos = jnp.arange(S)
    neg = jnp.finfo(jnp.float32).min

    def attend(args):
        qn, qr, blk = args
        s = (jnp.einsum('bqhd,bkhd->bhqk', qn, k_nope) +
             jnp.einsum('bqhr,bkr->bhqk', qr, k_rope)).astype(jnp.float32) * scale
        q_pos = blk * Q_BLOCK + jnp.arange(Q_BLOCK)
        s = jnp.where(key_pos[None, :] <= q_pos[:, None], s, neg)
        p = jax.nn.softmax(s, axis=-1).astype(v.dtype)
        return jnp.einsum('bhqk,bkhv->bqhv', p, v)

    o = lax.map(attend, (qn_blocks, qr_blocks, jnp.arange(nb)))
    o = o.transpose(1, 0, 2, 3, 4).reshape(B, S, MLA_HEADS * V_HEAD)
    return o @ w_out

def second_inputs(seed: int = 0) -> dict:
    key = jax.random.key(seed)
    ks = jax.random.split(key, 24)
    D = D_MODEL
    f32 = jnp.float32

    def w(k, shape, fan_in):
        return jax.random.normal(k, shape, f32) * fan_in ** -0.5

    def gain(k, shape):
        return 1.0 + 0.1 * jax.random.normal(k, shape, f32)

    def bias(k, shape):
        return 0.01 * jax.random.normal(k, shape, f32)

    gla_in_cols = 2 * GLA_HEADS * GLA_DK + 2 * GLA_HEADS * GLA_DV + GLA_GATE_RANK
    offsets = jax.random.randint(ks[2], (BATCH, 1), 0, MAX_POS_OFFSET, dtype=jnp.int32)
    return {
        'x': jax.random.normal(ks[0], (BATCH, SEQ, D), f32),
        'c': jax.random.normal(ks[1], (BATCH, D), f32),
        'positions': offsets + jnp.arange(SEQ, dtype=jnp.int32)[None, :],
        'cond_w': w(ks[3], (DEPTH_2, D, 3 * N_SUBLAYERS * D), D),
        'cond_b': bias(ks[4], (DEPTH_2, 3 * N_SUBLAYERS * D)),
        'norm_g': gain(ks[5], (DEPTH_2, N_SUBLAYERS, 2, D)),
        'ffn_w_gu': w(ks[6], (DEPTH_2, 2, D, 2 * D_FF), D),
        'ffn_w_down': w(ks[7], (DEPTH_2, 2, D_FF, D), D_FF),
        'gla_w_in': w(ks[8], (N_A_LAYERS, D, gla_in_cols), D),
        'gla_w_gate_up': w(ks[9], (N_A_LAYERS, GLA_GATE_RANK, GLA_HEADS * GLA_DK), GLA_GATE_RANK),
        'gla_b_gate': 0.1 * jax.random.normal(ks[10], (N_A_LAYERS, GLA_HEADS * GLA_DK), f32),
        'gla_g_out': gain(ks[11], (N_A_LAYERS, GLA_DV)),
        'gla_w_out': w(ks[12], (N_A_LAYERS, GLA_HEADS * GLA_DV, D), GLA_HEADS * GLA_DV),
        'kv_g_in': gain(ks[13], (D,)),
        'kv_cond_w': w(ks[14], (D, 2 * D), D),
        'kv_cond_b': bias(ks[15], (2 * D,)),
        'mla_w_kv_a': w(ks[16], (D, KV_LORA + QK_ROPE), D),
        'mla_g_kv': gain(ks[17], (KV_LORA,)),
        'mla_w_kv_b': w(ks[18], (KV_LORA, MLA_HEADS * (QK_NOPE + V_HEAD)), KV_LORA),
        'mla_w_dq': w(ks[19], (N_B_LAYERS, D, Q_LORA), D),
        'mla_g_q': gain(ks[20], (N_B_LAYERS, Q_LORA)),
        'mla_w_uq': w(ks[21], (N_B_LAYERS, Q_LORA, MLA_HEADS * (QK_NOPE + QK_ROPE)), Q_LORA),
        'mla_w_out': w(ks[22], (N_B_LAYERS, MLA_HEADS * V_HEAD, D), MLA_HEADS * V_HEAD),
    }

def second_block(x, c, positions, cond_w, cond_b, norm_g, ffn_w_gu, ffn_w_down,
              gla_w_in, gla_w_gate_up, gla_b_gate, gla_g_out, gla_w_out,
              kv_g_in, kv_cond_w, kv_cond_b, mla_w_kv_a, mla_g_kv, mla_w_kv_b,
              mla_w_dq, mla_g_q, mla_w_uq, mla_w_out):
    cos, sin = rope_tables(positions)
    c_act = jax.nn.silu(c)
    k_nope = k_rope = v_shared = None
    for layer in range(DEPTH_2):
        mods = jnp.split(c_act @ cond_w[layer] + cond_b[layer], 3 * N_SUBLAYERS, axis=-1)
        g = norm_g[layer]
        x = sublayer(x, mods[0], mods[1], mods[2], g[0, 0], g[0, 1],
                     lambda h: swiglu(h, ffn_w_gu[layer, 0], ffn_w_down[layer, 0]), 0.5)
        if layer < N_A_LAYERS:
            i = layer
            x = sublayer(x, mods[3], mods[4], mods[5], g[1, 0], g[1, 1],
                         lambda h: gla_mixer(h, gla_w_in[i], gla_w_gate_up[i], gla_b_gate[i],
                                             gla_g_out[i], gla_w_out[i]), 1.0)
        else:
            i = layer - N_A_LAYERS
            x = sublayer(x, mods[3], mods[4], mods[5], g[1, 0], g[1, 1],
                         lambda h: mla_mixer(h, k_nope, k_rope, v_shared, mla_w_dq[i], mla_g_q[i],
                                             mla_w_uq[i], mla_w_out[i], cos, sin), 1.0)
        x = sublayer(x, mods[6], mods[7], mods[8], g[2, 0], g[2, 1],
                     lambda h: swiglu(h, ffn_w_gu[layer, 1], ffn_w_down[layer, 1]), 0.5)
        if layer == N_A_LAYERS - 1:
            kv_shift, kv_scale = jnp.split(c_act @ kv_cond_w + kv_cond_b, 2, axis=-1)
            h_kv = rmsnorm_2(x, kv_g_in) * (1 + kv_scale[:, None, :]) + kv_shift[:, None, :]
            k_nope, k_rope, v_shared = mla_shared_kv(h_kv, mla_w_kv_a, mla_g_kv, mla_w_kv_b, cos, sin)
    return x


def setup_inputs(seed=0):
    out = dict(first_inputs(seed))
    for name, value in second_inputs(seed + 1).items():
        if name != "x":
            out[name + "_2"] = value
    return out


def reference(
    x, c, ctx, c_ctx, w_mod, b_mod, g_mix, g_ffn, a_w_in, a_b_gate, a_head_gain, a_w_out,
    b_w_in, b_w_conv, b_w_out, f_w_up, f_w_conv, f_b_conv, f_w_down, g_final, c_2, positions_2,
    cond_w_2, cond_b_2, norm_g_2, ffn_w_gu_2, ffn_w_down_2, gla_w_in_2, gla_w_gate_up_2,
    gla_b_gate_2, gla_g_out_2, gla_w_out_2, kv_g_in_2, kv_cond_w_2, kv_cond_b_2, mla_w_kv_a_2,
    mla_g_kv_2, mla_w_kv_b_2, mla_w_dq_2, mla_g_q_2, mla_w_uq_2, mla_w_out_2,
):
    x = first_block(
        x, c, ctx, c_ctx, w_mod, b_mod, g_mix, g_ffn, a_w_in, a_b_gate, a_head_gain, a_w_out,
        b_w_in, b_w_conv, b_w_out, f_w_up, f_w_conv, f_b_conv, f_w_down, g_final,
    )
    return second_block(
        x, c_2, positions_2, cond_w_2, cond_b_2, norm_g_2, ffn_w_gu_2, ffn_w_down_2, gla_w_in_2,
        gla_w_gate_up_2, gla_b_gate_2, gla_g_out_2, gla_w_out_2, kv_g_in_2, kv_cond_w_2,
        kv_cond_b_2, mla_w_kv_a_2, mla_g_kv_2, mla_w_kv_b_2, mla_w_dq_2, mla_g_q_2, mla_w_uq_2,
        mla_w_out_2,
    )


_drawn_inputs = setup_inputs


def setup_inputs(seed=0):
    import zlib

    import numpy as np

    out = dict(_drawn_inputs(seed))
    spreads = {}
    factors = {'g_ffn': 3.145,
     'a_head_gain': 5.197,
     'f_b_conv': 8.0,
     'kv_cond_b_2': 8.0,
     'mla_g_q_2': 3.983}
    for name, (base, spread) in spreads.items():
        noise = np.random.default_rng([zlib.crc32(name.encode()), seed]).standard_normal(out[name].shape)
        drawn = base * np.exp(spread * noise) if base else spread * noise
        out[name] = __import__('jax').numpy.asarray(drawn.astype(out[name].dtype))
    for name, factor in factors.items():
        out[name] = (out[name] * factor).astype(out[name].dtype)
    return out
```

```python
import concourse.bass as bass
from concourse import mybir
from contextlib import ExitStack
import numpy as np

D, SEQ, FF = 1024, 256, 2816
P = 128
DT = D // P
FT = FF // P
HEADS, DK, DV, CHUNK = 4, 128, 256, 64
MLA_HEADS, ROPE, Q_LORA = 8, 64, 384
EPS = 1e-6
TILES = 16
CW = TILES * P

FFN_CHUNKS = FT + FT // 2
C_LSTM = 0
C_FFN = [17, 50, 100, 133, 178]
C_GLA = 83
C_KV = 166
C_MLA = 170
N_CHUNKS = C_FFN[-1] + FFN_CHUNKS
M_COND = [48, 136]
M_KV = 120
N_MOD = 208
FIRST_MODS = 16
_names = [("g_mix", 8), ("g_ffn", 8), ("g_final", 8), ("gain", 8), ("cw0", FT), ("cw1", FT), ("cw2", FT),
          ("cb", FT), ("norm_g", 96), ("kv_g", 8), ("g_out", 2), ("b_gla", 4), ("g_kv", 2), ("g_q", 3),
          ("b_gate", 1), ("invf", 1)]
COL, _at = {}, N_MOD
for _n, _w in _names:
    COL[_n] = (_at, _w)
    _at += _w
N_COLS = _at
_names = [("ident", P), ("ones", P), ("sel", 8 * P), ("madd", 4 * SEQ), ("reset", SEQ),
          ("causal", SEQ), ("amask", 3 * P)]
CON, _at = {}, 0
for _n, _w in _names:
    CON[_n] = (_at, _w)
    _at += _w
N_CONST = _at


def build(nc, w_stream, w_first, m_stream, w_gup, xT, ctxT, c_cols, c_row, c2_row, cols_d, const_d,
          pos_d, out_d, stages=99):
    f32, f32r, i32 = mybir.dt.float32, mybir.dt.float32r, mybir.dt.int32
    ALU, ACT, AX = mybir.AluOpType, mybir.ActivationFunctionType, mybir.AxisListType
    LN_EXP = "natural_log_exp_and_others"
    NCH = {0: 0, 1: 17, 2: 50, 3: 83, 4: 100, 5: 133, 6: 166, 7: 178}.get(stages, N_CHUNKS)
    NMU = 32 + 40 * {0: 0, 1: 0, 2: 1, 3: 2, 4: 2, 5: 3}.get(stages, 4)
    XUP = {0: 0, 1: 8, 2: 24, 3: 32, 4: 40, 5: 48, 6: 56, 7: 64}.get(stages, 72)

    ctx = ExitStack()
    with ctx:
        def sb(name, shape, dt=f32):
            return ctx.enter_context(nc.sbuf_tensor(name, shape, dt))

        sems = {}

        def sem(name):
            if name not in sems:
                sems[name] = ctx.enter_context(nc.semaphore(name))
            return sems[name]

        raw = sb("raw", [P, 3, CW])
        whi = sb("whi", [P, 3, CW], f32r)
        wlo = sb("wlo", [P, 3, CW], f32r)
        mring = sb("mring", [P, 2, D])
        X = sb("X", [P, DT, SEQ])
        hhi = sb("hhi", [P, DT, SEQ], f32r)
        hlo = sb("hlo", [P, DT, SEQ], f32r)
        cb = sb("cb", [P, D])
        cols = sb("cols", [P, N_COLS])
        con = sb("con", [P, N_CONST])
        mod = sb("mod", [P, N_MOD])
        modc = sb("modc", [P, FIRST_MODS])
        ccol = sb("ccol", [P, DT, 2])
        scol = sb("scol", [P, DT, 2])
        coef = sb("coef", [P, 16, DT])
        eps = sb("eps", [P, 1])
        lnt = sb("lnt", [P, SEQ])
        rstd = sb("rstd", [P, 2, SEQ])
        T = sb("T", [P, 3, SEQ])
        SG = sb("SG", [P, 3, SEQ])
        CG = sb("CG", [P, SEQ])
        rd = sb("rd", [P, 2, SEQ])
        uc = sb("uc", [P, 4, 36])
        arena = sb("arena", [P, 68 * 256])
        base = nc.sbuf_base - 68 * 1024

        def at(name, kb, shape, dt=f32):
            return nc.alloc_sbuf_tensor_at(name, shape, dt, offset=base + int(kb * 1024))

        w0 = at("w0", 8, [P, 5, CW])
        hid_hi = at("hid_hi", 8, [P, FT, SEQ], f32r)
        hid_lo = at("hid_lo", 8 + FT, [P, FT, SEQ], f32r)
        XC = at("XC", 0, [P, DT, SEQ])
        H = at("H", 0, [P, DT, SEQ])
        chi = at("chi", 8, [P, DT, SEQ], f32r)
        OS = at("OS", 8, [P, DT, SEQ])
        clo = at("clo", 16, [P, DT, SEQ], f32r)
        EF = at("EF", 16, [P, 2, 4, SEQ])
        Q = at("Q", 24, [P, HEADS, SEQ])
        K = at("K", 28, [P, HEADS, 2 * SEQ])
        V = at("V", 36, [P, 4, D])
        GQ = at("GQ", 0, [P, HEADS, SEQ])
        GK = at("GK", 4, [P, HEADS, SEQ])
        LA = at("LA", 8, [P, HEADS, SEQ])
        LB = at("LB", 12, [P, HEADS, SEQ])
        EB = at("EB", 16, [P, HEADS, SEQ])
        EN = at("EN", 20, [P, HEADS, SEQ])
        GV = at("GV", 24, [P, 2, D])
        SR = at("SR", 32, [P, DT, SEQ])
        GKU = at("GKU", 40, [P, HEADS, SEQ])
        wgu = at("wgu", 44, [16, HEADS * DK])
        glow = at("glow", 46, [16, SEQ])
        ST = at("ST", 47, [P, 3, DV])
        att = at("att", 50, [P, 2, P])
        kut = at("kut", 51, [P, 2, P])
        KN = at("KN", 0, [P, MLA_HEADS, SEQ])
        VM = at("VM", 8, [P, 2, D])
        KR = at("KR", 16, [P, 2, SEQ])
        QN = at("QN", 18, [P, MLA_HEADS, SEQ])
        QR = at("QR", 26, [P, 2, 2, SEQ])
        KRM = at("KRM", 30, [P, 4, 2, SEQ])
        lhi = at("lhi", 38, [P, 3, SEQ], f32r)
        llo = at("llo", 41, [P, 3, SEQ], f32r)
        SC = at("SC", 44, [P, 2, 3 * P])
        PT = at("PT", 47, [P, 2, 3 * P])
        SQ = at("SQ", 52, [P, DT, SEQ])
        gf = at("gf", 54, [36, 512])
        ga = at("ga", 56, [36, 512])
        gb = at("gb", 58, [36, 512])
        XS = at("XS", 60, [P, DT, SEQ])
        g_all = at("g_all", 60, [P, 512])
        gi = at("gi", 62, [36, 512])
        ut = at("ut", 64, [36, 512])
        mt = at("mt", 66, [36, SEQ])
        th = at("th", 67, [36, SEQ])
        thb = SG[:, 0:2]
        mx = sb("mx", [P, 2, 2])
        sm = sb("sm", [P, 2, 2])

        bank = [ctx.enter_context(nc.psum_tensor(f"bank{b}", [P, 512], f32)) for b in range(8)]
        block = ctx.enter_context(nc.Block())

        def col(name, j=0, n=None):
            a, w = COL[name]
            return cols[:, a + j:a + j + (n or 1)]

        def cst(name):
            a, w = CON[name]
            return con[:, a:a + w]

        ident, ones = cst("ident"), cst("ones")

        s_raw = [sem(f"raw_loaded{j}") for j in range(3)]
        s_hi, s_lo, s_pe = sem("chunk_rounded"), sem("chunk_rest"), sem("chunk_used")
        s_mod = [sem(f"mod_loaded{j}") for j in range(2)]
        s_mused = sem("mod_used")

        def run(i, per):
            return 0 if i is None else i * per

        def act_split(act, c, i=None):
            if c >= NCH:
                return
            act.wait_ge(s_raw[c % 3], 16 * (c // 3 + 1) + run(i, 16))
            if c >= 3:
                act.wait_ge(s_pe, c - 2 + run(i, 3))
            nc.scalar.activation(whi[:, c % 3], raw[:, c % 3], ACT.Copy).then_inc(s_hi, 1)

        def dve_split(dve, c, i=None):
            if c >= NCH:
                return
            dve.wait_ge(s_hi, c + 1 + run(i, 3))
            nc.vector.tensor_tensor(wlo[:, c % 3], raw[:, c % 3], whi[:, c % 3].bitcast(f32),
                                    ALU.subtract).then_inc(s_lo, 1)

        def mm3(out, c, s, rhi, rlo, start):
            wh, wl = whi[:, c % 3, s * P:(s + 1) * P], wlo[:, c % 3, s * P:(s + 1) * P]
            nc.tensor.matmul(out, wh, rhi, start=start, stop=True, skip_group_check=True)
            nc.tensor.matmul(out, wh, rlo, start=False, stop=True, skip_group_check=True)
            return nc.tensor.matmul(out, wl, rhi, start=False, stop=True, skip_group_check=True)

        def mm(out, lhsT, rhs, start):
            return nc.tensor.matmul(out, lhsT, rhs, start=start, stop=True, skip_group_check=True)

        s_h = sem("input_tile_split")
        s_hhi = sem("input_tile_rounded")

        def pe_pair(pe, c, bk, hi=hhi, lo=hlo, last=True, wait=None):
            pe.wait_ge(s_lo, c + 1)
            for m in range(2):
                for k in range(DT):
                    if m == 0 and wait is not None:
                        pe.wait_ge(s_h, wait + k + 1)
                    ins = mm3(bank[bk][:, m * SEQ:(m + 1) * SEQ], c, m * DT + k, hi[:, k], lo[:, k], k == 0)
            if last:
                ins.then_inc(s_pe, 1)

        def pe_wide(pe, c, k0, outs, his, los):
            pe.wait_ge(s_lo, c + 1)
            for n, o in enumerate(outs):
                for g in range(4):
                    k = k0 + g
                    wh, wl = whi[:, c % 3, g * 512:(g + 1) * 512], wlo[:, c % 3, g * 512:(g + 1) * 512]
                    mm(o, his[n](k), wh, k == 0)
                    mm(o, his[n](k), wl, False)
                    ins = mm(o, los[n](k), wh, False)
            ins.then_inc(s_pe, 1)

        def pe_down_chunk(pe, c, khi, klo, first):
            for g in range(2):
                for m in range(DT):
                    ins = mm3(bank[m // 2][:, (m % 2) * SEQ:(m % 2 + 1) * SEQ], c, g * DT + m, khi[g], klo[g],
                              first and g == 0 and m % 2 == 0)
            ins.then_inc(s_pe, 1)

        def down(m):
            return bank[m // 2][:, (m % 2) * SEQ:(m % 2 + 1) * SEQ]

        s_sq, s_stat, s_rstd, s_ln = sem("squares"), sem("mean_square"), sem("rstd"), sem("log_mean_square")
        NORMS = ([8, 8] + [2] * 4 + [8, 8] + [8, 8] + [8] + [2] * 4 + [8] + [8, 8]
                 + [8, 8] + [8, 2] + [8, 3, 8] + [8, 8])
        N_CTX, N_X1, N_LSTM, N_F0, N_FIN, N_F1, N_GLA, N_GHEAD, N_GPOST, N_F2 = 0, 1, 2, 6, 7, 8, 10, 11, 15, 16
        N_F3, N_KV, N_KVL, N_MLA, N_QL, N_MPOST, N_F4 = 18, 20, 21, 22, 23, 24, 25

        def act_squares(act, n, src, wait=None):
            for j in range(NORMS[n]):
                if wait is not None:
                    act.wait_ge(*wait(j))
                if n and j == 0:
                    act.wait_ge(s_stat, n)
                nc.scalar.activation(SQ[:, j], src(j), ACT.Square).then_inc(s_sq, 1)

        def pe_stat(pe, n):
            before = sum(NORMS[:n])
            if n:
                pe.wait_ge(s_ln, n)
            for j in range(NORMS[n]):
                pe.wait_ge(s_sq, before + j + 1)
                ins = mm(bank[7][:, (n % 2) * SEQ:(n % 2 + 1) * SEQ], ones, SQ[:, j], j == 0)
            ins.then_inc(s_stat, 1)

        def act_rstd(act, n, dim):
            act.preload_act_table_set(LN_EXP)
            act.wait_ge(s_stat, n + 1)
            if n:
                act.wait_ge(s_rstd, n)
            nc.scalar.activation(lnt[:], bank[7][:, (n % 2) * SEQ:(n % 2 + 1) * SEQ], ACT.Ln, bias=eps[:, 0:1],
                                 scale=1.0 / dim).then_inc(s_ln, 1)
            act.wait_ge(s_ln, n + 1)
            nc.scalar.activation(rstd[:, n % 2], lnt[:], ACT.Exp, scale=-0.5).then_inc(s_rstd, 1)

        def rs(n):
            return rstd[:, n % 2]

        s_vstep = sem("vector_step")
        vsteps = [0]

        def link(dve, ins):
            vsteps[0] += 1
            ins.then_inc(s_vstep, 1)
            dve.wait_ge(s_vstep, vsteps[0])

        s_astep = sem("scalar_step")
        asteps = [0]

        def alink(act, ins):
            asteps[0] += 1
            ins.then_inc(s_astep, 1)
            act.wait_ge(s_astep, asteps[0])

        s_t = sem("input_tile_scaled")

        MODULATED = ["ctx", "x1", "f0", "f1", "gla", "f2", "f3", "kv", "mla", "f4"]

        def dve_modulate(dve, n, A, sh, stage, src=None, hi=hhi, lo=hlo):
            u0 = U[stage]
            dve.wait_ge(s_rstd, n + 1)
            for j in range(DT + 1):
                if j < DT:
                    if u0 or j >= 3:
                        dve.wait_ge(s_h, u0 + max(j - 2, 0))
                    nc.vector.scalar_tensor_tensor(out=T[:, j % 3], in0=(src or X)[:, j], scalar=A(j), in1=rs(n),
                                                   op0=ALU.mult, op1=ALU.mult).then_inc(s_t, 1)
                if j:
                    k = j - 1
                    dve.wait_ge(s_hhi, u0 + k + 1)
                    nc.vector.scalar_tensor_tensor(out=lo[:, k], in0=T[:, k % 3], scalar=sh(k),
                                                   in1=hi[:, k].bitcast(f32), op0=ALU.add,
                                                   op1=ALU.subtract).then_inc(s_h, 1)

        def act_modulate(act, sh, stage, hi=hhi):
            t0 = 8 * MODULATED.index(stage)
            for j in range(DT):
                act.wait_ge(s_t, t0 + j + 1)
                nc.scalar.activation(hi[:, j], T[:, j % 3], ACT.Identity, bias=sh(j)).then_inc(s_hhi, 1)

        U = {n: 8 * i for i, n in enumerate(
            ["ctx", "x1", "lstm_y", "f0", "f1", "gla", "gla_y", "f2", "f3", "kv", "mla", "mla_y", "f4"])}

        def dve_mod_unit(dve, u, i=None, per=0):
            dve.wait_ge(s_mod[u % 2], 16 * (u // 2 + 1) + run(i, 8 * per))
            a = FIRST_MODS + u
            dst = mod[:, a:a + 1] if i is None else mod[:, bass.ds(i * per + a, 1)]
            nc.vector.scalar_tensor_tensor(out=mring[:, u % 2], in0=mring[:, u % 2], scalar=1.0, in1=cb[:],
                                           op0=ALU.mult, op1=ALU.mult, accum_out=dst).then_inc(s_mused, 1)

        def dve_mod_bias(dve, a, b, units):
            dve.wait_ge(s_mused, units)
            link(dve, nc.vector.tensor_tensor(mod[:, a:b], mod[:, a:b], cols[:, a:b], ALU.add))

        def dve_coef_pre(dve, q, scale_at, g, src=None):
            src = mod if src is None else src
            link(dve, nc.vector.scalar_tensor_tensor(out=coef[:, q], in0=src[:, scale_at:scale_at + DT], scalar=1.0,
                                                     in1=g, op0=ALU.add, op1=ALU.mult))

        def dve_coef_post(dve, q, gate_at, g, w):
            link(dve, nc.vector.scalar_tensor_tensor(out=coef[:, q], in0=mod[:, gate_at:gate_at + DT], scalar=w,
                                                     in1=g, op0=ALU.mult, op1=ALU.mult))

        def mcol(a):
            return lambda j: mod[:, a + j:a + j + 1]

        def cq(q):
            return lambda j: coef[:, q, j:j + 1]

        s_x = sem("x_tile_updated")
        XU = {n: 8 * i for i, n in enumerate(["lstm", "f0", "fin", "f1", "gla", "f2", "f3", "mla", "f4"])}

        def dve_add_plain(dve, gate_at):
            for m in range(DT):
                nc.vector.scalar_tensor_tensor(out=X[:, m], in0=down(m), scalar=mod[:, gate_at + m:gate_at + m + 1],
                                               in1=X[:, m], op0=ALU.mult, op1=ALU.add).then_inc(s_x, 1)

        s_tp = sem("post_tile_scaled")
        tposts = [0]

        def dve_add_post(dve, n, q, x0):
            dve.wait_ge(s_rstd, n + 1)
            for m in range(DT + 1):
                if m < DT:
                    if m >= 3:
                        dve.wait_ge(s_x, x0 + m - 2)
                    nc.vector.scalar_tensor_tensor(out=T[:, m % 3], in0=down(m), scalar=coef[:, q, m:m + 1],
                                                   in1=rs(n), op0=ALU.mult, op1=ALU.mult).then_inc(s_tp, 1)
                if m:
                    tposts[0] += 1
                    dve.wait_ge(s_tp, tposts[0])
                    nc.vector.tensor_tensor(X[:, m - 1], X[:, m - 1], T[:, (m - 1) % 3], ALU.add).then_inc(s_x, 1)

        s_silu, s_prod = sem("hidden_silu"), sem("hidden_product")
        s_hidhi, s_hid, s_conv, s_cstep = sem("hidden_rounded"), sem("hidden_split"), sem("gate_conv"), sem("conv_step")
        UP_TURNS, DOWN_TURNS = FT // 3, 3

        def hid(t, i, buf):
            return buf[:, t] if i is None else buf[:, bass.ds(i * 3 + t, 1), :].rearrange("p a b -> p (a b)")

        def up_parts(body, eng):
            with eng.Fori(0, UP_TURNS) as i:
                for t in range(3):
                    body(t, i)
            body(FT - 1, None)

        def down_parts(body, eng, f):
            body(0, None)
            body(1, None)
            turns = DOWN_TURNS - (C_FFN[f] + FFN_CHUNKS == NCH)
            with eng.Fori(0, turns) as i:
                for d in range(2, 5):
                    body(d, i)
            for d in range(2 + 3 * turns, FT // 2):
                body(d, None)

        def pe_ffn(pe, f, u0):
            c0 = C_FFN[f]
            for k in range(DT):
                pe.wait_ge(s_h, u0 + k + 1)

            def up(t, i):
                pe.wait_ge(s_lo, c0 + t + 1 + run(i, 3))
                if f or t >= 3:
                    pe.wait_ge(s_prod, FT * f + t - 2 + run(i, 3))
                b = bank[4 + t % 3]
                for m in range(2):
                    for k in range(DT):
                        ins = mm3(b[:, m * SEQ:(m + 1) * SEQ], c0 + t, m * DT + k, hhi[:, k], hlo[:, k], k == 0)
                ins.then_inc(s_pe, 1)

            if f:
                up_parts(up, pe)
            else:
                for t in range(3):
                    up(t, None)
                with pe.Fori(0, UP_TURNS - 1) as i:
                    for t in range(3, 6):
                        up(t, i)
                up(FT - 1, None)

            def dn(d, i):
                c = c0 + FT + d
                pe.wait_ge(s_lo, c + 1 + run(i, 3))
                pe.wait_ge(s_hid, FT * f + 2 * d + 2 + run(i, 6))
                hi = [hid_hi[:, 2 * d + g] if i is None else
                      hid_hi[:, bass.ds(i * 6 + 2 * d + g, 1), :].rearrange("p a b -> p (a b)") for g in range(2)]
                lo = [hid_lo[:, 2 * d + g] if i is None else
                      hid_lo[:, bass.ds(i * 6 + 2 * d + g, 1), :].rearrange("p a b -> p (a b)") for g in range(2)]
                pe_down_chunk(pe, c, hi, lo, d == 0)

            down_parts(dn, pe, f)

        def act_ffn(act, f):
            c0 = C_FFN[f]

            def up(t, i):
                act_split(act, c0 + t + 2, i)
                if f:
                    act.wait_ge(s_pe, c0 + t + 1 + run(i, 3))
                    gate = bank[4 + t % 3][:, 0:SEQ]
                else:
                    act.wait_ge(s_conv, t + 1 + run(i, 3))
                    gate = CG[:]
                nc.scalar.activation(SG[:, t % 3], gate, ACT.Silu).then_inc(s_silu, 1)
                act.wait_ge(s_prod, FT * f + t + 1 + run(i, 3))
                nc.scalar.activation(hid(t, i, hid_hi), T[:, t % 3], ACT.Copy).then_inc(s_hidhi, 1)

            up_parts(up, act)
            down_parts(lambda d, i: act_split(act, c0 + FT + d + 2, i), act, f)

        def dve_ffn(dve, f):
            c0, u0 = C_FFN[f], 32 + 40 * f

            def up(t, i):
                dve_split(dve, c0 + t + 2, i)
                b = bank[4 + t % 3]
                if f == 0:
                    dve.wait_ge(s_pe, c0 + t + 1 + run(i, 3))
                    w = [cols[:, COL[n][0] + t:COL[n][0] + t + 1] if i is None else
                         cols[:, bass.ds(i * 3 + COL[n][0] + t, 1)] for n in ("cw0", "cw1", "cw2", "cb")]
                    nc.vector.tensor_scalar(CG[:], b[:, 0:SEQ], w[1], w[3], ALU.mult, ALU.add).then_inc(s_cstep, 1)
                    dve.wait_ge(s_cstep, 2 * t + 1 + run(i, 6))
                    nc.vector.scalar_tensor_tensor(out=CG[:, 64:256], in0=b[:, 0:192], scalar=w[0], in1=CG[:, 64:256],
                                                   op0=ALU.mult, op1=ALU.add).then_inc(s_cstep, 1)
                    dve.wait_ge(s_cstep, 2 * t + 2 + run(i, 6))
                    nc.vector.scalar_tensor_tensor(out=CG[:, 0:192], in0=b[:, 64:256], scalar=w[2], in1=CG[:, 0:192],
                                                   op0=ALU.mult, op1=ALU.add).then_inc(s_conv, 1)
                dve.wait_ge(s_silu, FT * f + t + 1 + run(i, 3))
                if t:
                    dve.wait_ge(s_hid, FT * f + t + run(i, 3))
                nc.vector.tensor_tensor(T[:, t % 3], SG[:, t % 3], b[:, SEQ:2 * SEQ], ALU.mult).then_inc(s_prod, 1)
                if f < 4 and i is not None:
                    for u in ((0,), (1,), (2, 3))[t]:
                        dve_mod_unit(dve, u0 + u, i, 4)
                dve.wait_ge(s_hidhi, FT * f + t + 1 + run(i, 3))
                nc.vector.tensor_tensor(hid(t, i, hid_lo), T[:, t % 3], hid(t, i, hid_hi).bitcast(f32),
                                        ALU.subtract).then_inc(s_hid, 1)

            up_parts(up, dve)

            def dn(d, i):
                dve_split(dve, c0 + FT + d + 2, i)
                if f < 4 and d >= 2:
                    for u in ((0,), (1,), (2, 3))[(d - 2) % 3]:
                        dve_mod_unit(dve, u0 + 4 * (UP_TURNS + (d - 2) // 3) + u, i, 4)

            down_parts(dn, dve, f)

        s_in = [sem(f"inputs_loaded{j}") for j in range(8)]
        s_gup, s_c2 = sem("gla_gate_weights_loaded"), sem("second_c_loaded")
        s_w0 = [sem(f"first_mods_loaded{j}") for j in range(5)]
        s_w0u = sem("first_mods_used")
        s_out = sem("output_stored")

        @block.sync
        def _(sp):
            sp.dma_start(ccol[:], c_cols).then_inc(s_in[0], 16)
            sp.dma_start(cols[:], cols_d).then_inc(s_in[1], 16)
            sp.dma_start(con[:], const_d).then_inc(s_in[1], 16)
            for k in range(5):
                sp.dma_start(w0[:, k], w_first[k]).then_inc(s_w0[k], 16)
            sp.dma_start(XC[:], ctxT).then_inc(s_in[2], 16)
            sp.dma_start(X[:], xT).then_inc(s_in[3], 16)
            for k in range(5, 8):
                sp.wait_ge(s_w0u, k - 4)
                sp.dma_start(w0[:, k - 5], w_first[k]).then_inc(s_w0[k - 5], 16)
            sp.dma_start(cb[:], c_row.partition_broadcast(P)).then_inc(s_in[4], 16)
            for c in range(min(3, NCH)):
                sp.dma_start(raw[:, c], w_stream[c]).then_inc(s_raw[c], 16)
            turns = NCH // 3 - 1
            if turns > 0:
                with sp.Fori(0, turns) as i:
                    for j in range(3):
                        sp.wait_ge(s_lo, i * 3 + (j + 1))
                        sp.dma_start(raw[:, j], w_stream[bass.ds(i * 3 + (j + 3), 1)]
                                     .rearrange("a p n -> p (a n)")).then_inc(s_raw[j], 16)
            for c in range(3 * (NCH // 3), NCH):
                sp.wait_ge(s_lo, c - 2)
                sp.dma_start(raw[:, c % 3], w_stream[c]).then_inc(s_raw[c % 3], 16)
            sp.wait_ge(s_x, XUP)
            sp.dma_start(out_d, X[:]).then_inc(s_out, 16)
            sp.wait_ge(s_out, 16)

        @block.gpsimd
        def _(pool):
            for u in range(2):
                pool.dma_start(mring[:, u], m_stream[u]).then_inc(s_mod[u], 16)

            def mods(u0, turns):
                with pool.Fori(0, turns) as i:
                    for j in range(2):
                        pool.wait_ge(s_mused, i * 2 + (u0 + j - 1))
                        pool.dma_start(mring[:, j], m_stream[bass.ds(i * 2 + (u0 + j), 1)]
                                       .rearrange("a p n -> p (a n)")).then_inc(s_mod[j], 16)

            mods(2, 15)
            if NMU > 32:
                pool.wait_ge(s_mused, 32)
                pool.dma_start(cb[:], c2_row.partition_broadcast(P)).then_inc(s_c2, 16)
                mods(32, (NMU - 32) // 2)

        s_scol, s_pm, s_mm0 = sem("c_silu"), sem("first_mods"), sem("first_mods_read")
        s_cb = sem("c_rows_silu")
        s_eps = sem("eps_set")
        s_qk = sem("qk_bank_read")
        s_v, s_vb = sem("v_bank_ready"), sem("v_bank_read")
        s_gr = sem("gates_read")
        s_ga, s_gd = sem("gate_exp_ln"), sem("gate_rows")
        s_uT, s_uc = sem("u_columns"), sem("u_columns_read")
        s_os, s_ad = sem("o_bank_read"), sem("denominators_abs")
        s_bc, s_s = sem("decay_rows_broadcast"), sem("qk_scores")
        s_arg, s_e = sem("decay_exponents"), sem("decay_weights")
        s_p, s_den = sem("weighted_scores"), sem("denominators")
        s_th, s_gw2, s_num, s_hc = sem("threshold_read"), sem("normalised_scores"), sem("numerators"), sem("head_read")
        s_y, s_yt = sem("gated_tile"), sem("gated_tile_half")

        def pe_lstm(pe):
            c = C_LSTM
            pe.wait_ge(s_scol, 1)
            for k in range(DT):
                pe.wait_ge(s_w0[k % 5], 16 * (k // 5 + 1))
                for m in range(FIRST_MODS):
                    ins = mm(bank[0][:, 2 * m:2 * m + 2], w0[:, k % 5, m * P:(m + 1) * P], scol[:, k],
                             k == 0 and m == 0)
                ins.then_inc(s_w0u, 1)
            ins = None
            pe.wait_ge(s_in[1], 32)
            pe_stat(pe, N_CTX)
            pe_stat(pe, N_X1)
            if stages == 0:
                return
            for j in range(2):
                pe_pair(pe, c + j, 4 + j, wait=U["x1"] if j == 0 else None)
            for j in range(2):
                for n, (hi, lo) in enumerate(((hhi, hlo), (chi, clo))):
                    a = 2 + 2 * j + n
                    if a >= 3:
                        pe.wait_ge(s_qk, a - 2)
                    pe_pair(pe, c + 2 + j, 4 + a % 3, hi, lo, n == 1)
            tiles = [(chi, clo, 0), (chi, clo, 1), (hhi, hlo, 0), (hhi, hlo, 1)]
            his = [lambda k, b=b, t=t: b[:, k, t * P:(t + 1) * P] for b, _, t in tiles]
            los = [lambda k, b=b, t=t: b[:, k, t * P:(t + 1) * P] for _, b, t in tiles]
            pe.wait_ge(s_mm0, 1)
            for j in range(4):
                if j == 2:
                    pe.wait_ge(s_vb, 4)
                pe_wide(pe, c + 4 + j, 4 * (j % 2), [bank[b][:] for b in range(4)], his, los)
            pe.wait_ge(s_lo, c + 9)
            pe.wait_ge(s_ln, 2)
            for n, (hi, lo) in enumerate(((chi, clo), (hhi, hlo))):
                for k in range(DT):
                    ins = mm3(bank[7][:, n * SEQ:(n + 1) * SEQ], c + 8, k, hi[:, k], lo[:, k], k == 0)
            ins.then_inc(s_pe, 1)
            pe.wait_ge(s_qk, 6)
            for j in range(4):
                if j == 3:
                    pe.wait_ge(s_os, 1)
                pe_pair(pe, c + 9 + j, 4 + j % 3)
            pe.wait_ge(s_gd, 1)
            pe.wait_ge(s_vb, 8)
            for st in range(4):
                ins = nc.tensor.transpose(bank[7][:, st * 36:(st + 1) * 36], ut[:, st * P:(st + 1) * P],
                                          ident[0:36, 0:36])
            ins.then_inc(s_uT, 1)
            pe.wait_ge(s_os, 4)
            for h in range(HEADS):
                if h:
                    pe.wait_ge(s_e, 8 * h)
                    pe.wait_ge(s_th, h)
                for d in range(2):
                    q = (d * 4 + h) * P
                    mm(bank[2][:, d * SEQ:(d + 1) * SEQ], cst("sel")[0:36, q:q + P], mt[:], True)
                    ins = mm(bank[3][:, d * SEQ:(d + 1) * SEQ], cst("sel")[0:36, q:q + P], th[:], True)
                ins.then_inc(s_bc, 1)
                if h:
                    pe.wait_ge(s_p, 2 * h)
                for st in range(4):
                    ins = mm(bank[st // 2][:, (st % 2) * SEQ:(st % 2 + 1) * SEQ], K[:, h, st * P:(st + 1) * P],
                             Q[:, h], True)
                ins.then_inc(s_s, 1)
                for d in range(2):
                    pe.wait_ge(s_p, 2 * h + d + 1)
                    for st in range(4):
                        ins = mm(bank[4][:, d * SEQ:(d + 1) * SEQ], ones, EF[:, d, st], st == 0)
                ins.then_inc(s_den, 1)
                pe.wait_ge(s_gw2, h + 1)
                for v in range(2):
                    for st in range(4):
                        ins = mm(bank[5][:, v * SEQ:(v + 1) * SEQ], V[:, st, h * DV + v * P:h * DV + (v + 1) * P],
                                 EF[:, 0, st], st == 0)
                ins.then_inc(s_num, 1)
                pe_stat(pe, N_LSTM + h)
            for j in range(4):
                pe.wait_ge(s_lo, c + 14 + j)
                for g in range(2):
                    pe.wait_ge(s_h, U["lstm_y"] + 2 * j + g + 1)
                pe_down_chunk(pe, c + 13 + j, [hhi[:, 2 * j], hhi[:, 2 * j + 1]], [hlo[:, 2 * j], hlo[:, 2 * j + 1]],
                              j == 0)

        def act_lstm(act):
            c = C_LSTM
            act.wait_ge(s_in[0], 16)
            nc.scalar.activation(scol[:], ccol[:], ACT.Silu).then_inc(s_scol, 1)
            act_squares(act, N_CTX, lambda j: XC[:, j], lambda j: (s_in[2], 16))
            act.wait_ge(s_in[3], 16)
            act.wait_ge(s_eps, 1)
            act_squares(act, N_X1, lambda j: X[:, j])
            act_rstd(act, N_CTX, D)
            act_rstd(act, N_X1, D)
            act.wait_ge(s_in[4], 16)
            nc.scalar.activation(cb[:], cb[:], ACT.Silu).then_inc(s_cb, 1)
            if stages == 0:
                return
            for j in range(2):
                act_split(act, j)
            act_modulate(act, lambda j: modc[:, j:j + 1], "ctx", chi)
            act_modulate(act, mcol(0), "x1")
            for j in range(9):
                act_split(act, c + j + 2)
                if j in (5, 7):
                    act.wait_ge(s_pe, c + j + 1)
                    for b in (1, 3):
                        nc.scalar.activation(V[:, b, (j - 5) * 256:(j - 5) * 256 + 512], bank[b][:], ACT.Copy)\
                            .then_inc(s_vb, 1)
            act.preload_act_table_set(LN_EXP)
            act.wait_ge(s_gr, 1)
            alink(act, nc.scalar.activation(ga[:], gf[:], ACT.Abs))
            alink(act, nc.scalar.activation(ga[:], ga[:], ACT.Exp, scale=-1.0))
            nc.scalar.activation(ga[:], ga[:], ACT.Ln, bias=1.0).then_inc(s_ga, 1)
            act.wait_ge(s_gr, 2)
            nc.scalar.activation(gb[:], ga[:], ACT.Exp, scale=-1.0).then_inc(s_ga, 1)
            for j in range(4):
                act_split(act, c + 9 + j + 2)
                act.wait_ge(s_pe, c + 9 + j + 1)
                nc.scalar.activation(OS[:, 2 * j:2 * j + 2].rearrange("p a b -> p (a b)"), bank[4 + j % 3][:],
                                     ACT.Sigmoid).then_inc(s_os, 1)
            act.preload_act_table_set(LN_EXP)
            act.wait_ge(s_uc, 1)
            for h in range(HEADS):
                act.wait_ge(s_bc, h + 1)
                if h:
                    act.wait_ge(s_num, h)
                    act.wait_ge(s_den, h)
                nc.scalar.activation(thb.rearrange("p a b -> p (a b)"), bank[3][:], ACT.Copy).then_inc(s_th, 1)
                act.wait_ge(s_arg, 4 * h + 4)
                for d in range(2):
                    for st in range(2):
                        nc.scalar.activation(EF[:, d, st], bank[2][:, d * SEQ:(d + 1) * SEQ], ACT.Exp,
                                             bias=uc[:, st, 32 * d + h:32 * d + h + 1]).then_inc(s_e, 1)
                for d in range(2):
                    for st in range(2):
                        nc.scalar.activation(EF[:, d, 2 + st], EF[:, d, 2 + st], ACT.Exp).then_inc(s_e, 1)
                act.wait_ge(s_den, h + 1)
                nc.scalar.activation(rd[:].rearrange("p a b -> p (a b)"), bank[4][:], ACT.Abs).then_inc(s_ad, 1)
                act_squares(act, N_LSTM + h, lambda j: bank[5][:, j * SEQ:(j + 1) * SEQ], lambda j: (s_num, h + 1))
                act_rstd(act, N_LSTM + h, DV)
                for v in range(2):
                    j = 2 * h + v
                    act.wait_ge(s_y, j + 1)
                    nc.scalar.activation(hhi[:, j], T[:, v], ACT.Copy).then_inc(s_hhi, 1)
            for j in range(4):
                act_split(act, c + 13 + j + 2)

        def dve_lstm(dve):
            c = C_LSTM
            nc.vector.memset(eps[:], EPS).then_inc(s_eps, 1)
            nc.vector.memset(gi[:], 0.0)
            nc.vector.memset(ut[:], 0.0)
            nc.vector.memset(mt[:], 0.0)
            nc.vector.memset(th[:], 0.0)
            dve.wait_ge(s_in[1], 32)
            dve.wait_ge(s_w0u, 8)
            pm = bank[0][:, 0:2 * FIRST_MODS].rearrange("p (m t) -> p t m", t=2)
            link(dve, nc.vector.tensor_tensor(mod[:, 0:FIRST_MODS], pm[:, 0], cols[:, 0:FIRST_MODS], ALU.add))
            ins = nc.vector.tensor_tensor(modc[:], pm[:, 1], cols[:, 0:FIRST_MODS], ALU.add)
            ins.then_inc(s_mm0, 1)
            dve.wait_ge(s_mm0, 1)
            dve_coef_pre(dve, 0, 8, col("g_mix", 0, 8), modc)
            dve_coef_pre(dve, 1, 8, col("g_mix", 0, 8))
            if stages == 0:
                return
            for j in range(2):
                dve_split(dve, j)
            dve_modulate(dve, N_CTX, cq(0), lambda j: modc[:, j:j + 1], "ctx", XC, chi, clo)
            dve_modulate(dve, N_X1, cq(1), mcol(0), "x1")
            dve.wait_ge(s_cb, 1)
            nc.vector.memset(gf[:], 0.0)
            for j in range(2):
                dve_split(dve, c + j + 2)
                dve.wait_ge(s_pe, c + j + 1)
                nc.vector.tensor_copy(Q[:, 2 * j:2 * j + 2].rearrange("p a b -> p (a b)"), bank[4 + j][:])\
                    .then_inc(s_qk, 1)
                for u in range(2):
                    dve_mod_unit(dve, 2 * j + u)
            for j in range(2):
                dve_split(dve, c + j + 4)
                dve.wait_ge(s_pe, c + 2 + j + 1)
                for n in range(2):
                    a = 2 + 2 * j + n
                    nc.vector.tensor_scalar(K[:, 2 * j:2 * j + 2, (1 - n) * SEQ:(2 - n) * SEQ],
                                            bank[4 + a % 3][:].rearrange("p (m t) -> p m t", m=2),
                                            DK ** -0.5, None, ALU.mult).then_inc(s_qk, 1)
                for u in range(2):
                    dve_mod_unit(dve, 4 + 2 * j + u)
            for j in range(4):
                dve_split(dve, c + j + 6)
                if j % 2:
                    dve.wait_ge(s_pe, c + 4 + j + 1)
                    for b in (0, 2):
                        nc.vector.tensor_copy(V[:, b, (j - 1) * 256:(j - 1) * 256 + 512], bank[b][:])\
                            .then_inc(s_vb, 1)
                for u in range(2):
                    dve_mod_unit(dve, 8 + 2 * j + u)
            dve_split(dve, c + 10)
            dve.wait_ge(s_pe, c + 9)
            link(dve, nc.vector.tensor_scalar(g_all[:], bank[7][:], col("b_gate"), None, ALU.add))
            two = lambda x: x.rearrange("p (a b) -> p a b", a=2)
            nc.vector.tensor_copy(gi[0:4], g_all[0:4])
            nc.vector.tensor_copy(two(gi[32:36]), two(g_all[32:36])[:, :, ::-1])
            nc.vector.tensor_copy(gf[0:4], g_all[64:68])
            nc.vector.tensor_copy(two(gf[32:36]), two(g_all[96:100])[:, :, ::-1]).then_inc(s_gr, 1)
            dve.wait_ge(s_ga, 1)
            link(dve, nc.vector.scalar_tensor_tensor(out=gf[:], in0=gf[:], scalar=0.0, in1=ga[:], op0=ALU.min,
                                                     op1=ALU.subtract))
            link(dve, nc.vector.tensor_tensor_scan(g_all[0:36], ones[0:36, 0:1].to_broadcast([36, 512]), gf[:], 0.0,
                                                   ALU.mult, ALU.add))
            link(dve, nc.vector.tensor_tensor(gi[:], gi[:], g_all[0:36], ALU.subtract))
            link(dve, nc.vector.tensor_tensor_scan(gf[:], gi[:], gi[:], 0.0, ALU.max, ALU.max))
            nc.vector.tensor_tensor(ga[:], gf[:], g_all[0:36], ALU.add).then_inc(s_gr, 1)
            nc.vector.tensor_copy(ut[0:4], gi[0:4])
            nc.vector.tensor_copy(two(ut[32:36]), two(gi[32:36])[:, :, ::-1])
            nc.vector.tensor_scalar(mt[0:4], gf[0:4, SEQ:], -1.0, None, ALU.mult)
            nc.vector.tensor_scalar(mt[32:36], gf[32:36, SEQ:][:, ::-1], -1.0, None, ALU.mult)
            dve.wait_ge(s_ga, 2)
            nc.vector.tensor_copy(th[0:4], gb[0:4, SEQ:])
            nc.vector.tensor_copy(th[32:36], gb[32:36, SEQ:][:, ::-1]).then_inc(s_gd, 1)
            for j in range(4):
                dve_split(dve, c + 9 + j + 2)
                for u in range(2):
                    dve_mod_unit(dve, 16 + 2 * j + u)
            dve.wait_ge(s_uT, 1)
            nc.vector.tensor_copy(uc[:].rearrange("p a b -> p (a b)"), bank[7][:, 0:144]).then_inc(s_uc, 1)
            dve.wait_ge(s_uc, 1)
            madd = cst("madd").rearrange("p (d s t) -> p d s t", d=2, s=2)
            for h in range(HEADS):
                dve.wait_ge(s_bc, h + 1)
                if h:
                    dve.wait_ge(s_num, h)
                for d in range(2):
                    for st in range(2):
                        nc.vector.scalar_tensor_tensor(out=EF[:, d, 2 + st], in0=bank[2][:, d * SEQ:(d + 1) * SEQ],
                                                       scalar=uc[:, 2 + st, 32 * d + h:32 * d + h + 1],
                                                       in1=madd[:, d, st], op0=ALU.add, op1=ALU.add)\
                            .then_inc(s_arg, 1)
                for u in range(2):
                    dve_mod_unit(dve, 24 + 2 * h + u)
                dve.wait_ge(s_s, h + 1)
                dve.wait_ge(s_e, 8 * (h + 1))
                for d in range(2):
                    for b in range(2):
                        if d == 0 and b == 0 and h:
                            dve.wait_ge(s_gw2, h)
                        e = EF[:, d, 2 * b:2 * b + 2].rearrange("p a b -> p (a b)")
                        ins = nc.vector.tensor_tensor(e, e, bank[b][:], ALU.mult)
                    ins.then_inc(s_p, 1)
                dve.wait_ge(s_ad, h + 1)
                r = rd[:].rearrange("p a b -> p (a b)")
                link(dve, nc.vector.tensor_tensor(r, r, thb.rearrange("p a b -> p (a b)"), ALU.max))
                link(dve, nc.vector.reciprocal(r, r))
                for d in range(2):
                    ins = nc.vector.tensor_tensor(EF[:, d], EF[:, d], rd[:, d:d + 1].to_broadcast([P, 4, SEQ]),
                                                  ALU.mult)
                link(dve, ins)
                nc.vector.tensor_tensor(EF[:, 0], EF[:, 0], EF[:, 1], ALU.add).then_inc(s_gw2, 1)
                dve.wait_ge(s_rstd, N_LSTM + h + 1)
                dve.wait_ge(s_h, U["lstm_y"] + 2 * h)
                for v in range(2):
                    j = 2 * h + v
                    link(dve, nc.vector.scalar_tensor_tensor(out=T[:, v], in0=bank[5][:, v * SEQ:(v + 1) * SEQ],
                                                             scalar=col("gain", j), in1=rs(N_LSTM + h),
                                                             op0=ALU.mult, op1=ALU.mult))
                    nc.vector.tensor_tensor(T[:, v], T[:, v], OS[:, j], ALU.mult).then_inc(s_y, 1)
                for v in range(2):
                    j = 2 * h + v
                    dve.wait_ge(s_hhi, U["lstm_y"] + j + 1)
                    nc.vector.tensor_tensor(hlo[:, j], T[:, v], hhi[:, j].bitcast(f32), ALU.subtract)\
                        .then_inc(s_h, 1)
            for j in range(4):
                dve_split(dve, c + 13 + j + 2)
            dve_mod_bias(dve, FIRST_MODS, M_COND[0], 32)
            dve.wait_ge(s_pe, c + 17)
            dve_add_plain(dve, 16)

        def x_ready(u):
            return lambda j: (s_x, u + j + 1)

        def ng(layer, sub, post):
            return col("norm_g", ((layer * 3 + sub) * 2 + post) * DT, DT)

        SWIGLU = {1: (0, 0, N_F1, "f1", "fin"), 2: (0, 2, N_F2, "f2", "gla"), 3: (1, 0, N_F3, "f3", "f2"),
                  4: (1, 2, N_F4, "f4", "mla")}

        def pe_swiglu(pe, f):
            _, _, n, name, _ = SWIGLU[f]
            pe_stat(pe, n)
            pe_ffn(pe, f, U[name])
            pe_stat(pe, n + 1)

        def act_swiglu(act, f):
            layer, sub, n, name, before = SWIGLU[f]
            act_squares(act, n, lambda j: X[:, j], x_ready(XU[before]))
            act_rstd(act, n, D)
            act_modulate(act, mcol(M_COND[layer] + 3 * sub * DT), name)
            if f == 3:
                nc.scalar.activation(XS[:], X[:], ACT.Copy).then_inc(s_xs, 1)
            act_ffn(act, f)
            act_squares(act, n + 1, down, lambda j: (s_pe, C_FFN[f] + FFN_CHUNKS))
            act_rstd(act, n + 1, D)

        def dve_swiglu(dve, f):
            layer, sub, n, name, _ = SWIGLU[f]
            m0 = M_COND[layer] + 3 * sub * DT
            dve_coef_pre(dve, 3, m0 + DT, ng(layer, sub, 0))
            dve_coef_post(dve, 4, m0 + 2 * DT, ng(layer, sub, 1), 0.5)
            dve_modulate(dve, n, cq(3), mcol(m0), name)
            dve_ffn(dve, f)
            if f < 4:
                dve_mod_bias(dve, 48 + 40 * f, 88 + 40 * f, 72 + 40 * f)
            if f == 3:
                dve.wait_ge(s_xs, 1)
            dve_add_post(dve, n + 1, 4, XU[name])

        s_xs = sem("layer0_output_kept")

        s_gb, s_z, s_zr = sem("gla_bank_read"), sem("gate_products"), sem("gate_products_read")
        s_gln, s_gsc, s_gex = sem("gla_gate_ln"), sem("gla_gate_scan"), sem("gla_gate_exp")
        s_qkd, s_gvb, s_r = sem("gla_qk_decayed"), sem("gla_v_bank_read"), sem("gla_r_bank_read")
        s_att, s_attr, s_kut = sem("gla_scores"), sem("gla_scores_read"), sem("gla_keys_transposed_read")
        s_upd, s_st, s_o = sem("gla_updates"), sem("gla_states"), sem("gla_head_output")

        def upd(n):
            return bank[2 + n % 2][:, (n // 2) * DV:(n // 2 + 1) * DV]

        def pe_gla(pe):
            c, n0 = C_GLA, N_GLA
            pe_stat(pe, n0)
            pe.wait_ge(s_lo, c + 1)
            for k in range(DT):
                pe.wait_ge(s_h, U["gla"] + k + 1)
                ins = mm3(bank[4][:, 0:SEQ], c, k, hhi[:, k], hlo[:, k], k == 0)
            ins.then_inc(s_pe, 1)
            for j, b in enumerate((5, 6, 4, 5)):
                if j >= 2:
                    pe.wait_ge(s_gb, j - 1)
                pe_pair(pe, c + 1 + j, b)
            pe.wait_ge(s_gb, 4)
            pe.wait_ge(s_gup, 16)
            for h in range(HEADS):
                ins = mm(bank[(6, 4)[h // 2]][:, (h % 2) * SEQ:(h % 2 + 1) * SEQ], wgu[:, h * DK:(h + 1) * DK], glow[:],
                         h % 2 == 0)
            ins.then_inc(s_z, 1)
            his = [lambda k, t=t: hhi[:, k, t * P:(t + 1) * P] for t in range(2)]
            los = [lambda k, t=t: hlo[:, k, t * P:(t + 1) * P] for t in range(2)]
            for j in range(4):
                b = 2 * (j // 2)
                pe_wide(pe, c + 5 + j, 4 * (j % 2), [bank[b][:], bank[b + 1][:]], his, los)
            for j, b in enumerate((5, 6, 4, 5)):
                if j == 0:
                    pe.wait_ge(s_gb, 5)
                elif j == 1:
                    pe.wait_ge(s_zr, 4)
                elif j == 3:
                    pe.wait_ge(s_r, 1)
                pe_pair(pe, c + 9 + j, b)
            pe.wait_ge(s_gvb, 4)
            for h in range(HEADS):
                pe.wait_ge(s_qkd, 2)
                if h:
                    pe.wait_ge(s_attr, h)
                    pe.wait_ge(s_kut, h)
                for t in range(2):
                    tt = slice(t * P, (t + 1) * P)
                    mm(bank[0][:, tt], GK[:, h, tt], GQ[:, h, tt], t == 0)
                for t in range(2):
                    tt = slice(t * P, (t + 1) * P)
                    ins = nc.tensor.transpose(bank[1][:, tt], GKU[:, h, tt], ident)
                ins.then_inc(s_att, 1)
                pe.wait_ge(s_kut, h + 1)
                if h:
                    pe.wait_ge(s_st, 3 * h)
                for n in range(3):
                    half = slice(64 * (n % 2), 64 * (n % 2) + 64)
                    ins = mm(upd(n), kut[half, n // 2], GV[half, n // 2, h * DV:(h + 1) * DV], n < 2)
                ins.then_inc(s_upd, 1)
                pe.wait_ge(s_attr, h + 1)
                pe.wait_ge(s_st, 3 * h + 3)
                if h:
                    pe.wait_ge(s_r, 4)
                    pe.wait_ge(s_y, 2 * HEADS + 2 * h)
                for v in range(2):
                    for t in range(2):
                        mm(bank[5][:, v * SEQ + t * P:v * SEQ + (t + 1) * P],
                           GV[:, t, h * DV + v * P:h * DV + (v + 1) * P], att[:, t], v == 0 and t == 0)
                    for n in range(1, 4):
                        ins = mm(bank[5][:, v * SEQ + n * CHUNK:v * SEQ + (n + 1) * CHUNK],
                                 ST[:, n - 1, v * P:(v + 1) * P], GQ[:, h, n * CHUNK:(n + 1) * CHUNK], False)
                ins.then_inc(s_o, 1)
                pe_stat(pe, N_GHEAD + h)
            for j in range(4):
                pe.wait_ge(s_lo, c + 14 + j)
                for g in range(2):
                    pe.wait_ge(s_h, U["gla_y"] + 2 * j + g + 1)
                pe_down_chunk(pe, c + 13 + j, [hhi[:, 2 * j], hhi[:, 2 * j + 1]], [hlo[:, 2 * j], hlo[:, 2 * j + 1]],
                              j == 0)
            pe_stat(pe, N_GPOST)

        flat = lambda x: x.rearrange("p a b -> p (a b)")

        def act_gla(act):
            c = C_GLA
            act_squares(act, N_GLA, lambda j: X[:, j], x_ready(XU["f1"]))
            act.wait_ge(s_pe, c)
            act.dma_start(wgu[:], w_gup).then_inc(s_gup, 16)
            act_rstd(act, N_GLA, D)
            act_modulate(act, mcol(M_COND[0] + 3 * DT), "gla")
            for j in range(5):
                act_split(act, c + j + 2)
            act.preload_act_table_set(LN_EXP)
            act.wait_ge(s_z, 1)
            for h in range(HEADS):
                nc.scalar.activation(LA[:, h], bank[(6, 4)[h // 2]][:, (h % 2) * SEQ:(h % 2 + 1) * SEQ], ACT.Identity,
                                     bias=col("b_gla", h)).then_inc(s_zr, 1)
            act.wait_ge(s_zr, 4)
            alink(act, nc.scalar.activation(LB[:], LA[:], ACT.Abs))
            alink(act, nc.scalar.activation(LB[:], LB[:], ACT.Exp, scale=-1.0))
            nc.scalar.activation(LB[:], LB[:], ACT.Ln, bias=1.0).then_inc(s_gln, 1)
            for j in range(2):
                act_split(act, c + 5 + j + 2)
            act.wait_ge(s_gsc, 1)
            nc.scalar.activation(EB[:], LB[:], ACT.Exp, scale=1 / 16).then_inc(s_gex, 1)
            nc.scalar.activation(EN[:], LB[:], ACT.Exp, scale=-1 / 16).then_inc(s_gex, 1)
            act.wait_ge(s_gsc, 2)
            nc.scalar.activation(LA[:], LA[:], ACT.Exp, scale=1 / 16).then_inc(s_gex, 1)
            for j in range(2, 4):
                act_split(act, c + 5 + j + 2)
            for j in range(4):
                act_split(act, c + 9 + j + 2)
                act.wait_ge(s_pe, c + 9 + j + 1)
                nc.scalar.activation(flat(SR[:, 2 * j:2 * j + 2]), bank[(5, 6, 4, 5)[j]][:], ACT.Silu)\
                    .then_inc(s_r, 1)
            for h in range(HEADS):
                act.wait_ge(s_att, h + 1)
                if h:
                    act.wait_ge(s_upd, h)
                nc.scalar.activation(flat(kut[:]), bank[1][:, 0:SEQ], ACT.Copy).then_inc(s_kut, 1)
                act_squares(act, N_GHEAD + h, lambda j: bank[5][:, j * SEQ:(j + 1) * SEQ], lambda j: (s_o, h + 1))
                act_rstd(act, N_GHEAD + h, DV)
                for v in range(2):
                    j = 2 * h + v
                    act.wait_ge(s_y, 2 * HEADS + j + 1)
                    nc.scalar.activation(hhi[:, j], T[:, v], ACT.Copy).then_inc(s_hhi, 1)
            for j in range(4):
                act_split(act, c + 13 + j + 2)
            act_squares(act, N_GPOST, down, lambda j: (s_pe, c + 17))
            act_rstd(act, N_GPOST, D)

        def dve_gla(dve):
            c, m0 = C_GLA, M_COND[0] + 3 * DT
            dve_coef_pre(dve, 3, m0 + DT, ng(0, 1, 0))
            dve_coef_post(dve, 4, m0 + 2 * DT, ng(0, 1, 1), 1.0)
            dve_modulate(dve, N_GLA, cq(3), mcol(m0), "gla")
            for j in range(5):
                dve_split(dve, c + j + 2)
                dve.wait_ge(s_pe, c + j + 1)
                if j == 0:
                    nc.vector.tensor_copy(glow[:], bank[4][0:16, 0:SEQ]).then_inc(s_gb, 1)
                elif j < 3:
                    nc.vector.tensor_scalar(flat(GQ[:, 2 * j - 2:2 * j]), bank[4 + j][:], DK ** -0.5, None,
                                            ALU.mult).then_inc(s_gb, 1)
                else:
                    nc.vector.tensor_copy(flat(GK[:, 2 * j - 6:2 * j - 4]), bank[1 + j][:]).then_inc(s_gb, 1)
            dve.wait_ge(s_gln, 1)
            link(dve, nc.vector.scalar_tensor_tensor(out=flat(LA[:]), in0=flat(LA[:]), scalar=0.0, in1=flat(LB[:]),
                                                     op0=ALU.min, op1=ALU.subtract))
            for h in range(HEADS):
                ins = nc.vector.tensor_tensor_scan(LB[:, h], cst("reset"), LA[:, h], 0.0, ALU.mult, ALU.add)
            ins.then_inc(s_gsc, 1)
            dve.wait_ge(s_gsc, 1)
            b4 = flat(LB[:]).rearrange("p (n c) -> p n c", c=CHUNK)
            nc.vector.tensor_tensor(flat(LA[:]).rearrange("p (n c) -> p n c", c=CHUNK),
                                    b4[:, :, CHUNK - 1:CHUNK].to_broadcast([P, 16, CHUNK]), b4, ALU.subtract)\
                .then_inc(s_gsc, 1)
            for j in range(2):
                dve_split(dve, c + 5 + j + 2)
            dve.wait_ge(s_gex, 3)
            nc.vector.tensor_tensor(flat(GQ[:]), flat(GQ[:]), flat(EB[:]), ALU.mult).then_inc(s_qkd, 1)
            link(dve, nc.vector.tensor_tensor(flat(GKU[:]), flat(GK[:]), flat(LA[:]), ALU.mult))
            nc.vector.tensor_tensor(flat(GK[:]), flat(GK[:]), flat(EN[:]), ALU.mult).then_inc(s_qkd, 1)
            for j in range(2, 4):
                dve_split(dve, c + 5 + j + 2)
                dve.wait_ge(s_pe, c + 5 + 2 * (j - 2) + 2)
                for t in range(2):
                    nc.vector.tensor_copy(GV[:, t, (j - 2) * 512:(j - 1) * 512], bank[2 * (j - 2) + t][:])\
                        .then_inc(s_gvb, 1)
            for j in range(4):
                dve_split(dve, c + 9 + j + 2)
            eb4 = flat(EB[:]).rearrange("p (n c) -> p n c", c=CHUNK)
            for h in range(HEADS):
                dve.wait_ge(s_att, h + 1)
                if h:
                    dve.wait_ge(s_o, h)
                link(dve, nc.vector.tensor_scalar(flat(att[:]), bank[0][:, 0:SEQ], 3e38, -3e38, ALU.min, ALU.max))
                nc.vector.tensor_tensor(flat(att[:]), flat(att[:]), cst("causal"), ALU.mult).then_inc(s_attr, 1)
                dve.wait_ge(s_upd, h + 1)
                nc.vector.tensor_copy(ST[:, 0], bank[2][:, 0:DV]).then_inc(s_st, 1)
                for n in range(1, 3):
                    dve.wait_ge(s_st, 3 * h + n)
                    nc.vector.scalar_tensor_tensor(out=ST[:, n], in0=ST[:, n - 1],
                                                   scalar=eb4[:, 4 * h + n, CHUNK - 1:CHUNK],
                                                   in1=upd(n),
                                                   op0=ALU.mult, op1=ALU.add).then_inc(s_st, 1)
                dve.wait_ge(s_rstd, N_GHEAD + h + 1)
                dve.wait_ge(s_h, U["gla_y"] + 2 * h)
                for v in range(2):
                    j = 2 * h + v
                    link(dve, nc.vector.scalar_tensor_tensor(out=T[:, v], in0=bank[5][:, v * SEQ:(v + 1) * SEQ],
                                                             scalar=col("g_out", v), in1=rs(N_GHEAD + h),
                                                             op0=ALU.mult, op1=ALU.mult))
                    nc.vector.tensor_tensor(T[:, v], T[:, v], SR[:, j], ALU.mult).then_inc(s_y, 1)
                for v in range(2):
                    j = 2 * h + v
                    dve.wait_ge(s_hhi, U["gla_y"] + j + 1)
                    nc.vector.tensor_tensor(hlo[:, j], T[:, v], hhi[:, j].bitcast(f32), ALU.subtract)\
                        .then_inc(s_h, 1)
            for j in range(4):
                dve_split(dve, c + 13 + j + 2)
            dve_add_post(dve, N_GPOST, 4, XU["gla"])

        s_lt, s_lhi, s_l = sem("latent_scaled"), sem("latent_rounded"), sem("latent_split")
        s_pos, s_ang, s_cs = sem("positions_loaded"), sem("angles"), sem("cos_sin")
        s_kr, s_kn, s_vm = sem("rotary_key"), sem("key_bank_read"), sem("value_bank_read")
        s_qn, s_qr, s_sc = sem("query_bank_read"), sem("rotary_query"), sem("mla_scores")
        s_scr, s_pexp, s_pn = sem("scores_masked"), sem("scores_exp"), sem("probabilities")
        s_pt, s_ptr, s_pv = sem("probabilities_transposed"), sem("transposes_read"), sem("mla_head")
        s_mxx = sem("scores_max")

        def act_latent(act, l0, n):
            for j in range(n):
                act.wait_ge(s_lt, l0 + j + 1)
                nc.scalar.activation(lhi[:, j], T[:, j], ACT.Copy).then_inc(s_lhi, 1)

        def dve_latent(dve, l0, n, norm, g, srcs):
            dve.wait_ge(s_rstd, norm + 1)
            for j in range(n):
                nc.vector.scalar_tensor_tensor(out=T[:, j], in0=srcs[j], scalar=col(g, j), in1=rs(norm),
                                               op0=ALU.mult, op1=ALU.mult).then_inc(s_lt, 1)
            for j in range(n):
                dve.wait_ge(s_lhi, l0 + j + 1)
                nc.vector.tensor_tensor(llo[:, j], T[:, j], lhi[:, j].bitcast(f32), ALU.subtract).then_inc(s_l, 1)

        def dve_rope(dve, first, second, x1, x2, s_done):
            for out, a, b, op in ((first, rd[:, 0], rd[:, 1], ALU.subtract), (second, rd[:, 1], rd[:, 0], ALU.add)):
                nc.vector.tensor_tensor(out, x1, a, ALU.mult)
                link(dve, nc.vector.tensor_tensor(CG[:], x2, b, ALU.mult))
                ins = nc.vector.tensor_tensor(out, out, CG[:], op)
                if out is first:
                    link(dve, ins)
            ins.then_inc(s_done, 1)
            return ins

        def pe_kv(pe):
            c = C_KV
            pe_stat(pe, N_KV)
            pe_pair(pe, c, 4, wait=U["kv"])
            pe_pair(pe, c + 1, 5)
            pe_stat(pe, N_KVL)
            pe.wait_ge(s_lo, c + 3)
            pe.wait_ge(s_l, 2)
            for m in range(MLA_HEADS):
                for k in range(2):
                    ins = mm3(down(m), c + 2, 2 * m + k, lhi[:, k], llo[:, k], m % 2 == 0 and k == 0)
            ins.then_inc(s_pe, 1)
            pe.wait_ge(s_lo, c + 4)
            sl = (c + 3) % 3
            for n, (t, half, b) in enumerate(((0, 0, 4), (0, 1, 5), (1, 0, 6), (1, 1, 0))):
                if b == 5:
                    pe.wait_ge(s_kr, 1)
                if b == 0:
                    pe.wait_ge(s_kn, 4)
                for k in range(2):
                    w = slice(k * D + half * 512, k * D + half * 512 + 512)
                    tt = slice(t * P, (t + 1) * P)
                    mm(bank[b][:], lhi[:, k, tt], whi[:, sl, w], k == 0)
                    mm(bank[b][:], lhi[:, k, tt], wlo[:, sl, w], False)
                    ins = mm(bank[b][:], llo[:, k, tt], whi[:, sl, w], False)
            ins.then_inc(s_pe, 1)

        def act_kv(act):
            c = C_KV
            act.wait_ge(s_x, XU["f3"])
            act.dma_start(CG[:].bitcast(i32), pos_d.partition_broadcast(P)).then_inc(s_pos, 16)
            act_squares(act, N_KV, lambda j: XS[:, j], lambda j: (s_xs, 1))
            act_rstd(act, N_KV, D)
            act_modulate(act, mcol(M_KV), "kv")
            for j in range(2):
                act_split(act, c + j + 2)
            act.wait_ge(s_ang, 1)
            nc.scalar.activation(rd[:], SG[:, 0:2], ACT.Sin).then_inc(s_cs, 1)
            act_squares(act, N_KVL, lambda j: bank[4][:, j * SEQ:(j + 1) * SEQ], lambda j: (s_pe, c + 1))
            act_rstd(act, N_KVL, 256)
            act_latent(act, 0, 2)
            for j in range(2, 4):
                act_split(act, c + j + 2)

        def dve_kv(dve):
            c = C_KV
            TURN = 2 * np.pi
            C1 = 6.28125
            C2 = float(np.float32(np.round((TURN - C1) * 2 ** 20) / 2 ** 20))
            C3 = TURN - C1 - C2
            dve.wait_ge(s_pos, 16)
            link(dve, nc.vector.tensor_copy(SG[:, 2], CG[:].bitcast(i32)))
            link(dve, nc.vector.tensor_scalar(SG[:, 2], SG[:, 2], col("invf"), None, ALU.mult))
            for n, add in ((0, 0.25), (1, 0.0)):
                link(dve, nc.vector.tensor_scalar(CG[:], SG[:, 2], 1 / TURN, add, ALU.mult, ALU.add))
                link(dve, nc.vector.tensor_scalar(CG[:], CG[:], 1.5 * 2 ** 23, None, ALU.add))
                link(dve, nc.vector.tensor_scalar(CG[:], CG[:], -1.5 * 2 ** 23, None, ALU.add))
                src = SG[:, 2]
                for part in (C1, C2, C3):
                    link(dve, nc.vector.scalar_tensor_tensor(out=SG[:, n], in0=CG[:], scalar=-part, in1=src,
                                                             op0=ALU.mult, op1=ALU.add))
                    src = SG[:, n]
                if n == 0:
                    link(dve, nc.vector.tensor_scalar(SG[:, 0], SG[:, 0], TURN / 4, None, ALU.add))
            pi = float(np.nextafter(np.float32(np.pi), np.float32(0)))
            nc.vector.tensor_scalar(flat(SG[:, 0:2]), flat(SG[:, 0:2]), pi, -pi, ALU.min, ALU.max).then_inc(s_ang, 1)
            dve_coef_pre(dve, 3, M_KV + DT, col("kv_g", 0, DT))
            dve_modulate(dve, N_KV, cq(3), mcol(M_KV), "kv", XS)
            for j in range(2):
                dve_split(dve, c + j + 2)
            dve.wait_ge(s_cs, 1)
            dve.wait_ge(s_pe, c + 2)
            dve_rope(dve, KR[:, 0], KR[:, 1], bank[5][:, 0:SEQ], bank[5][:, SEQ:], s_kr)
            dve_latent(dve, 0, 2, N_KVL, "g_kv", [bank[4][:, 0:SEQ], bank[4][:, SEQ:]])
            link(dve, nc.vector.memset(KRM[:], 0.0))
            dve_split(dve, c + 4)
            dve.wait_ge(s_pe, c + 3)
            for b in range(4):
                nc.vector.tensor_copy(flat(KN[:, 2 * b:2 * b + 2]), bank[b][:]).then_inc(s_kn, 1)
            dve_split(dve, c + 5)
            dve.wait_ge(s_kr, 1)
            for h in range(4):
                rows = slice(32 * h, 32 * h + 32)
                ins = nc.vector.tensor_copy(KRM[rows, h], KR[rows])
            ins.then_inc(s_kr, 1)
            dve.wait_ge(s_pe, c + 4)
            for t, half, b in ((0, 0, 4), (0, 1, 5), (1, 0, 6), (1, 1, 0)):
                nc.vector.tensor_copy(VM[:, t, half * 512:(half + 1) * 512], bank[b][:]).then_inc(s_vm, 1)

        def pe_mla(pe):
            c = C_MLA
            pe_stat(pe, N_MLA)
            pe.wait_ge(s_vm, 4)
            pe_pair(pe, c, 4, wait=U["mla"])
            pe.wait_ge(s_lo, c + 2)
            for k in range(DT):
                ins = mm3(bank[5][:, 0:SEQ], c + 1, k, hhi[:, k], hlo[:, k], k == 0)
            ins.then_inc(s_q2, 1)
            pe_stat(pe, N_QL)
            pe.wait_ge(s_l, 5)
            outs = [down(m) for m in range(8)] + [bank[6][:, 0:SEQ], bank[6][:, SEQ:], bank[4][:, 0:SEQ],
                                                  bank[4][:, SEQ:]]
            m = 0
            for j, (s0, count) in enumerate(((8, 2), (0, 5), (0, 5))):
                pe.wait_ge(s_lo, c + 2 + j)
                for n in range(count):
                    for k in range(3):
                        ins = mm3(outs[m], c + 1 + j, s0 + 3 * n + k, lhi[:, k], llo[:, k], m % 2 == 0 and k == 0)
                    m += 1
                ins.then_inc(s_pe, 1)
            scale_banks = (4, 5)

            def scores(h):
                b = bank[scale_banks[h % 2]]
                if h >= 2:
                    pe.wait_ge(s_scr, h - 1)
                for qb in range(2):
                    w = P * (qb + 1)
                    o = b[:, qb * P:qb * P + w]
                    qq = slice(qb * P, qb * P + P)
                    mm(o, QN[:, h, qq], KN[:, h, 0:w], qb == 0)
                    mm(o, QR[:, 0, h // 4, qq], KRM[:, h % 4, 0, 0:w], False)
                    ins = mm(o, QR[:, 1, h // 4, qq], KRM[:, h % 4, 1, 0:w], False)
                ins.then_inc(s_sc, 1)

            pe.wait_ge(s_qr, 2)
            pe.wait_ge(s_qn, 4)
            scores(0)
            for h in range(MLA_HEADS):
                if h + 1 < MLA_HEADS:
                    scores(h + 1)
                pe.wait_ge(s_pn, h + 1)
                if h:
                    pe.wait_ge(s_ptr, h)
                for n in range(3):
                    ins = nc.tensor.transpose(bank[6][:, n * P:(n + 1) * P], SC[:, h % 2, n * P:(n + 1) * P], ident)
                ins.then_inc(s_pt, 1)
                pe.wait_ge(s_ptr, h + 1)
                vh = lambda t: VM[:, t, h * P:(h + 1) * P]
                if h:
                    pe.wait_ge(s_h, U["mla_y"] + h)
                mm(down(h)[:, 0:P], vh(0), PT[:, h % 2, 0:P], h % 2 == 0)
                mm(down(h)[:, P:], vh(0), PT[:, h % 2, P:2 * P], False)
                mm(down(h)[:, P:], vh(1), PT[:, h % 2, 2 * P:], False).then_inc(s_pv, 1)
            pe.wait_ge(s_h, U["mla_y"] + MLA_HEADS)
            for j in range(4):
                pe.wait_ge(s_lo, c + 5 + j)
                pe_down_chunk(pe, c + 4 + j, [hhi[:, 2 * j], hhi[:, 2 * j + 1]], [hlo[:, 2 * j], hlo[:, 2 * j + 1]],
                              j == 0)
            pe_stat(pe, N_MPOST)

        s_q2 = sem("query_latent_ready")

        def act_mla(act):
            c = C_MLA
            act_squares(act, N_MLA, lambda j: X[:, j])
            act_rstd(act, N_MLA, D)
            act_modulate(act, mcol(M_COND[1] + 3 * DT), "mla")
            act_split(act, c + 2)
            act_squares(act, N_QL, lambda j: (bank[4][:, 0:SEQ], bank[4][:, SEQ:], bank[5][:, 0:SEQ])[j],
                        lambda j: (s_q2, 1))
            act_rstd(act, N_QL, Q_LORA)
            act_latent(act, 2, 3)
            for j in range(1, 4):
                act_split(act, c + j + 2)
            for h in range(MLA_HEADS):
                act.wait_ge(s_mxx, h + 1)
                for qb in range(2):
                    s = SC[:, h % 2, qb * P:qb * P + P * (qb + 1)]
                    ins = nc.scalar.activation(s, s, ACT.Exp, bias=mx[:, h % 2, qb:qb + 1],
                                               accum_out=sm[:, h % 2, qb:qb + 1])
                ins.then_inc(s_pexp, 1)
                act.wait_ge(s_pt, h + 1)
                nc.scalar.activation(PT[:, h % 2], bank[6][:, 0:3 * P], ACT.Copy).then_inc(s_ptr, 1)
                act.wait_ge(s_pv, h + 1)
                nc.scalar.activation(hhi[:, h], down(h), ACT.Copy).then_inc(s_hhi, 1)
            for j in range(4, 8):
                act_split(act, c + j + 2)
            act_squares(act, N_MPOST, down, lambda j: (s_pe, c + 8))
            act_rstd(act, N_MPOST, D)

        def dve_mla(dve):
            c, m0 = C_MLA, M_COND[1] + 3 * DT
            dve_coef_pre(dve, 3, m0 + DT, ng(1, 1, 0))
            dve_coef_post(dve, 4, m0 + 2 * DT, ng(1, 1, 1), 1.0)
            dve_modulate(dve, N_MLA, cq(3), mcol(m0), "mla")
            dve_split(dve, c + 2)
            dve_latent(dve, 2, 3, N_QL, "g_q", [bank[4][:, 0:SEQ], bank[4][:, SEQ:], bank[5][:, 0:SEQ]])
            for j in range(1, 4):
                dve_split(dve, c + j + 2)
            dve.wait_ge(s_pe, c + 4)
            for g in range(2):
                dve_rope(dve, QR[:, 0, g], QR[:, 1, g], bank[6][:, g * SEQ:(g + 1) * SEQ],
                         bank[4][:, g * SEQ:(g + 1) * SEQ], s_qr)
                dve.wait_ge(s_qr, g + 1)
            for b in range(4):
                nc.vector.tensor_copy(flat(QN[:, 2 * b:2 * b + 2]), bank[b][:]).then_inc(s_qn, 1)

            def softmax(h):
                dve.wait_ge(s_sc, h + 1)
                if h >= 2:
                    dve.wait_ge(s_pt, h - 1)
                s = SC[:, h % 2]
                nc.vector.scalar_tensor_tensor(out=s, in0=bank[(4, 5)[h % 2]][:, 0:3 * P], scalar=(P + ROPE) ** -0.5,
                                               in1=cst("amask"), op0=ALU.mult, op1=ALU.add).then_inc(s_scr, 1)
                dve.wait_ge(s_scr, h + 1)
                for qb in range(2):
                    ins = nc.vector.tensor_reduce(mx[:, h % 2, qb:qb + 1], SC[:, h % 2, qb * P:qb * P + P * (qb + 1)],
                                                  AX.X, ALU.max)
                link(dve, ins)
                nc.vector.tensor_scalar(mx[:, h % 2], mx[:, h % 2], -1.0, None, ALU.mult).then_inc(s_mxx, 1)

            softmax(0)
            for h in range(MLA_HEADS):
                if h + 1 < MLA_HEADS:
                    softmax(h + 1)
                dve.wait_ge(s_pexp, h + 1)
                link(dve, nc.vector.reciprocal(sm[:, h % 2], sm[:, h % 2]))
                for qb in range(2):
                    s = SC[:, h % 2, qb * P:qb * P + P * (qb + 1)]
                    ins = nc.vector.tensor_scalar(s, s, sm[:, h % 2, qb:qb + 1], None, ALU.mult)
                ins.then_inc(s_pn, 1)
                dve.wait_ge(s_hhi, U["mla_y"] + h + 1)
                nc.vector.tensor_tensor(hlo[:, h], down(h), hhi[:, h].bitcast(f32), ALU.subtract).then_inc(s_h, 1)
            for j in range(4, 8):
                dve_split(dve, c + j + 2)
            dve_add_post(dve, N_MPOST, 4, XU["mla"])

        def pe_rest(pe):
            for n, stage in enumerate((lambda: pe_swiglu(pe, 1), lambda: pe_gla(pe), lambda: pe_swiglu(pe, 2),
                                       lambda: pe_swiglu(pe, 3), lambda: (pe_kv(pe), pe_mla(pe)),
                                       lambda: pe_swiglu(pe, 4))):
                if stages >= 3 + n:
                    stage()

        def act_rest(act):
            for n, stage in enumerate((lambda: act_swiglu(act, 1), lambda: act_gla(act), lambda: act_swiglu(act, 2),
                                       lambda: act_swiglu(act, 3), lambda: (act_kv(act), act_mla(act)),
                                       lambda: act_swiglu(act, 4))):
                if stages >= 3 + n:
                    stage()

        def dve_rest(dve):
            for n, stage in enumerate((lambda: dve_swiglu(dve, 1), lambda: dve_gla(dve), lambda: dve_swiglu(dve, 2),
                                       lambda: dve_swiglu(dve, 3), lambda: (dve_kv(dve), dve_mla(dve)),
                                       lambda: dve_swiglu(dve, 4))):
                if stages >= 3 + n:
                    stage()

        @block.tensor
        def _(pe):
            pe_lstm(pe)
            if stages >= 2:
                pe_stat(pe, N_F0)
                pe_ffn(pe, 0, U["f0"])
                pe_stat(pe, N_FIN)
            pe_rest(pe)

        @block.scalar
        def _(act):
            act_lstm(act)
            if stages >= 2:
                act_squares(act, N_F0, lambda j: X[:, j], x_ready(XU["lstm"]))
                act_rstd(act, N_F0, D)
                act_modulate(act, mcol(24), "f0")
                act.wait_ge(s_c2, 16)
                nc.scalar.activation(cb[:], cb[:], ACT.Silu).then_inc(s_cb, 1)
                act_ffn(act, 0)
                act_squares(act, N_FIN, lambda j: X[:, j], x_ready(XU["f0"]))
                act_rstd(act, N_FIN, D)
            act_rest(act)

        @block.vector
        def _(dve):
            dve_lstm(dve)
            if stages >= 2:
                dve_coef_pre(dve, 2, 32, col("g_ffn", 0, 8))
                dve_modulate(dve, N_F0, cq(2), mcol(24), "f0")
                dve.wait_ge(s_cb, 2)
                dve_ffn(dve, 0)
                dve_mod_bias(dve, 48, 88, 72)
                dve.wait_ge(s_pe, C_FFN[0] + FFN_CHUNKS)
                dve_add_plain(dve, 40)
                dve.wait_ge(s_rstd, N_FIN + 1)
                for j in range(DT):
                    nc.vector.scalar_tensor_tensor(out=X[:, j], in0=X[:, j], scalar=col("g_final", j), in1=rs(N_FIN),
                                                   op0=ALU.mult, op1=ALU.mult).then_inc(s_x, 1)
            dve_rest(dve)


def _feature_cols(a):
    import numpy as np
    return np.asarray(a).reshape(-1, P).T


def _tiles(w):
    k, m = w.shape
    return w.reshape(k // P, P, m // P, P).transpose(1, 2, 0, 3)


def _by_output(w):
    return _tiles(w).reshape(P, -1, CW).transpose(1, 0, 2)


def _by_input(w):
    return _tiles(w).transpose(0, 2, 1, 3).reshape(P, -1, CW).transpose(1, 0, 2)


def _wide(w):
    k, m = w.shape
    return w.reshape(k // P, P, m // 512, 512).transpose(1, 2, 0, 3).reshape(P, -1, CW).transpose(1, 0, 2)


def _up_pairs(w):
    k = w.shape[0]
    t = _tiles(w).reshape(P, 2, FT, k // P, P)
    return t.transpose(0, 2, 1, 3, 4).reshape(P, FT, CW).transpose(1, 0, 2)


def _padded(a, width):
    import numpy as np
    out = np.zeros(a.shape[:-1] + (width,), a.dtype)
    out[..., :a.shape[-1]] = a
    return out


def _constants():
    import numpy as np
    con = np.zeros((P, N_CONST), np.float32)

    def put(name, a):
        at, w = CON[name]
        con[:a.shape[0], at:at + w] = a.reshape(a.shape[0], -1)

    put("ident", np.eye(P, dtype=np.float32))
    put("ones", np.ones((P, P), np.float32))
    sel = np.zeros((36, 8, P), np.float32)
    for d in range(2):
        for h in range(4):
            sel[32 * d + h, d * 4 + h] = 1
    put("sel", sel)
    s, t = np.arange(P)[:, None], np.arange(SEQ)[None, :]
    no = np.float32(-1e30)
    madd = np.zeros((P, 2, 2, SEQ), np.float32)
    for st in range(2):
        madd[:, 0, st] = np.where(s + P * st <= t, 0, no)
        madd[:, 1, st] = np.where(s + P * st >= t, 0, no)
    put("madd", madd)
    put("reset", np.broadcast_to((np.arange(SEQ) % CHUNK != 0).astype(np.float32), (P, SEQ)))
    i = np.arange(P)[None, :]
    causal = ((s <= i) & (s // CHUNK == i // CHUNK)).astype(np.float32)
    put("causal", np.concatenate([causal, causal], axis=1))
    put("amask", np.concatenate([np.where(i <= s, 0, no), np.zeros((P, P)), np.where(i <= s, 0, no)], axis=1))
    return con


def kernel(**inputs):
    import numpy as np
    import concourse.bacc as bacc
    from concourse.bass_utils import run_bass_kernel_spmd as run

    v = {k: np.asarray(a) for k, a in inputs.items()}
    w_in, w_gla = v["a_w_in"][0], v["gla_w_in_2"][0]
    gates = w_in[:, 3072:]
    wg = np.zeros((D, P), np.float32)
    b_gate = np.zeros((P, 1), np.float32)
    for n, row in enumerate((0, 32, 64, 96)):
        wg[:, row:row + HEADS] = gates[:, n * HEADS:(n + 1) * HEADS]
        b_gate[row:row + HEADS, 0] = v["a_b_gate"][0, n * HEADS:(n + 1) * HEADS]
    kv_a, kv_b = v["mla_w_kv_a_2"], v["mla_w_kv_b_2"].reshape(256, MLA_HEADS, 2, P)
    pe = [kv_a[:, 256 + 32 * n:288 + 32 * n] for n in range(2)]
    uq = v["mla_w_uq_2"][0].reshape(Q_LORA, MLA_HEADS, P + ROPE)
    uq = np.concatenate([uq[:, :, :P].reshape(Q_LORA, -1), uq[:, :, P:P + 32].reshape(Q_LORA, -1),
                         uq[:, :, P + 32:].reshape(Q_LORA, -1)], axis=1)
    uq = _tiles(uq).reshape(P, 12, 3 * P)
    dq = _tiles(v["mla_w_dq_2"][0]).reshape(P, 3, DT * P)
    gu, dn = v["ffn_w_gu_2"], v["ffn_w_down_2"]

    def ffn(up, down):
        return [_up_pairs(up), _by_input(down)]

    stream = [_by_output(w_in[:, :1024]), _wide(w_in[:, 1024:2048]), _padded(_tiles(wg).reshape(P, -1), CW)[None],
              _by_output(w_in[:, 2048:3072]), _by_input(v["a_w_out"][0]),
              *ffn(v["f_w_up"][0], v["f_w_down"][0]), *ffn(gu[0, 0], dn[0, 0]),
              _padded(_tiles(_padded(w_gla[:, 2048:2064], P)).reshape(P, -1), CW)[None],
              _by_output(w_gla[:, :1024]), _wide(w_gla[:, 1024:2048]), _by_output(w_gla[:, 2064:]),
              _by_input(v["gla_w_out_2"][0]), *ffn(gu[0, 1], dn[0, 1]), *ffn(gu[1, 0], dn[1, 0]),
              _by_output(np.concatenate([kv_a[:, :256]] + [pe[0]] * 4 + [pe[1]] * 4, axis=1)),
              _by_output(kv_b[:, :, 0].reshape(256, -1)),
              kv_b[:, :, 1].reshape(2, P, D).transpose(1, 0, 2).reshape(1, P, CW),
              dq[:, :2].reshape(1, P, CW),
              _padded(np.concatenate([dq[:, 2], uq[:, :2].reshape(P, -1)], axis=1), CW)[None],
              _padded(uq[:, 2:7].reshape(P, -1), CW)[None], _padded(uq[:, 7:].reshape(P, -1), CW)[None],
              _by_input(v["mla_w_out_2"][0]), *ffn(gu[1, 1], dn[1, 1])]
    w_stream = np.ascontiguousarray(np.concatenate(stream, axis=0))
    assert w_stream.shape == (N_CHUNKS, P, CW)
    w_mod = v["w_mod"][0]
    rows = np.concatenate([w_mod[:, FIRST_MODS * P:].T, v["cond_w_2"][0].T, v["kv_cond_w_2"].T, v["cond_w_2"][1].T])
    invf = (10000.0 ** (-np.arange(0, ROPE, 2, dtype=np.float32) / np.float32(ROPE))).astype(np.float32)
    cw = v["f_w_conv"][0]
    cols = np.concatenate([_feature_cols(a) for a in (
        v["b_mod"][0], v["cond_b_2"][0], v["kv_cond_b_2"], v["cond_b_2"][1], v["g_mix"][0], v["g_ffn"][0],
        v["g_final"], v["a_head_gain"][0], cw[0], cw[1], cw[2], v["f_b_conv"][0], v["norm_g_2"].reshape(-1),
        v["kv_g_in_2"], v["gla_g_out_2"][0], v["gla_b_gate_2"][0], v["mla_g_kv_2"], v["mla_g_q_2"][0], b_gate,
        np.tile(invf, 4))], axis=1)

    def features(x):
        return x.reshape(SEQ, DT, P).transpose(2, 1, 0)

    data = {
        "w_stream": w_stream, "w_first": w_mod[:, :FIRST_MODS * P].reshape(DT, P, CW),
        "m_stream": rows.reshape(-1, P, D), "w_gup": v["gla_w_gate_up_2"][0],
        "xT": features(v["x"]), "ctxT": features(v["ctx"]),
        "c_cols": np.stack([_feature_cols(v["c"]), _feature_cols(v["c_ctx"])], axis=2),
        "c_row": v["c"].reshape(D), "c2_row": v["c_2"].reshape(D), "cols_d": cols, "const_d": _constants(),
        "pos_d": v["positions_2"].reshape(SEQ),
    }
    nc = bacc.Bacc("TRN2", target_bir_lowering=False, num_devices=1)
    dt, arrays, args = mybir.dt, {}, {}
    for name, a in data.items():
        a = np.ascontiguousarray(a)
        arrays[name] = a
        args[name] = nc.dram_tensor(name, a.shape, dt.int32 if a.dtype.kind == "i" else dt.float32,
                                    kind="ExternalInput").ap()
    out = nc.dram_tensor("y", (P, DT, SEQ), dt.float32, kind="ExternalOutput").ap()
    build(nc, **args, out_d=out)
    y = run(nc, [arrays], core_ids=[0]).results[0]["y"]
    return np.ascontiguousarray(np.asarray(y).transpose(2, 1, 0)).reshape(1, SEQ, D)
```

```python
import concourse.bass as bass
from concourse import mybir
from contextlib import ExitStack
import numpy as np

D, SEQ, FF = 1024, 256, 2816
P = 128
DT = D // P
FT = FF // P
HEADS, DK, DV, CHUNK = 4, 128, 256, 64
MLA_HEADS, ROPE, Q_LORA = 8, 64, 384
EPS = 1e-6
TILES = 16
CW = TILES * P

FFN_CHUNKS = FT + FT // 2
C_LSTM = DT
C_FFN = [25, 58, 108, 141, 186]
C_GLA = 91
C_KV = 174
C_MLA = 178
N_CHUNKS = C_FFN[-1] + FFN_CHUNKS
M_COND = [48, 136]
M_KV = 120
N_MOD = 208
FIRST_MODS = 16
_names = [("g_mix", 8), ("g_ffn", 8), ("g_final", 8), ("gain", 8), ("cw0", FT), ("cw1", FT), ("cw2", FT),
          ("cb", FT), ("norm_g", 96), ("kv_g", 8), ("g_out", 2), ("b_gla", 4), ("g_kv", 2), ("g_q", 3),
          ("b_gate", 1), ("invf", 1)]
COL, _at = {}, N_MOD
for _n, _w in _names:
    COL[_n] = (_at, _w)
    _at += _w
N_COLS = _at
_names = [("ident", P), ("ones", P), ("sel", 8 * P), ("madd", 4 * SEQ), ("reset", SEQ),
          ("causal", SEQ), ("amask", 3 * P)]
CON, _at = {}, 0
for _n, _w in _names:
    CON[_n] = (_at, _w)
    _at += _w
N_CONST = _at


def build(nc, w_stream, m_stream, w_gup, xT, ctxT, c_cols, c_row, c2_row, cols_d, const_d,
          pos_d, out_d, stages=99):
    f32, f32r, i32 = mybir.dt.float32, mybir.dt.float32r, mybir.dt.int32
    ALU, ACT, AX = mybir.AluOpType, mybir.ActivationFunctionType, mybir.AxisListType
    LN_EXP = "natural_log_exp_and_others"
    NCH = {1: 25, 2: 58, 3: 91, 4: 108, 5: 141, 6: 174, 7: 186}.get(stages, N_CHUNKS)
    NMU = 32 + 40 * {0: 0, 1: 0, 2: 1, 3: 2, 4: 2, 5: 3}.get(stages, 4)
    XUP = {0: 0, 1: 8, 2: 24, 3: 32, 4: 40, 5: 48, 6: 56, 7: 64}.get(stages, 72)

    ctx = ExitStack()
    with ctx:
        def sb(name, shape, dt=f32):
            return ctx.enter_context(nc.sbuf_tensor(name, shape, dt))

        sems = {}

        def sem(name):
            if name not in sems:
                sems[name] = ctx.enter_context(nc.semaphore(name))
            return sems[name]

        raw = sb("raw", [P, 3, CW])
        whi = sb("whi", [P, 3, CW], f32r)
        wlo = sb("wlo", [P, 3, CW], f32r)
        mring = sb("mring", [P, 2, D])
        X = sb("X", [P, DT, SEQ])
        hhi = sb("hhi", [P, DT, SEQ], f32r)
        hlo = sb("hlo", [P, DT, SEQ], f32r)
        cb = sb("cb", [P, D])
        cols = sb("cols", [P, N_COLS])
        con = sb("con", [P, N_CONST])
        mod = sb("mod", [P, N_MOD])
        modc = sb("modc", [P, FIRST_MODS])
        ccol = sb("ccol", [P, DT, 2])
        scol = sb("scol", [P, DT, 2])
        coef = sb("coef", [P, 16, DT])
        eps = sb("eps", [P, 1])
        lnt = sb("lnt", [P, SEQ])
        rstd = sb("rstd", [P, 2, SEQ])
        T = sb("T", [P, 3, SEQ])
        SG = sb("SG", [P, 3, SEQ])
        CG = sb("CG", [P, SEQ])
        rd = sb("rd", [P, 2, SEQ])
        uc = sb("uc", [P, 4, 36])
        arena = sb("arena", [P, 68 * 256])
        base = nc.sbuf_base - 68 * 1024

        def at(name, kb, shape, dt=f32):
            return nc.alloc_sbuf_tensor_at(name, shape, dt, offset=base + int(kb * 1024))

        c4 = at("c4", 0, [P, DT, P], f32r)
        mrow = at("mrow", 4, [4, FIRST_MODS * P])
        hid_hi = at("hid_hi", 8, [P, FT, SEQ], f32r)
        hid_lo = at("hid_lo", 8 + FT, [P, FT, SEQ], f32r)
        XC = at("XC", 44, [P, DT, SEQ])
        thb = at("thb", 0, [P, HEADS, 2, SEQ])
        chi = at("chi", 8, [P, DT, SEQ], f32r)
        OS = at("OS", 8, [P, DT, SEQ])
        clo = at("clo", 16, [P, DT, SEQ], f32r)
        EF = [at("EF0", 54, [P, 2, 4, SEQ]), at("EF1", 16, [P, 2, 4, SEQ])]
        Q = at("Q", 24, [P, HEADS, SEQ])
        K = at("K", 28, [P, HEADS, 2 * SEQ])
        V = at("V", 36, [P, 4, D])
        GQ = at("GQ", 0, [P, HEADS, SEQ])
        GK = at("GK", 4, [P, HEADS, SEQ])
        LA = at("LA", 8, [P, HEADS, SEQ])
        LB = at("LB", 12, [P, HEADS, SEQ])
        EB = at("EB", 16, [P, HEADS, SEQ])
        EN = at("EN", 20, [P, HEADS, SEQ])
        GV = at("GV", 24, [P, 2, D])
        SR = at("SR", 32, [P, DT, SEQ])
        GKU = at("GKU", 40, [P, HEADS, SEQ])
        wgu = at("wgu", 44, [16, HEADS * DK])
        glow = at("glow", 46, [16, SEQ])
        ST = at("ST", 47, [P, 3, DV])
        att = at("att", 50, [P, 2, P])
        kut = at("kut", 51, [P, 2, P])
        KN = at("KN", 0, [P, MLA_HEADS, SEQ])
        VM = at("VM", 8, [P, 2, D])
        KR = at("KR", 16, [P, 2, SEQ])
        QN = at("QN", 18, [P, MLA_HEADS, SEQ])
        QR = at("QR", 26, [P, 2, 2, SEQ])
        KRM = at("KRM", 30, [P, 4, 2, SEQ])
        lhi = at("lhi", 38, [P, 3, SEQ], f32r)
        llo = at("llo", 41, [P, 3, SEQ], f32r)
        SC = at("SC", 44, [P, 2, 3 * P])
        PT = at("PT", 47, [P, 2, 3 * P])
        SQ = at("SQ", 52, [P, DT, SEQ])
        gf = at("gf", 54, [36, 512])
        ga = at("ga", 56, [36, 512])
        gb = at("gb", 58, [36, 512])
        XS = at("XS", 60, [P, DT, SEQ])
        g_all = at("g_all", 60, [P, 512])
        gi = at("gi", 62, [36, 512])
        ut = at("ut", 64, [36, 512])
        mt = at("mt", 66, [36, SEQ])
        th = at("th", 67, [36, SEQ])
        mx = sb("mx", [P, 2, 2])
        sm = sb("sm", [P, 2, 2])

        bank = [ctx.enter_context(nc.psum_tensor(f"bank{b}", [P, 512], f32)) for b in range(8)]
        block = ctx.enter_context(nc.Block())

        def col(name, j=0, n=None):
            a, w = COL[name]
            return cols[:, a + j:a + j + (n or 1)]

        def cst(name):
            a, w = CON[name]
            return con[:, a:a + w]

        ident, ones = cst("ident"), cst("ones")

        s_raw = [sem(f"raw_loaded{j}") for j in range(3)]
        s_hi, s_lo, s_pe = sem("chunk_rounded"), sem("chunk_rest"), sem("chunk_used")
        s_mod = [sem(f"mod_loaded{j}") for j in range(2)]
        s_mused = sem("mod_used")

        def run(i, per):
            return 0 if i is None else i * per

        def act_split(act, c, i=None):
            if c >= NCH:
                return
            act.wait_ge(s_raw[c % 3], 16 * (c // 3 + 1) + run(i, 16))
            if c >= 3:
                act.wait_ge(s_pe, c - 2 + run(i, 3))
            nc.scalar.activation(whi[:, c % 3], raw[:, c % 3], ACT.Copy).then_inc(s_hi, 1)

        def dve_split(dve, c, i=None):
            if c >= NCH:
                return
            dve.wait_ge(s_hi, c + 1 + run(i, 3))
            nc.vector.tensor_tensor(wlo[:, c % 3], raw[:, c % 3], whi[:, c % 3].bitcast(f32),
                                    ALU.subtract).then_inc(s_lo, 1)

        def mm3(out, c, s, rhi, rlo, start):
            wh, wl = whi[:, c % 3, s * P:(s + 1) * P], wlo[:, c % 3, s * P:(s + 1) * P]
            nc.tensor.matmul(out, wh, rhi, start=start, stop=True, skip_group_check=True)
            nc.tensor.matmul(out, wh, rlo, start=False, stop=True, skip_group_check=True)
            return nc.tensor.matmul(out, wl, rhi, start=False, stop=True, skip_group_check=True)

        def mm(out, lhsT, rhs, start):
            return nc.tensor.matmul(out, lhsT, rhs, start=start, stop=True, skip_group_check=True)

        s_h = sem("input_tile_split")
        s_hhi = sem("input_tile_rounded")

        def pe_pair(pe, c, bk, hi=hhi, lo=hlo, last=True, wait=None):
            pe.wait_ge(s_lo, c + 1)
            for m in range(2):
                for k in range(DT):
                    if m == 0 and wait is not None:
                        pe.wait_ge(s_h, wait + k + 1)
                    ins = mm3(bank[bk][:, m * SEQ:(m + 1) * SEQ], c, m * DT + k, hi[:, k], lo[:, k], k == 0)
            if last:
                ins.then_inc(s_pe, 1)

        def pe_wide(pe, c, k0, outs, his, los):
            pe.wait_ge(s_lo, c + 1)
            for n, o in enumerate(outs):
                for g in range(4):
                    k = k0 + g
                    wh, wl = whi[:, c % 3, g * 512:(g + 1) * 512], wlo[:, c % 3, g * 512:(g + 1) * 512]
                    mm(o, his[n](k), wh, k == 0)
                    mm(o, his[n](k), wl, False)
                    ins = mm(o, los[n](k), wh, False)
            ins.then_inc(s_pe, 1)

        s_down = sem("output_bank_ready")

        def pe_down_chunk(pe, c, khi, klo, first, last=False):
            order = [(g, m + n) for m in range(0, DT, 2) for g in range(2) for n in range(2)] if last else \
                [(g, m) for g in range(2) for m in range(DT)]
            for g, m in order:
                ins = mm3(down(m), c, g * DT + m, khi[g], klo[g], first and g == 0 and m % 2 == 0)
                if last and g and m % 2 and m < DT - 1:
                    ins.then_inc(s_down, 1)
            ins.then_inc(s_pe, 1)

        def down(m):
            return bank[m // 2][:, (m % 2) * SEQ:(m % 2 + 1) * SEQ]

        s_sq, s_stat, s_rstd, s_ln = sem("squares"), sem("mean_square"), sem("rstd"), sem("log_mean_square")
        NORMS = ([8, 8] + [2] * 4 + [8, 8] + [8, 8] + [8] + [2] * 4 + [8] + [8, 8]
                 + [8, 8] + [8, 2] + [8, 3, 8] + [8, 8])
        N_X1, N_CTX, N_LSTM, N_F0, N_FIN, N_F1, N_GLA, N_GHEAD, N_GPOST, N_F2 = 0, 1, 2, 6, 7, 8, 10, 11, 15, 16
        N_F3, N_KV, N_KVL, N_MLA, N_QL, N_MPOST, N_F4 = 18, 20, 21, 22, 23, 24, 25

        def act_squares(act, n, src, wait=None, table=True):
            if table:
                act.preload_act_table_set(LN_EXP)
            for j in range(NORMS[n]):
                if wait is not None:
                    act.wait_ge(*wait(j))
                if n and j == 0:
                    act.wait_ge(s_stat, n)
                nc.scalar.activation(SQ[:, j], src(j), ACT.Square).then_inc(s_sq, 1)

        def pe_stat(pe, n):
            before = sum(NORMS[:n])
            if n:
                pe.wait_ge(s_ln, n)
            for j in range(NORMS[n]):
                pe.wait_ge(s_sq, before + j + 1)
                ins = mm(bank[7][:, (n % 2) * SEQ:(n % 2 + 1) * SEQ], ones, SQ[:, j], j == 0)
            ins.then_inc(s_stat, 1)

        def act_rstd(act, n, dim):
            act.wait_ge(s_stat, n + 1)
            if n:
                act.wait_ge(s_rstd, n)
            nc.scalar.activation(lnt[:], bank[7][:, (n % 2) * SEQ:(n % 2 + 1) * SEQ], ACT.Ln, bias=eps[:, 0:1],
                                 scale=1.0 / dim).then_inc(s_ln, 1)
            act.wait_ge(s_ln, n + 1)
            nc.scalar.activation(rstd[:, n % 2], lnt[:], ACT.Exp, scale=-0.5).then_inc(s_rstd, 1)

        def rs(n):
            return rstd[:, n % 2]

        s_vstep = sem("vector_step")
        vsteps = [0]

        def link(dve, ins):
            vsteps[0] += 1
            ins.then_inc(s_vstep, 1)
            dve.wait_ge(s_vstep, vsteps[0])

        s_astep = sem("scalar_step")
        asteps = [0]

        def alink(act, ins):
            asteps[0] += 1
            ins.then_inc(s_astep, 1)
            act.wait_ge(s_astep, asteps[0])

        s_t = sem("input_tile_scaled")

        MODULATED = ["x1", "ctx", "f0", "f1", "gla", "f2", "f3", "kv", "mla", "f4"]

        def dve_modulate(dve, n, A, sh, stage, src=None, hi=hhi, lo=hlo):
            u0 = U[stage]
            dve.wait_ge(s_rstd, n + 1)
            for j in range(DT + 1):
                if j < DT:
                    if u0 or j >= 3:
                        dve.wait_ge(s_h, u0 + max(j - 2, 0))
                    nc.vector.scalar_tensor_tensor(out=T[:, j % 3], in0=(src or X)[:, j], scalar=A(j), in1=rs(n),
                                                   op0=ALU.mult, op1=ALU.mult).then_inc(s_t, 1)
                if j:
                    k = j - 1
                    dve.wait_ge(s_hhi, u0 + k + 1)
                    nc.vector.scalar_tensor_tensor(out=lo[:, k], in0=T[:, k % 3], scalar=sh(k),
                                                   in1=hi[:, k].bitcast(f32), op0=ALU.add,
                                                   op1=ALU.subtract).then_inc(s_h, 1)

        def act_modulate(act, sh, stage, hi=hhi):
            t0 = 8 * MODULATED.index(stage)
            for j in range(DT):
                act.wait_ge(s_t, t0 + j + 1)
                nc.scalar.activation(hi[:, j], T[:, j % 3], ACT.Identity, bias=sh(j)).then_inc(s_hhi, 1)

        U = {n: 8 * i for i, n in enumerate(
            ["x1", "ctx", "lstm_y", "f0", "f1", "gla", "gla_y", "f2", "f3", "kv", "mla", "mla_y", "f4"])}

        def dve_mod_unit(dve, u, i=None, per=0):
            dve.wait_ge(s_mod[u % 2], 16 * (u // 2 + 1) + run(i, 8 * per))
            a = FIRST_MODS + u
            dst = mod[:, a:a + 1] if i is None else mod[:, bass.ds(i * per + a, 1)]
            nc.vector.scalar_tensor_tensor(out=mring[:, u % 2], in0=mring[:, u % 2], scalar=1.0, in1=cb[:],
                                           op0=ALU.mult, op1=ALU.mult, accum_out=dst).then_inc(s_mused, 1)

        def dve_mod_bias(dve, a, b, units):
            dve.wait_ge(s_mused, units)
            link(dve, nc.vector.tensor_tensor(mod[:, a:b], mod[:, a:b], cols[:, a:b], ALU.add))

        def dve_coef_pre(dve, q, scale_at, g, src=None):
            src = mod if src is None else src
            link(dve, nc.vector.scalar_tensor_tensor(out=coef[:, q], in0=src[:, scale_at:scale_at + DT], scalar=1.0,
                                                     in1=g, op0=ALU.add, op1=ALU.mult))

        def dve_coef_post(dve, q, gate_at, g, w):
            link(dve, nc.vector.scalar_tensor_tensor(out=coef[:, q], in0=mod[:, gate_at:gate_at + DT], scalar=w,
                                                     in1=g, op0=ALU.mult, op1=ALU.mult))

        def mcol(a):
            return lambda j: mod[:, a + j:a + j + 1]

        def cq(q):
            return lambda j: coef[:, q, j:j + 1]

        s_x = sem("x_tile_updated")
        XU = {n: 8 * i for i, n in enumerate(["lstm", "f0", "fin", "f1", "gla", "f2", "f3", "mla", "f4"])}

        def down_done(d, m, c):
            return (s_pe, c + 1) if m >= DT - 2 else (s_down, 3 * d + m // 2 + 1)

        def dve_add_plain(dve, gate_at, d, c):
            for m in range(DT):
                if m % 2 == 0:
                    dve.wait_ge(*down_done(d, m, c))
                nc.vector.scalar_tensor_tensor(out=X[:, m], in0=down(m), scalar=mod[:, gate_at + m:gate_at + m + 1],
                                               in1=X[:, m], op0=ALU.mult, op1=ALU.add).then_inc(s_x, 1)

        s_tp = sem("post_tile_scaled")
        tposts = [0]

        def dve_add_post(dve, n, q, x0):
            dve.wait_ge(s_rstd, n + 1)
            for m in range(DT + 1):
                if m < DT:
                    if m >= 3:
                        dve.wait_ge(s_x, x0 + m - 2)
                    nc.vector.scalar_tensor_tensor(out=T[:, m % 3], in0=down(m), scalar=coef[:, q, m:m + 1],
                                                   in1=rs(n), op0=ALU.mult, op1=ALU.mult).then_inc(s_tp, 1)
                if m:
                    tposts[0] += 1
                    dve.wait_ge(s_tp, tposts[0])
                    nc.vector.tensor_tensor(X[:, m - 1], X[:, m - 1], T[:, (m - 1) % 3], ALU.add).then_inc(s_x, 1)

        s_silu, s_prod = sem("hidden_silu"), sem("hidden_product")
        s_hidhi, s_hid, s_conv, s_cstep = sem("hidden_rounded"), sem("hidden_split"), sem("gate_conv"), sem("conv_step")
        UP_TURNS, DOWN_TURNS = FT // 3, 2

        def hid(t, i, buf):
            return buf[:, t] if i is None else buf[:, bass.ds(i * 3 + t, 1), :].rearrange("p a b -> p (a b)")

        def up_parts(body, eng, f):
            peeled = 1 if f else 4
            for t in range(peeled):
                body(t, None)
            with eng.Fori(0, (FT - peeled) // 3) as i:
                for t in range(peeled, peeled + 3):
                    body(t, i)

        def down_parts(body, eng):
            body(0, None)
            body(1, None)
            with eng.Fori(0, DOWN_TURNS) as i:
                for d in range(2, 5):
                    body(d, i)
            for d in range(2 + 3 * DOWN_TURNS, FT // 2):
                body(d, None)

        def pe_ffn(pe, f, u0):
            c0 = C_FFN[f]
            def up(t, i):
                pe.wait_ge(s_lo, c0 + t + 1 + run(i, 3))
                if f or t >= 3:
                    pe.wait_ge(s_prod, FT * f + t - 2 + run(i, 3))
                b = bank[4 + t % 3]
                if t == 0 and i is None:
                    for k in range(DT):
                        pe.wait_ge(s_h, u0 + k + 1)
                        for m in range(2):
                            ins = mm3(b[:, m * SEQ:(m + 1) * SEQ], c0, m * DT + k, hhi[:, k], hlo[:, k],
                                      k == 0 and m == 0)
                else:
                    for m in range(2):
                        for k in range(DT):
                            ins = mm3(b[:, m * SEQ:(m + 1) * SEQ], c0 + t, m * DT + k, hhi[:, k], hlo[:, k], k == 0)
                ins.then_inc(s_pe, 1)

            up_parts(up, pe, f)

            def dn(d, i):
                c = c0 + FT + d
                pe.wait_ge(s_lo, c + 1 + run(i, 3))
                pe.wait_ge(s_hid, FT * f + 2 * d + 2 + run(i, 6))
                hi = [hid_hi[:, 2 * d + g] if i is None else
                      hid_hi[:, bass.ds(i * 6 + 2 * d + g, 1), :].rearrange("p a b -> p (a b)") for g in range(2)]
                lo = [hid_lo[:, 2 * d + g] if i is None else
                      hid_lo[:, bass.ds(i * 6 + 2 * d + g, 1), :].rearrange("p a b -> p (a b)") for g in range(2)]
                pe_down_chunk(pe, c, hi, lo, d == 0, d == FT // 2 - 1)

            down_parts(dn, pe)

        def conv_columns(t, i):
            return [cols[:, COL[n][0] + t:COL[n][0] + t + 1] if i is None else
                    cols[:, bass.ds(i * 3 + COL[n][0] + t, 1)] for n in ("cw0", "cw1", "cw2", "cb")]

        def act_ffn(act, f):
            c0 = C_FFN[f]
            act_split(act, c0 + 2)

            def up(t, i):
                act.wait_ge(s_pe, c0 + t + 1 + run(i, 3))
                gate = bank[4 + t % 3][:, 0:SEQ]
                if f == 0:
                    w = conv_columns(t, i)
                    nc.scalar.activation(CG[:], gate, ACT.Identity, bias=w[3], scale=w[1]).then_inc(s_cstep, 1)
                    act.wait_ge(s_conv, t + 1 + run(i, 3))
                    gate = CG[:]
                nc.scalar.activation(SG[:, t % 3], gate, ACT.Silu).then_inc(s_silu, 1)
                act_split(act, c0 + t + 3, i)
                act.wait_ge(s_prod, FT * f + t + 1 + run(i, 3))
                nc.scalar.activation(hid(t, i, hid_hi), T[:, t % 3], ACT.Copy).then_inc(s_hidhi, 1)

            up_parts(up, act, f)
            down_parts(lambda d, i: d < FT // 2 - 1 and act_split(act, c0 + FT + d + 3, i), act)

        def dve_ffn(dve, f):
            c0, u0 = C_FFN[f], 32 + 40 * f

            def rest(t, i):
                dve.wait_ge(s_hidhi, FT * f + t + 1 + run(i, 3))
                nc.vector.tensor_tensor(hid(t, i, hid_lo), T[:, t % 3], hid(t, i, hid_hi).bitcast(f32),
                                        ALU.subtract).then_inc(s_hid, 1)

            def mods(t, i, at):
                if f < 4 and t:
                    for u in ((0,), (1,), (2, 3))[(t - 1) % 3][at:at + 1]:
                        dve_mod_unit(dve, u0 + 4 * ((t - 1) // 3) + u, i, 4)

            def up(t, i):
                dve_split(dve, c0 + t + 2, i)
                b = bank[4 + t % 3]
                if f == 0:
                    w = conv_columns(t, i)
                    dve.wait_ge(s_cstep, 2 * t + 1 + run(i, 6))
                    nc.vector.scalar_tensor_tensor(out=CG[:, 64:256], in0=b[:, 0:192], scalar=w[0], in1=CG[:, 64:256],
                                                   op0=ALU.mult, op1=ALU.add).then_inc(s_cstep, 1)
                    dve.wait_ge(s_cstep, 2 * t + 2 + run(i, 6))
                    nc.vector.scalar_tensor_tensor(out=CG[:, 0:192], in0=b[:, 64:256], scalar=w[2], in1=CG[:, 0:192],
                                                   op0=ALU.mult, op1=ALU.add).then_inc(s_conv, 1)
                mods(t, i, 0)
                dve.wait_ge(s_silu, FT * f + t + 1 + run(i, 3))
                if FT * f + t > 2:
                    dve.wait_ge(s_hid, FT * f + t - 2 + run(i, 3))
                nc.vector.tensor_tensor(T[:, t % 3], SG[:, t % 3], b[:, SEQ:2 * SEQ], ALU.mult).then_inc(s_prod, 1)
                if t:
                    rest(t - 1, i)
                mods(t, i, 1)

            up_parts(up, dve, f)
            rest(FT - 1, None)

            def dn(d, i):
                dve_split(dve, c0 + FT + d + 2, i)
                if f < 4 and d >= 2:
                    for u in ((0,), (1,), (2, 3))[(d - 2) % 3]:
                        dve_mod_unit(dve, u0 + 4 * (UP_TURNS + (d - 2) // 3) + u, i, 4)

            down_parts(dn, dve)

        s_in = [sem(f"inputs_loaded{j}") for j in range(8)]
        s_gup, s_c2 = sem("gla_gate_weights_loaded"), sem("second_c_loaded")
        s_out = sem("output_stored")

        @block.sync
        def _(sp):
            sp.dma_start(ccol[:], c_cols).then_inc(s_in[0], 16)
            for c in range(3):
                sp.dma_start(raw[:, c], w_stream[c]).then_inc(s_raw[c], 16)
            sp.dma_start(X[:], xT).then_inc(s_in[3], 16)
            sp.dma_start(con[:, 0:2 * P], const_d[:, 0:2 * P]).then_inc(s_in[1], 16)

            def chunks(a, b):
                for c in range(a, b):
                    sp.wait_ge(s_lo, c - 2)
                    sp.dma_start(raw[:, c % 3], w_stream[c]).then_inc(s_raw[c % 3], 16)

            chunks(3, 5)
            sp.dma_start(cols[:], cols_d).then_inc(s_in[1], 16)
            sp.dma_start(XC[:], ctxT).then_inc(s_in[2], 16)
            chunks(5, 12)
            sp.dma_start(con[:, 2 * P:], const_d[:, 2 * P:]).then_inc(s_in[5], 16)
            turns = (NCH - 12) // 3
            with sp.Fori(0, turns) as i:
                for j in range(3):
                    sp.wait_ge(s_lo, i * 3 + (j + 10))
                    sp.dma_start(raw[:, j], w_stream[bass.ds(i * 3 + (j + 12), 1)]
                                 .rearrange("a p n -> p (a n)")).then_inc(s_raw[j], 16)
            chunks(12 + 3 * turns, NCH)
            sp.wait_ge(s_x, XUP)
            sp.dma_start(out_d, X[:]).then_inc(s_out, 16)
            sp.wait_ge(s_out, 16)

        @block.gpsimd
        def _(pool):
            pool.wait_ge(s_lo, 6)
            pool.dma_start(cb[:], c_row.partition_broadcast(P)).then_inc(s_in[4], 16)
            for u in range(2):
                pool.dma_start(mring[:, u], m_stream[u]).then_inc(s_mod[u], 16)

            def mods(u0, turns):
                with pool.Fori(0, turns) as i:
                    for j in range(2):
                        pool.wait_ge(s_mused, i * 2 + (u0 + j - 1))
                        pool.dma_start(mring[:, j], m_stream[bass.ds(i * 2 + (u0 + j), 1)]
                                       .rearrange("a p n -> p (a n)")).then_inc(s_mod[j], 16)

            mods(2, 15)
            if NMU > 32:
                pool.wait_ge(s_mused, 32)
                pool.dma_start(cb[:], c2_row.partition_broadcast(P)).then_inc(s_c2, 16)
                mods(32, (NMU - 32) // 2)

        s_scol, s_c4h, s_c4 = sem("c_silu"), sem("c_rounded"), sem("c_split")
        s_mrow, s_mT, s_mm0 = sem("first_mods_rows"), sem("first_mods_columns"), sem("first_mods_read")
        s_cb = sem("c_rows_silu")
        s_eps = sem("eps_set")
        s_qk, s_vb = sem("qk_bank_read"), sem("v_bank_read")
        s_gr = sem("gates_read")
        s_ga, s_gd = sem("gate_exp_ln"), sem("gate_rows")
        s_uT, s_uc = sem("u_columns"), sem("u_columns_read")
        s_os, s_ad, s_sg = sem("o_bank_read"), sem("denominators_abs"), sem("o_sigmoid")
        s_bc, s_s = sem("decay_rows_broadcast"), sem("qk_scores")
        s_arg, s_e = sem("decay_exponents"), sem("decay_weights")
        s_p, s_den = sem("weighted_scores"), sem("denominators")
        s_th, s_gw2, s_num = sem("threshold_read"), sem("normalised_scores"), sem("numerators")
        s_y = sem("gated_tile")
        EXPS = 5

        def head_bank(h):
            return bank[(6, 4)[h % 2]]

        def pe_lstm(pe):
            c = C_LSTM
            pe.wait_ge(s_c4, 1)
            for k in range(DT):
                pe.wait_ge(s_lo, k + 1)
                for g in range(4):
                    mm(bank[g][:], c4[:, k], whi[:, k % 3, g * 512:(g + 1) * 512], k == 0)
                    ins = mm(bank[g][:], c4[:, k], wlo[:, k % 3, g * 512:(g + 1) * 512], False)
                ins.then_inc(s_pe, 1)
                if k == 4:
                    pe.wait_ge(s_in[1], 32)
                    pe_stat(pe, N_X1)
            pe_stat(pe, N_CTX)
            pe.wait_ge(s_mrow, 4)
            for m in range(FIRST_MODS):
                ins = nc.tensor.transpose(bank[4][:, 4 * m:4 * m + 4], mrow[:, m * P:(m + 1) * P], ident[0:4, 0:4])
            ins.then_inc(s_mT, 1)
            pe.wait_ge(s_mm0, 1)
            for j in range(2):
                pe_pair(pe, c + j, 4 + j, wait=U["x1"] if j == 0 else None)
            pe.wait_ge(s_lo, c + 3)
            pe.wait_ge(s_ln, 2)
            for n, hi, lo in ((1, hhi, hlo), (0, chi, clo)):
                for k in range(DT):
                    if n == 0:
                        pe.wait_ge(s_h, U["ctx"] + k + 1)
                    ins = mm3(bank[7][:, n * SEQ:(n + 1) * SEQ], c + 2, k, hi[:, k], lo[:, k], k == 0)
            ins.then_inc(s_pe, 1)
            for j in range(2):
                for n, (hi, lo) in enumerate(((hhi, hlo), (chi, clo))):
                    a = 2 + 2 * j + n
                    if a >= 3:
                        pe.wait_ge(s_qk, a - 2)
                    pe_pair(pe, c + 3 + j, 4 + a % 3, hi, lo, n == 1)
            tiles = [(chi, clo, 0), (chi, clo, 1), (hhi, hlo, 0), (hhi, hlo, 1)]
            his = [lambda k, b=b, t=t: b[:, k, t * P:(t + 1) * P] for b, _, t in tiles]
            los = [lambda k, b=b, t=t: b[:, k, t * P:(t + 1) * P] for _, b, t in tiles]
            def values(j):
                pe_wide(pe, c + 5 + j, 4 * (j % 2), [bank[b + 4 * (j // 2)][:] for b in range(4)], his, los)

            values(0)
            values(1)
            pe.wait_ge(s_qk, 6)
            values(2)

            def rows(h):
                if h:
                    pe.wait_ge(s_th, h)
                    pe.wait_ge(s_e, EXPS * h - 1)
                for d in range(2):
                    q = (d * 4 + h) * P
                    mm(bank[2][:, d * SEQ:(d + 1) * SEQ], cst("sel")[0:36, q:q + P], mt[:], True)
                    ins = mm(bank[3][:, d * SEQ:(d + 1) * SEQ], cst("sel")[0:36, q:q + P], th[:], True)
                ins.then_inc(s_bc, 1)

            def scores(h):
                if h:
                    pe.wait_ge(s_p, 2 * h)
                for st in range(4):
                    ins = mm(bank[st // 2][:, (st % 2) * SEQ:(st % 2 + 1) * SEQ], K[:, h, st * P:(st + 1) * P],
                             Q[:, h], True)
                ins.then_inc(s_s, 1)

            def denominators(h):
                for d in range(2):
                    pe.wait_ge(s_p, 2 * h + d + 1)
                    if h and d == 0:
                        pe.wait_ge(s_ad, h)
                    for st in range(4):
                        ins = mm(bank[5][:, d * SEQ:(d + 1) * SEQ], ones, EF[h % 2][:, d, st], st == 0)
                ins.then_inc(s_den, 1)

            def numerators(h):
                pe.wait_ge(s_gw2, h + 1)
                if h >= 2:
                    pe.wait_ge(s_y, 2 * h - 2)
                for v in range(2):
                    for st in range(4):
                        ins = mm(head_bank(h)[:, v * SEQ:(v + 1) * SEQ], V[:, st, h * DV + v * P:h * DV + (v + 1) * P],
                                 EF[h % 2][:, 0, st], st == 0)
                ins.then_inc(s_num, 1)

            def output_gate(j):
                if j:
                    pe.wait_ge(s_os, j)
                pe_pair(pe, c + 9 + j, 4)

            def out_chunk(j):
                pe.wait_ge(s_lo, c + 14 + j)
                for g in range(2):
                    pe.wait_ge(s_h, U["lstm_y"] + 2 * j + g + 1)
                pe_down_chunk(pe, c + 13 + j, [hhi[:, 2 * j], hhi[:, 2 * j + 1]], [hlo[:, 2 * j], hlo[:, 2 * j + 1]],
                              j == 0, j == 3)

            pe.wait_ge(s_in[5], 16)
            pe.wait_ge(s_gd, 1)
            pe.wait_ge(s_vb, 4)
            rows(0)
            for st in range(4):
                ins = nc.tensor.transpose(bank[1][:, st * 36:(st + 1) * 36], ut[:, st * P:(st + 1) * P],
                                          ident[0:36, 0:36])
            ins.then_inc(s_uT, 1)
            values(3)
            pe.wait_ge(s_uc, 1)
            scores(0)
            pe.wait_ge(s_vb, 8)
            output_gate(0)
            rows(1)
            output_gate(1)
            denominators(0)
            scores(1)
            output_gate(2)
            denominators(1)
            scores(2)
            output_gate(3)
            pe.wait_ge(s_os, 4)
            for h in range(HEADS):
                if 1 <= h < HEADS - 1:
                    denominators(h + 1)
                if h == 1:
                    scores(3)
                if h >= 2:
                    out_chunk(h - 2)
                numerators(h)
                if h + 2 < HEADS:
                    rows(h + 2)
                pe_stat(pe, N_LSTM + h)
            out_chunk(2)
            out_chunk(3)

        def act_lstm(act):
            c = C_LSTM
            act.wait_ge(s_in[0], 16)
            nc.scalar.activation(scol[:], ccol[:], ACT.Silu).then_inc(s_scol, 1)
            act.wait_ge(s_scol, 1)
            act.wait_ge(s_eps, 1)
            for n in range(2):
                nc.scalar.activation(c4[:, :, 2 * n:2 * n + 1], scol[:, :, n:n + 1], ACT.Copy).then_inc(s_c4h, 1)
            act_split(act, 0)
            act_split(act, 1)
            act_split(act, 2)
            act_squares(act, N_X1, lambda j: X[:, j], lambda j: (s_in[3], 16))
            for j in range(3, 7):
                act_split(act, j)
            act_rstd(act, N_X1, D)
            act_split(act, 7)
            act_squares(act, N_CTX, lambda j: XC[:, j], lambda j: (s_in[2], 16), False)
            act_split(act, c)
            act.wait_ge(s_pe, 8)
            for g in range(2):
                nc.scalar.activation(mrow[:, g * 512:(g + 1) * 512], bank[g][0:4], ACT.Copy).then_inc(s_mrow, 1)
            act_rstd(act, N_CTX, D)
            act_modulate(act, mcol(0), "x1")
            act_split(act, c + 1)
            act_split(act, c + 2)
            act_modulate(act, lambda j: modc[:, j:j + 1], "ctx", chi)
            act_split(act, c + 3)
            act.wait_ge(s_in[4], 16)
            nc.scalar.activation(cb[:], cb[:], ACT.Silu).then_inc(s_cb, 1)
            act.preload_act_table_set(LN_EXP)

            def values_read(half):
                act.wait_ge(s_pe, c + 7 + 2 * half)
                for b in (1, 3):
                    nc.scalar.activation(V[:, b, half * 512:(half + 1) * 512], bank[b + 4 * half][:], ACT.Copy)\
                        .then_inc(s_vb, 1)

            for j in range(9):
                if j > 1:
                    act_split(act, c + j + 2)
                if j == 6:
                    values_read(0)
                if j == 4:
                    act.wait_ge(s_gr, 1)
                    alink(act, nc.scalar.activation(ga[:], gf[:], ACT.Abs))
                    alink(act, nc.scalar.activation(ga[:], ga[:], ACT.Exp, scale=-1.0))
                    nc.scalar.activation(ga[:], ga[:], ACT.Ln, bias=1.0).then_inc(s_ga, 1)
                if j == 6:
                    act.wait_ge(s_gr, 2)
                    nc.scalar.activation(gb[:], ga[:], ACT.Exp, scale=-1.0).then_inc(s_ga, 1)

            def decay(h):
                e = EF[h % 2]
                act.wait_ge(s_bc, h + 1)
                if h >= 2:
                    act.wait_ge(s_num, h - 1)
                nc.scalar.activation(flat(thb[:, h]), bank[3][:], ACT.Copy).then_inc(s_th, 1)
                act.wait_ge(s_arg, 4 * h + 4)
                for d in range(2):
                    for st in range(2):
                        nc.scalar.activation(e[:, d, st], bank[2][:, d * SEQ:(d + 1) * SEQ], ACT.Exp,
                                             bias=uc[:, st, 32 * d + h:32 * d + h + 1]).then_inc(s_e, 1)
                nc.scalar.activation(e[:, :, 2:4], e[:, :, 2:4], ACT.Exp).then_inc(s_e, 1)

            def gate_read(j):
                act_split(act, c + 9 + j + 2)
                act.wait_ge(s_pe, c + 9 + j + 1)
                nc.scalar.activation(flat(OS[:, 2 * j:2 * j + 2]), bank[4][:], ACT.Copy).then_inc(s_os, 1)

            def magnitudes(h):
                act.wait_ge(s_den, h + 1)
                if h:
                    act.wait_ge(s_gw2, h)
                nc.scalar.activation(flat(rd[:]), bank[5][:], ACT.Abs).then_inc(s_ad, 1)

            def round_head(h):
                for j in (2 * h, 2 * h + 1):
                    act.wait_ge(s_y, j + 1)
                    nc.scalar.activation(hhi[:, j], T[:, j % 2], ACT.Copy).then_inc(s_hhi, 1)

            act.wait_ge(s_uc, 1)
            decay(0)
            values_read(1)
            gate_read(0)
            decay(1)
            gate_read(1)
            magnitudes(0)
            gate_read(2)
            magnitudes(1)
            gate_read(3)
            act.wait_ge(s_os, 4)
            nc.scalar.activation(OS[:], OS[:], ACT.Sigmoid).then_inc(s_sg, 1)
            for h in range(HEADS):
                if 1 <= h < HEADS - 1:
                    magnitudes(h + 1)
                if h:
                    round_head(h - 1)
                    act_split(act, c + 14 + h)
                act_squares(act, N_LSTM + h, lambda j: head_bank(h)[:, j * SEQ:(j + 1) * SEQ],
                            lambda j: (s_num, h + 1), h == 0)
                if h + 2 < HEADS:
                    decay(h + 2)
                act_rstd(act, N_LSTM + h, DV)
            round_head(HEADS - 1)
            act_split(act, c + 18)

        def dve_lstm(dve):
            c = C_LSTM
            nc.vector.memset(eps[:], EPS)
            nc.vector.memset(c4[:].bitcast(f32), 0.0).then_inc(s_eps, 1)
            nc.vector.memset(gi[:], 0.0)
            nc.vector.memset(ut[:], 0.0)
            nc.vector.memset(mt[:], 0.0)
            nc.vector.memset(th[:], 0.0)
            dve.wait_ge(s_c4h, 2)
            nc.vector.tensor_tensor(c4[:, :, 1:4:2], scol[:], c4[:, :, 0:4:2].bitcast(f32), ALU.subtract)\
                .then_inc(s_c4, 1)
            for j in range(9):
                dve_split(dve, j)
            dve.wait_ge(s_mrow, 2)
            for g in range(2, 4):
                nc.vector.tensor_copy(mrow[:, g * 512:(g + 1) * 512], bank[g][0:4]).then_inc(s_mrow, 1)
            dve.wait_ge(s_in[1], 32)
            dve.wait_ge(s_mT, 1)
            nc.vector.tensor_reduce(CG[:, 0:2 * FIRST_MODS],
                                    bank[4][:, 0:4 * FIRST_MODS].rearrange("p (m t) -> p m t", t=2), AX.X, ALU.add)\
                .then_inc(s_mm0, 1)
            dve.wait_ge(s_mm0, 1)
            pm = CG[:, 0:2 * FIRST_MODS].rearrange("p (m t) -> p t m", t=2)
            nc.vector.tensor_tensor(modc[:], pm[:, 1], cols[:, 0:FIRST_MODS], ALU.add)
            link(dve, nc.vector.tensor_tensor(mod[:, 0:FIRST_MODS], pm[:, 0], cols[:, 0:FIRST_MODS], ALU.add))
            dve_coef_pre(dve, 1, 8, col("g_mix", 0, 8))
            dve_modulate(dve, N_X1, cq(1), mcol(0), "x1")
            dve_coef_pre(dve, 0, 8, col("g_mix", 0, 8), modc)
            dve_split(dve, c + 1)
            dve_split(dve, c + 2)
            dve_modulate(dve, N_CTX, cq(0), lambda j: modc[:, j:j + 1], "ctx", XC, chi, clo)
            nc.vector.memset(gf[:], 0.0)
            dve.wait_ge(s_cb, 1)
            two = lambda x: x.rearrange("p (a b) -> p a b", a=2)

            def mods(u, n):
                for k in range(n):
                    dve_mod_unit(dve, u + k)

            dve_split(dve, c + 3)
            for j in range(2):
                dve.wait_ge(s_pe, c + j + 1)
                nc.vector.tensor_copy(flat(Q[:, 2 * j:2 * j + 2]), bank[4 + j][:]).then_inc(s_qk, 1)
                mods(2 * j, 2)
            dve_split(dve, c + 4)
            dve.wait_ge(s_pe, c + 3)
            link(dve, nc.vector.tensor_scalar(g_all[:], bank[7][:], col("b_gate"), None, ALU.add))
            nc.vector.tensor_copy(gi[0:4], g_all[0:4])
            nc.vector.tensor_copy(two(gi[32:36]), two(g_all[32:36])[:, :, ::-1])
            nc.vector.tensor_copy(gf[0:4], g_all[64:68])
            nc.vector.tensor_copy(two(gf[32:36]), two(g_all[96:100])[:, :, ::-1]).then_inc(s_gr, 1)
            mods(4, 2)
            for j in range(2):
                dve_split(dve, c + 3 + j + 2)
                dve.wait_ge(s_pe, c + 3 + j + 1)
                for n in range(2):
                    a = 2 + 2 * j + n
                    nc.vector.tensor_scalar(K[:, 2 * j:2 * j + 2, (1 - n) * SEQ:(2 - n) * SEQ],
                                            bank[4 + a % 3][:].rearrange("p (m t) -> p m t", m=2),
                                            DK ** -0.5, None, ALU.mult).then_inc(s_qk, 1)
                mods(6 + 2 * j, 2)
            dve.wait_ge(s_ga, 1)
            link(dve, nc.vector.scalar_tensor_tensor(out=gf[:], in0=gf[:], scalar=0.0, in1=ga[:], op0=ALU.min,
                                                     op1=ALU.subtract))
            link(dve, nc.vector.tensor_tensor_scan(g_all[0:36], ones[0:36, 0:1].to_broadcast([36, 512]), gf[:], 0.0,
                                                   ALU.mult, ALU.add))
            link(dve, nc.vector.tensor_tensor(gi[:], gi[:], g_all[0:36], ALU.subtract))
            link(dve, nc.vector.tensor_tensor_scan(gf[:], gi[:], gi[:], 0.0, ALU.max, ALU.max))
            nc.vector.tensor_tensor(ga[:], gf[:], g_all[0:36], ALU.add).then_inc(s_gr, 1)
            nc.vector.tensor_copy(ut[0:4], gi[0:4])
            nc.vector.tensor_copy(two(ut[32:36]), two(gi[32:36])[:, :, ::-1])
            nc.vector.tensor_scalar(mt[0:4], gf[0:4, SEQ:], -1.0, None, ALU.mult)
            nc.vector.tensor_scalar(mt[32:36], gf[32:36, SEQ:][:, ::-1], -1.0, None, ALU.mult)
            mods(10, 2)
            dve_split(dve, c + 7)
            mods(12, 2)
            dve_split(dve, c + 8)
            dve.wait_ge(s_ga, 2)
            nc.vector.tensor_copy(th[0:4], gb[0:4, SEQ:])
            nc.vector.tensor_copy(th[32:36], gb[32:36, SEQ:][:, ::-1]).then_inc(s_gd, 1)
            mods(14, 2)

            def values_read(half):
                dve.wait_ge(s_pe, c + 7 + 2 * half)
                for b in (0, 2):
                    nc.vector.tensor_copy(V[:, b, half * 512:(half + 1) * 512], bank[b + 4 * half][:])\
                        .then_inc(s_vb, 1)

            values_read(0)
            mods(16, 2)
            dve_split(dve, c + 9)
            dve.wait_ge(s_uT, 1)
            nc.vector.tensor_copy(flat(uc[:]), bank[1][:, 0:144]).then_inc(s_uc, 1)
            mods(18, 2)
            dve_split(dve, c + 10)
            dve.wait_ge(s_uc, 1)
            madd = cst("madd").rearrange("p (d s t) -> p d s t", d=2, s=2)

            def exponents(h):
                e = EF[h % 2]
                dve.wait_ge(s_bc, h + 1)
                if h >= 2:
                    dve.wait_ge(s_num, h - 1)
                for d in range(2):
                    for st in range(2):
                        nc.vector.scalar_tensor_tensor(out=e[:, d, 2 + st], in0=bank[2][:, d * SEQ:(d + 1) * SEQ],
                                                       scalar=uc[:, 2 + st, 32 * d + h:32 * d + h + 1],
                                                       in1=madd[:, d, st], op0=ALU.add, op1=ALU.add)\
                            .then_inc(s_arg, 1)

            def weighted(h):
                dve.wait_ge(s_s, h + 1)
                dve.wait_ge(s_e, EXPS * (h + 1))
                for d in range(2):
                    for b in range(2):
                        e = flat(EF[h % 2][:, d, 2 * b:2 * b + 2])
                        ins = nc.vector.tensor_tensor(e, e, bank[b][:], ALU.mult)
                    ins.then_inc(s_p, 1)

            def normalise(h):
                e = EF[h % 2]
                dve.wait_ge(s_ad, h + 1)
                link(dve, nc.vector.tensor_tensor(flat(rd[:]), flat(rd[:]), flat(thb[:, h]), ALU.max))
                link(dve, nc.vector.reciprocal(flat(rd[:]), flat(rd[:])))
                for d in range(2):
                    ins = nc.vector.tensor_tensor(e[:, d], e[:, d], rd[:, d:d + 1].to_broadcast([P, 4, SEQ]),
                                                  ALU.mult)
                link(dve, ins)
                nc.vector.tensor_tensor(e[:, 0], e[:, 0], e[:, 1], ALU.add).then_inc(s_gw2, 1)

            def finish_head(h):
                dve.wait_ge(s_rstd, N_LSTM + h + 1)
                dve.wait_ge(s_sg, 1)
                dve.wait_ge(s_h, U["lstm_y"] + 2 * h)
                for v in range(2):
                    ins = nc.vector.scalar_tensor_tensor(out=T[:, v], in0=head_bank(h)[:, v * SEQ:(v + 1) * SEQ],
                                                         scalar=col("gain", 2 * h + v), in1=rs(N_LSTM + h),
                                                         op0=ALU.mult, op1=ALU.mult)
                link(dve, ins)
                for v in range(2):
                    nc.vector.tensor_tensor(T[:, v], T[:, v], OS[:, 2 * h + v], ALU.mult).then_inc(s_y, 1)
                for v in range(2):
                    j = 2 * h + v
                    dve.wait_ge(s_hhi, U["lstm_y"] + j + 1)
                    nc.vector.tensor_tensor(hlo[:, j], T[:, v], hhi[:, j].bitcast(f32), ALU.subtract)\
                        .then_inc(s_h, 1)

            dve.wait_ge(s_in[5], 16)
            exponents(0)
            mods(20, 2)
            values_read(1)
            dve_split(dve, c + 11)
            weighted(0)
            mods(22, 1)
            exponents(1)
            dve_split(dve, c + 12)
            weighted(1)
            for h in range(HEADS):
                normalise(h)
                if h == 0:
                    dve_split(dve, c + 13)
                    dve_split(dve, c + 14)
                    mods(23, 2)
                else:
                    finish_head(h - 1)
                    dve_split(dve, c + 14 + h)
                    if h < 3:
                        mods(23 + 2 * h, 2)
                if h + 2 < HEADS:
                    exponents(h + 2)
                    weighted(h + 2)
            mods(29, 1)
            finish_head(HEADS - 1)
            dve_split(dve, c + 18)
            mods(30, 2)
            dve_mod_bias(dve, FIRST_MODS, M_COND[0], 32)
            dve_add_plain(dve, 16, 0, c + 16)

        def x_ready(u):
            return lambda j: (s_x, u + j + 1)

        def ng(layer, sub, post):
            return col("norm_g", ((layer * 3 + sub) * 2 + post) * DT, DT)

        SWIGLU = {1: (0, 0, N_F1, "f1", "fin"), 2: (0, 2, N_F2, "f2", "gla"), 3: (1, 0, N_F3, "f3", "f2"),
                  4: (1, 2, N_F4, "f4", "mla")}

        OUTS = {"f1": 2, "gla": 3, "f2": 4, "f3": 5, "mla": 6, "f4": 7}

        def pe_swiglu(pe, f):
            _, _, n, name, _ = SWIGLU[f]
            pe_stat(pe, n)
            pe_ffn(pe, f, U[name])
            pe_stat(pe, n + 1)

        def act_swiglu(act, f):
            layer, sub, n, name, before = SWIGLU[f]
            act_squares(act, n, lambda j: X[:, j], x_ready(XU[before]))
            act_rstd(act, n, D)
            act_modulate(act, mcol(M_COND[layer] + 3 * sub * DT), name)
            if f == 3:
                nc.scalar.activation(XS[:], X[:], ACT.Copy).then_inc(s_xs, 1)
            act_ffn(act, f)
            act_squares(act, n + 1, down, lambda j: down_done(OUTS[name], j, C_FFN[f] + FFN_CHUNKS - 1))
            act_rstd(act, n + 1, D)

        def dve_swiglu(dve, f):
            layer, sub, n, name, _ = SWIGLU[f]
            m0 = M_COND[layer] + 3 * sub * DT
            dve_coef_pre(dve, 3, m0 + DT, ng(layer, sub, 0))
            dve_coef_post(dve, 4, m0 + 2 * DT, ng(layer, sub, 1), 0.5)
            dve_modulate(dve, n, cq(3), mcol(m0), name)
            dve_ffn(dve, f)
            if f < 4:
                dve_mod_bias(dve, 48 + 40 * f, 88 + 40 * f, 72 + 40 * f)
            if f == 3:
                dve.wait_ge(s_xs, 1)
            dve_add_post(dve, n + 1, 4, XU[name])

        s_xs = sem("layer0_output_kept")

        s_gb, s_z, s_zr = sem("gla_bank_read"), sem("gate_products"), sem("gate_products_read")
        s_gln, s_gsc, s_gex = sem("gla_gate_ln"), sem("gla_gate_scan"), sem("gla_gate_exp")
        s_qkd, s_gvb, s_r = sem("gla_qk_decayed"), sem("gla_v_bank_read"), sem("gla_r_bank_read")
        s_att, s_attr, s_kut = sem("gla_scores"), sem("gla_scores_read"), sem("gla_keys_transposed_read")
        s_upd, s_st, s_o = sem("gla_updates"), sem("gla_states"), sem("gla_head_output")

        def upd(n):
            return bank[2 + n % 2][:, (n // 2) * DV:(n // 2 + 1) * DV]

        def pe_gla(pe):
            c, n0 = C_GLA, N_GLA
            pe_stat(pe, n0)
            pe.wait_ge(s_lo, c + 1)
            for k in range(DT):
                pe.wait_ge(s_h, U["gla"] + k + 1)
                ins = mm3(bank[4][:, 0:SEQ], c, k, hhi[:, k], hlo[:, k], k == 0)
            ins.then_inc(s_pe, 1)
            for j, b in enumerate((5, 6, 4, 5)):
                if j >= 2:
                    pe.wait_ge(s_gb, j - 1)
                pe_pair(pe, c + 1 + j, b)
            pe.wait_ge(s_gb, 4)
            pe.wait_ge(s_gup, 16)
            for h in range(HEADS):
                ins = mm(bank[(6, 4)[h // 2]][:, (h % 2) * SEQ:(h % 2 + 1) * SEQ], wgu[:, h * DK:(h + 1) * DK], glow[:],
                         h % 2 == 0)
            ins.then_inc(s_z, 1)
            his = [lambda k, t=t: hhi[:, k, t * P:(t + 1) * P] for t in range(2)]
            los = [lambda k, t=t: hlo[:, k, t * P:(t + 1) * P] for t in range(2)]
            for j in range(4):
                b = 2 * (j // 2)
                pe_wide(pe, c + 5 + j, 4 * (j % 2), [bank[b][:], bank[b + 1][:]], his, los)
            for j, b in enumerate((5, 6, 4, 5)):
                if j == 0:
                    pe.wait_ge(s_gb, 5)
                elif j == 1:
                    pe.wait_ge(s_zr, 4)
                elif j == 3:
                    pe.wait_ge(s_r, 1)
                pe_pair(pe, c + 9 + j, b)
            pe.wait_ge(s_gvb, 4)
            for h in range(HEADS):
                pe.wait_ge(s_qkd, 2)
                if h:
                    pe.wait_ge(s_attr, h)
                    pe.wait_ge(s_kut, h)
                for t in range(2):
                    tt = slice(t * P, (t + 1) * P)
                    mm(bank[0][:, tt], GK[:, h, tt], GQ[:, h, tt], t == 0)
                for t in range(2):
                    tt = slice(t * P, (t + 1) * P)
                    ins = nc.tensor.transpose(bank[1][:, tt], GKU[:, h, tt], ident)
                ins.then_inc(s_att, 1)
                pe.wait_ge(s_kut, h + 1)
                if h:
                    pe.wait_ge(s_st, 3 * h)
                for n in range(3):
                    half = slice(64 * (n % 2), 64 * (n % 2) + 64)
                    ins = mm(upd(n), kut[half, n // 2], GV[half, n // 2, h * DV:(h + 1) * DV], n < 2)
                ins.then_inc(s_upd, 1)
                pe.wait_ge(s_attr, h + 1)
                pe.wait_ge(s_st, 3 * h + 3)
                if h:
                    pe.wait_ge(s_r, 4)
                    pe.wait_ge(s_y, 2 * HEADS + 2 * h)
                for v in range(2):
                    for t in range(2):
                        mm(bank[5][:, v * SEQ + t * P:v * SEQ + (t + 1) * P],
                           GV[:, t, h * DV + v * P:h * DV + (v + 1) * P], att[:, t], v == 0 and t == 0)
                    for n in range(1, 4):
                        ins = mm(bank[5][:, v * SEQ + n * CHUNK:v * SEQ + (n + 1) * CHUNK],
                                 ST[:, n - 1, v * P:(v + 1) * P], GQ[:, h, n * CHUNK:(n + 1) * CHUNK], False)
                ins.then_inc(s_o, 1)
                pe_stat(pe, N_GHEAD + h)
            for j in range(4):
                pe.wait_ge(s_lo, c + 14 + j)
                for g in range(2):
                    pe.wait_ge(s_h, U["gla_y"] + 2 * j + g + 1)
                pe_down_chunk(pe, c + 13 + j, [hhi[:, 2 * j], hhi[:, 2 * j + 1]], [hlo[:, 2 * j], hlo[:, 2 * j + 1]],
                              j == 0, j == 3)
            pe_stat(pe, N_GPOST)

        flat = lambda x: x.rearrange("p a b -> p (a b)")

        def act_gla(act):
            c = C_GLA
            act_squares(act, N_GLA, lambda j: X[:, j], x_ready(XU["f1"]))
            act.wait_ge(s_pe, c)
            act.dma_start(wgu[:], w_gup).then_inc(s_gup, 16)
            act_rstd(act, N_GLA, D)
            act_modulate(act, mcol(M_COND[0] + 3 * DT), "gla")
            for j in range(5):
                act_split(act, c + j + 2)
            act.preload_act_table_set(LN_EXP)
            act.wait_ge(s_z, 1)
            for h in range(HEADS):
                nc.scalar.activation(LA[:, h], bank[(6, 4)[h // 2]][:, (h % 2) * SEQ:(h % 2 + 1) * SEQ], ACT.Identity,
                                     bias=col("b_gla", h)).then_inc(s_zr, 1)
            act.wait_ge(s_zr, 4)
            alink(act, nc.scalar.activation(LB[:], LA[:], ACT.Abs))
            alink(act, nc.scalar.activation(LB[:], LB[:], ACT.Exp, scale=-1.0))
            nc.scalar.activation(LB[:], LB[:], ACT.Ln, bias=1.0).then_inc(s_gln, 1)
            for j in range(2):
                act_split(act, c + 5 + j + 2)
            act.wait_ge(s_gsc, 1)
            nc.scalar.activation(EB[:], LB[:], ACT.Exp, scale=1 / 16).then_inc(s_gex, 1)
            nc.scalar.activation(EN[:], LB[:], ACT.Exp, scale=-1 / 16).then_inc(s_gex, 1)
            act.wait_ge(s_gsc, 2)
            nc.scalar.activation(LA[:], LA[:], ACT.Exp, scale=1 / 16).then_inc(s_gex, 1)
            for j in range(2, 4):
                act_split(act, c + 5 + j + 2)
            for j in range(4):
                act_split(act, c + 9 + j + 2)
                act.wait_ge(s_pe, c + 9 + j + 1)
                nc.scalar.activation(flat(SR[:, 2 * j:2 * j + 2]), bank[(5, 6, 4, 5)[j]][:], ACT.Silu)\
                    .then_inc(s_r, 1)
            for h in range(HEADS):
                act.wait_ge(s_att, h + 1)
                if h:
                    act.wait_ge(s_upd, h)
                nc.scalar.activation(flat(kut[:]), bank[1][:, 0:SEQ], ACT.Copy).then_inc(s_kut, 1)
                act_squares(act, N_GHEAD + h, lambda j: bank[5][:, j * SEQ:(j + 1) * SEQ], lambda j: (s_o, h + 1))
                act_rstd(act, N_GHEAD + h, DV)
                for v in range(2):
                    j = 2 * h + v
                    act.wait_ge(s_y, 2 * HEADS + j + 1)
                    nc.scalar.activation(hhi[:, j], T[:, v], ACT.Copy).then_inc(s_hhi, 1)
            for j in range(4):
                act_split(act, c + 13 + j + 2)
            act_squares(act, N_GPOST, down, lambda j: down_done(OUTS["gla"], j, c + 16))
            act_rstd(act, N_GPOST, D)

        def dve_gla(dve):
            c, m0 = C_GLA, M_COND[0] + 3 * DT
            dve_coef_pre(dve, 3, m0 + DT, ng(0, 1, 0))
            dve_coef_post(dve, 4, m0 + 2 * DT, ng(0, 1, 1), 1.0)
            dve_modulate(dve, N_GLA, cq(3), mcol(m0), "gla")
            for j in range(5):
                dve_split(dve, c + j + 2)
                dve.wait_ge(s_pe, c + j + 1)
                if j == 0:
                    nc.vector.tensor_copy(glow[:], bank[4][0:16, 0:SEQ]).then_inc(s_gb, 1)
                elif j < 3:
                    nc.vector.tensor_scalar(flat(GQ[:, 2 * j - 2:2 * j]), bank[4 + j][:], DK ** -0.5, None,
                                            ALU.mult).then_inc(s_gb, 1)
                else:
                    nc.vector.tensor_copy(flat(GK[:, 2 * j - 6:2 * j - 4]), bank[1 + j][:]).then_inc(s_gb, 1)
            dve.wait_ge(s_gln, 1)
            link(dve, nc.vector.scalar_tensor_tensor(out=flat(LA[:]), in0=flat(LA[:]), scalar=0.0, in1=flat(LB[:]),
                                                     op0=ALU.min, op1=ALU.subtract))
            for h in range(HEADS):
                ins = nc.vector.tensor_tensor_scan(LB[:, h], cst("reset"), LA[:, h], 0.0, ALU.mult, ALU.add)
            ins.then_inc(s_gsc, 1)
            dve.wait_ge(s_gsc, 1)
            b4 = flat(LB[:]).rearrange("p (n c) -> p n c", c=CHUNK)
            nc.vector.tensor_tensor(flat(LA[:]).rearrange("p (n c) -> p n c", c=CHUNK),
                                    b4[:, :, CHUNK - 1:CHUNK].to_broadcast([P, 16, CHUNK]), b4, ALU.subtract)\
                .then_inc(s_gsc, 1)
            for j in range(2):
                dve_split(dve, c + 5 + j + 2)
            dve.wait_ge(s_gex, 3)
            nc.vector.tensor_tensor(flat(GQ[:]), flat(GQ[:]), flat(EB[:]), ALU.mult).then_inc(s_qkd, 1)
            link(dve, nc.vector.tensor_tensor(flat(GKU[:]), flat(GK[:]), flat(LA[:]), ALU.mult))
            nc.vector.tensor_tensor(flat(GK[:]), flat(GK[:]), flat(EN[:]), ALU.mult).then_inc(s_qkd, 1)
            for j in range(2, 4):
                dve_split(dve, c + 5 + j + 2)
                dve.wait_ge(s_pe, c + 5 + 2 * (j - 2) + 2)
                for t in range(2):
                    nc.vector.tensor_copy(GV[:, t, (j - 2) * 512:(j - 1) * 512], bank[2 * (j - 2) + t][:])\
                        .then_inc(s_gvb, 1)
            for j in range(4):
                dve_split(dve, c + 9 + j + 2)
            eb4 = flat(EB[:]).rearrange("p (n c) -> p n c", c=CHUNK)
            for h in range(HEADS):
                dve.wait_ge(s_att, h + 1)
                if h:
                    dve.wait_ge(s_o, h)
                link(dve, nc.vector.tensor_scalar(flat(att[:]), bank[0][:, 0:SEQ], 3e38, -3e38, ALU.min, ALU.max))
                nc.vector.tensor_tensor(flat(att[:]), flat(att[:]), cst("causal"), ALU.mult).then_inc(s_attr, 1)
                dve.wait_ge(s_upd, h + 1)
                nc.vector.tensor_copy(ST[:, 0], bank[2][:, 0:DV]).then_inc(s_st, 1)
                for n in range(1, 3):
                    dve.wait_ge(s_st, 3 * h + n)
                    nc.vector.scalar_tensor_tensor(out=ST[:, n], in0=ST[:, n - 1],
                                                   scalar=eb4[:, 4 * h + n, CHUNK - 1:CHUNK],
                                                   in1=upd(n),
                                                   op0=ALU.mult, op1=ALU.add).then_inc(s_st, 1)
                dve.wait_ge(s_rstd, N_GHEAD + h + 1)
                dve.wait_ge(s_h, U["gla_y"] + 2 * h)
                for v in range(2):
                    j = 2 * h + v
                    link(dve, nc.vector.scalar_tensor_tensor(out=T[:, v], in0=bank[5][:, v * SEQ:(v + 1) * SEQ],
                                                             scalar=col("g_out", v), in1=rs(N_GHEAD + h),
                                                             op0=ALU.mult, op1=ALU.mult))
                    nc.vector.tensor_tensor(T[:, v], T[:, v], SR[:, j], ALU.mult).then_inc(s_y, 1)
                for v in range(2):
                    j = 2 * h + v
                    dve.wait_ge(s_hhi, U["gla_y"] + j + 1)
                    nc.vector.tensor_tensor(hlo[:, j], T[:, v], hhi[:, j].bitcast(f32), ALU.subtract)\
                        .then_inc(s_h, 1)
            for j in range(4):
                dve_split(dve, c + 13 + j + 2)
            dve_add_post(dve, N_GPOST, 4, XU["gla"])

        s_lt, s_lhi, s_l = sem("latent_scaled"), sem("latent_rounded"), sem("latent_split")
        s_pos, s_ang, s_cs = sem("positions_loaded"), sem("angles"), sem("cos_sin")
        s_kr, s_kn, s_vm = sem("rotary_key"), sem("key_bank_read"), sem("value_bank_read")
        s_qn, s_qr, s_sc = sem("query_bank_read"), sem("rotary_query"), sem("mla_scores")
        s_scr, s_pexp, s_pn = sem("scores_masked"), sem("scores_exp"), sem("probabilities")
        s_pt, s_ptr, s_pv = sem("probabilities_transposed"), sem("transposes_read"), sem("mla_head")
        s_mxx = sem("scores_max")

        def act_latent(act, l0, n):
            for j in range(n):
                act.wait_ge(s_lt, l0 + j + 1)
                nc.scalar.activation(lhi[:, j], T[:, j], ACT.Copy).then_inc(s_lhi, 1)

        def dve_latent(dve, l0, n, norm, g, srcs):
            dve.wait_ge(s_rstd, norm + 1)
            for j in range(n):
                nc.vector.scalar_tensor_tensor(out=T[:, j], in0=srcs[j], scalar=col(g, j), in1=rs(norm),
                                               op0=ALU.mult, op1=ALU.mult).then_inc(s_lt, 1)
            for j in range(n):
                dve.wait_ge(s_lhi, l0 + j + 1)
                nc.vector.tensor_tensor(llo[:, j], T[:, j], lhi[:, j].bitcast(f32), ALU.subtract).then_inc(s_l, 1)

        def dve_rope(dve, first, second, x1, x2, s_done):
            for out, a, b, op in ((first, rd[:, 0], rd[:, 1], ALU.subtract), (second, rd[:, 1], rd[:, 0], ALU.add)):
                nc.vector.tensor_tensor(out, x1, a, ALU.mult)
                link(dve, nc.vector.tensor_tensor(CG[:], x2, b, ALU.mult))
                ins = nc.vector.tensor_tensor(out, out, CG[:], op)
                if out is first:
                    link(dve, ins)
            ins.then_inc(s_done, 1)
            return ins

        def pe_kv(pe):
            c = C_KV
            pe_stat(pe, N_KV)
            pe_pair(pe, c, 4, wait=U["kv"])
            pe_pair(pe, c + 1, 5)
            pe_stat(pe, N_KVL)
            pe.wait_ge(s_lo, c + 3)
            pe.wait_ge(s_l, 2)
            for m in range(MLA_HEADS):
                for k in range(2):
                    ins = mm3(down(m), c + 2, 2 * m + k, lhi[:, k], llo[:, k], m % 2 == 0 and k == 0)
            ins.then_inc(s_pe, 1)
            pe.wait_ge(s_lo, c + 4)
            sl = (c + 3) % 3
            for n, (t, half, b) in enumerate(((0, 0, 4), (0, 1, 5), (1, 0, 6), (1, 1, 0))):
                if b == 5:
                    pe.wait_ge(s_kr, 1)
                if b == 0:
                    pe.wait_ge(s_kn, 4)
                for k in range(2):
                    w = slice(k * D + half * 512, k * D + half * 512 + 512)
                    tt = slice(t * P, (t + 1) * P)
                    mm(bank[b][:], lhi[:, k, tt], whi[:, sl, w], k == 0)
                    mm(bank[b][:], lhi[:, k, tt], wlo[:, sl, w], False)
                    ins = mm(bank[b][:], llo[:, k, tt], whi[:, sl, w], False)
            ins.then_inc(s_pe, 1)

        def act_kv(act):
            c = C_KV
            act.wait_ge(s_x, XU["f3"])
            act.dma_start(CG[:].bitcast(i32), pos_d.partition_broadcast(P)).then_inc(s_pos, 16)
            act_squares(act, N_KV, lambda j: XS[:, j], lambda j: (s_xs, 1))
            act_rstd(act, N_KV, D)
            act_modulate(act, mcol(M_KV), "kv")
            for j in range(2):
                act_split(act, c + j + 2)
            act.wait_ge(s_ang, 1)
            nc.scalar.activation(rd[:], SG[:, 0:2], ACT.Sin).then_inc(s_cs, 1)
            act_squares(act, N_KVL, lambda j: bank[4][:, j * SEQ:(j + 1) * SEQ], lambda j: (s_pe, c + 1))
            act_rstd(act, N_KVL, 256)
            act_latent(act, 0, 2)
            for j in range(2, 4):
                act_split(act, c + j + 2)

        def dve_kv(dve):
            c = C_KV
            TURN = 2 * np.pi
            C1 = 6.28125
            C2 = float(np.float32(np.round((TURN - C1) * 2 ** 20) / 2 ** 20))
            C3 = TURN - C1 - C2
            dve.wait_ge(s_pos, 16)
            link(dve, nc.vector.tensor_copy(SG[:, 2], CG[:].bitcast(i32)))
            link(dve, nc.vector.tensor_scalar(SG[:, 2], SG[:, 2], col("invf"), None, ALU.mult))
            for n, add in ((0, 0.25), (1, 0.0)):
                link(dve, nc.vector.tensor_scalar(CG[:], SG[:, 2], 1 / TURN, add, ALU.mult, ALU.add))
                link(dve, nc.vector.tensor_scalar(CG[:], CG[:], 1.5 * 2 ** 23, None, ALU.add))
                link(dve, nc.vector.tensor_scalar(CG[:], CG[:], -1.5 * 2 ** 23, None, ALU.add))
                src = SG[:, 2]
                for part in (C1, C2, C3):
                    link(dve, nc.vector.scalar_tensor_tensor(out=SG[:, n], in0=CG[:], scalar=-part, in1=src,
                                                             op0=ALU.mult, op1=ALU.add))
                    src = SG[:, n]
                if n == 0:
                    link(dve, nc.vector.tensor_scalar(SG[:, 0], SG[:, 0], TURN / 4, None, ALU.add))
            pi = float(np.nextafter(np.float32(np.pi), np.float32(0)))
            nc.vector.tensor_scalar(flat(SG[:, 0:2]), flat(SG[:, 0:2]), pi, -pi, ALU.min, ALU.max).then_inc(s_ang, 1)
            dve_coef_pre(dve, 3, M_KV + DT, col("kv_g", 0, DT))
            dve_modulate(dve, N_KV, cq(3), mcol(M_KV), "kv", XS)
            for j in range(2):
                dve_split(dve, c + j + 2)
            dve.wait_ge(s_cs, 1)
            dve.wait_ge(s_pe, c + 2)
            dve_rope(dve, KR[:, 0], KR[:, 1], bank[5][:, 0:SEQ], bank[5][:, SEQ:], s_kr)
            dve_latent(dve, 0, 2, N_KVL, "g_kv", [bank[4][:, 0:SEQ], bank[4][:, SEQ:]])
            link(dve, nc.vector.memset(KRM[:], 0.0))
            dve_split(dve, c + 4)
            dve.wait_ge(s_pe, c + 3)
            for b in range(4):
                nc.vector.tensor_copy(flat(KN[:, 2 * b:2 * b + 2]), bank[b][:]).then_inc(s_kn, 1)
            dve_split(dve, c + 5)
            dve.wait_ge(s_kr, 1)
            for h in range(4):
                rows = slice(32 * h, 32 * h + 32)
                ins = nc.vector.tensor_copy(KRM[rows, h], KR[rows])
            ins.then_inc(s_kr, 1)
            dve.wait_ge(s_pe, c + 4)
            for t, half, b in ((0, 0, 4), (0, 1, 5), (1, 0, 6), (1, 1, 0)):
                nc.vector.tensor_copy(VM[:, t, half * 512:(half + 1) * 512], bank[b][:]).then_inc(s_vm, 1)

        def pe_mla(pe):
            c = C_MLA
            pe_stat(pe, N_MLA)
            pe.wait_ge(s_vm, 4)
            pe_pair(pe, c, 4, wait=U["mla"])
            pe.wait_ge(s_lo, c + 2)
            for k in range(DT):
                ins = mm3(bank[5][:, 0:SEQ], c + 1, k, hhi[:, k], hlo[:, k], k == 0)
            ins.then_inc(s_q2, 1)
            pe_stat(pe, N_QL)
            pe.wait_ge(s_l, 5)
            outs = [down(m) for m in range(8)] + [bank[6][:, 0:SEQ], bank[6][:, SEQ:], bank[4][:, 0:SEQ],
                                                  bank[4][:, SEQ:]]
            m = 0
            for j, (s0, count) in enumerate(((8, 2), (0, 5), (0, 5))):
                pe.wait_ge(s_lo, c + 2 + j)
                for n in range(count):
                    for k in range(3):
                        ins = mm3(outs[m], c + 1 + j, s0 + 3 * n + k, lhi[:, k], llo[:, k], m % 2 == 0 and k == 0)
                    m += 1
                ins.then_inc(s_pe, 1)
            scale_banks = (4, 5)

            def scores(h):
                b = bank[scale_banks[h % 2]]
                if h >= 2:
                    pe.wait_ge(s_scr, h - 1)
                for qb in range(2):
                    w = P * (qb + 1)
                    o = b[:, qb * P:qb * P + w]
                    qq = slice(qb * P, qb * P + P)
                    mm(o, QN[:, h, qq], KN[:, h, 0:w], qb == 0)
                    mm(o, QR[:, 0, h // 4, qq], KRM[:, h % 4, 0, 0:w], False)
                    ins = mm(o, QR[:, 1, h // 4, qq], KRM[:, h % 4, 1, 0:w], False)
                ins.then_inc(s_sc, 1)

            pe.wait_ge(s_qr, 2)
            pe.wait_ge(s_qn, 4)
            scores(0)
            for h in range(MLA_HEADS):
                if h + 1 < MLA_HEADS:
                    scores(h + 1)
                pe.wait_ge(s_pn, h + 1)
                if h:
                    pe.wait_ge(s_ptr, h)
                for n in range(3):
                    ins = nc.tensor.transpose(bank[6][:, n * P:(n + 1) * P], SC[:, h % 2, n * P:(n + 1) * P], ident)
                ins.then_inc(s_pt, 1)
                pe.wait_ge(s_ptr, h + 1)
                vh = lambda t: VM[:, t, h * P:(h + 1) * P]
                if h:
                    pe.wait_ge(s_h, U["mla_y"] + h)
                mm(down(h)[:, 0:P], vh(0), PT[:, h % 2, 0:P], h % 2 == 0)
                mm(down(h)[:, P:], vh(0), PT[:, h % 2, P:2 * P], False)
                mm(down(h)[:, P:], vh(1), PT[:, h % 2, 2 * P:], False).then_inc(s_pv, 1)
            pe.wait_ge(s_h, U["mla_y"] + MLA_HEADS)
            for j in range(4):
                pe.wait_ge(s_lo, c + 5 + j)
                pe_down_chunk(pe, c + 4 + j, [hhi[:, 2 * j], hhi[:, 2 * j + 1]], [hlo[:, 2 * j], hlo[:, 2 * j + 1]],
                              j == 0, j == 3)
            pe_stat(pe, N_MPOST)

        s_q2 = sem("query_latent_ready")

        def act_mla(act):
            c = C_MLA
            act_squares(act, N_MLA, lambda j: X[:, j])
            act_rstd(act, N_MLA, D)
            act_modulate(act, mcol(M_COND[1] + 3 * DT), "mla")
            act_split(act, c + 2)
            act_squares(act, N_QL, lambda j: (bank[4][:, 0:SEQ], bank[4][:, SEQ:], bank[5][:, 0:SEQ])[j],
                        lambda j: (s_q2, 1))
            act_rstd(act, N_QL, Q_LORA)
            act_latent(act, 2, 3)
            for j in range(1, 4):
                act_split(act, c + j + 2)
            for h in range(MLA_HEADS):
                act.wait_ge(s_mxx, h + 1)
                for qb in range(2):
                    s = SC[:, h % 2, qb * P:qb * P + P * (qb + 1)]
                    ins = nc.scalar.activation(s, s, ACT.Exp, bias=mx[:, h % 2, qb:qb + 1],
                                               accum_out=sm[:, h % 2, qb:qb + 1])
                ins.then_inc(s_pexp, 1)
                act.wait_ge(s_pt, h + 1)
                nc.scalar.activation(PT[:, h % 2], bank[6][:, 0:3 * P], ACT.Copy).then_inc(s_ptr, 1)
                act.wait_ge(s_pv, h + 1)
                nc.scalar.activation(hhi[:, h], down(h), ACT.Copy).then_inc(s_hhi, 1)
            for j in range(4, 8):
                act_split(act, c + j + 2)
            act_squares(act, N_MPOST, down, lambda j: down_done(OUTS["mla"], j, c + 7))
            act_rstd(act, N_MPOST, D)

        def dve_mla(dve):
            c, m0 = C_MLA, M_COND[1] + 3 * DT
            dve_coef_pre(dve, 3, m0 + DT, ng(1, 1, 0))
            dve_coef_post(dve, 4, m0 + 2 * DT, ng(1, 1, 1), 1.0)
            dve_modulate(dve, N_MLA, cq(3), mcol(m0), "mla")
            dve_split(dve, c + 2)
            dve_latent(dve, 2, 3, N_QL, "g_q", [bank[4][:, 0:SEQ], bank[4][:, SEQ:], bank[5][:, 0:SEQ]])
            for j in range(1, 4):
                dve_split(dve, c + j + 2)
            dve.wait_ge(s_pe, c + 4)
            for g in range(2):
                dve_rope(dve, QR[:, 0, g], QR[:, 1, g], bank[6][:, g * SEQ:(g + 1) * SEQ],
                         bank[4][:, g * SEQ:(g + 1) * SEQ], s_qr)
                dve.wait_ge(s_qr, g + 1)
            for b in range(4):
                nc.vector.tensor_copy(flat(QN[:, 2 * b:2 * b + 2]), bank[b][:]).then_inc(s_qn, 1)

            def softmax(h):
                dve.wait_ge(s_sc, h + 1)
                if h >= 2:
                    dve.wait_ge(s_pt, h - 1)
                s = SC[:, h % 2]
                nc.vector.scalar_tensor_tensor(out=s, in0=bank[(4, 5)[h % 2]][:, 0:3 * P], scalar=(P + ROPE) ** -0.5,
                                               in1=cst("amask"), op0=ALU.mult, op1=ALU.add).then_inc(s_scr, 1)
                dve.wait_ge(s_scr, h + 1)
                for qb in range(2):
                    ins = nc.vector.tensor_reduce(mx[:, h % 2, qb:qb + 1], SC[:, h % 2, qb * P:qb * P + P * (qb + 1)],
                                                  AX.X, ALU.max)
                link(dve, ins)
                nc.vector.tensor_scalar(mx[:, h % 2], mx[:, h % 2], -1.0, None, ALU.mult).then_inc(s_mxx, 1)

            softmax(0)
            for h in range(MLA_HEADS):
                if h + 1 < MLA_HEADS:
                    softmax(h + 1)
                dve.wait_ge(s_pexp, h + 1)
                link(dve, nc.vector.reciprocal(sm[:, h % 2], sm[:, h % 2]))
                for qb in range(2):
                    s = SC[:, h % 2, qb * P:qb * P + P * (qb + 1)]
                    ins = nc.vector.tensor_scalar(s, s, sm[:, h % 2, qb:qb + 1], None, ALU.mult)
                ins.then_inc(s_pn, 1)
                dve.wait_ge(s_hhi, U["mla_y"] + h + 1)
                nc.vector.tensor_tensor(hlo[:, h], down(h), hhi[:, h].bitcast(f32), ALU.subtract).then_inc(s_h, 1)
            for j in range(4, 8):
                dve_split(dve, c + j + 2)
            dve_add_post(dve, N_MPOST, 4, XU["mla"])

        def pe_rest(pe):
            for n, stage in enumerate((lambda: pe_swiglu(pe, 1), lambda: pe_gla(pe), lambda: pe_swiglu(pe, 2),
                                       lambda: pe_swiglu(pe, 3), lambda: (pe_kv(pe), pe_mla(pe)),
                                       lambda: pe_swiglu(pe, 4))):
                if stages >= 3 + n:
                    stage()

        def act_rest(act):
            for n, stage in enumerate((lambda: act_swiglu(act, 1), lambda: act_gla(act), lambda: act_swiglu(act, 2),
                                       lambda: act_swiglu(act, 3), lambda: (act_kv(act), act_mla(act)),
                                       lambda: act_swiglu(act, 4))):
                if stages >= 3 + n:
                    stage()

        def dve_rest(dve):
            for n, stage in enumerate((lambda: dve_swiglu(dve, 1), lambda: dve_gla(dve), lambda: dve_swiglu(dve, 2),
                                       lambda: dve_swiglu(dve, 3), lambda: (dve_kv(dve), dve_mla(dve)),
                                       lambda: dve_swiglu(dve, 4))):
                if stages >= 3 + n:
                    stage()

        @block.tensor
        def _(pe):
            pe_lstm(pe)
            if stages >= 2:
                pe_stat(pe, N_F0)
                pe_ffn(pe, 0, U["f0"])
                pe_stat(pe, N_FIN)
            pe_rest(pe)

        @block.scalar
        def _(act):
            act_lstm(act)
            if stages >= 2:
                act_squares(act, N_F0, lambda j: X[:, j], x_ready(XU["lstm"]))
                act_rstd(act, N_F0, D)
                act_modulate(act, mcol(24), "f0")
                act.wait_ge(s_c2, 16)
                nc.scalar.activation(cb[:], cb[:], ACT.Silu).then_inc(s_cb, 1)
                act_ffn(act, 0)
                act_squares(act, N_FIN, lambda j: X[:, j], x_ready(XU["f0"]))
                act_rstd(act, N_FIN, D)
            act_rest(act)

        @block.vector
        def _(dve):
            dve_lstm(dve)
            if stages >= 2:
                dve_coef_pre(dve, 2, 32, col("g_ffn", 0, 8))
                dve_modulate(dve, N_F0, cq(2), mcol(24), "f0")
                dve.wait_ge(s_cb, 2)
                dve_ffn(dve, 0)
                dve_mod_bias(dve, 48, 88, 72)
                dve_add_plain(dve, 40, 1, C_FFN[0] + FFN_CHUNKS - 1)
                dve.wait_ge(s_rstd, N_FIN + 1)
                for j in range(DT):
                    nc.vector.scalar_tensor_tensor(out=X[:, j], in0=X[:, j], scalar=col("g_final", j), in1=rs(N_FIN),
                                                   op0=ALU.mult, op1=ALU.mult).then_inc(s_x, 1)
            dve_rest(dve)


def _feature_cols(a):
    import numpy as np
    return np.asarray(a).reshape(-1, P).T


def _tiles(w):
    k, m = w.shape
    return w.reshape(k // P, P, m // P, P).transpose(1, 2, 0, 3)


def _by_output(w):
    return _tiles(w).reshape(P, -1, CW).transpose(1, 0, 2)


def _by_input(w):
    return _tiles(w).transpose(0, 2, 1, 3).reshape(P, -1, CW).transpose(1, 0, 2)


def _wide(w):
    k, m = w.shape
    return w.reshape(k // P, P, m // 512, 512).transpose(1, 2, 0, 3).reshape(P, -1, CW).transpose(1, 0, 2)


def _up_pairs(w):
    k = w.shape[0]
    t = _tiles(w).reshape(P, 2, FT, k // P, P)
    return t.transpose(0, 2, 1, 3, 4).reshape(P, FT, CW).transpose(1, 0, 2)


def _padded(a, width):
    import numpy as np
    out = np.zeros(a.shape[:-1] + (width,), a.dtype)
    out[..., :a.shape[-1]] = a
    return out


def _constants():
    import numpy as np
    con = np.zeros((P, N_CONST), np.float32)

    def put(name, a):
        at, w = CON[name]
        con[:a.shape[0], at:at + w] = a.reshape(a.shape[0], -1)

    put("ident", np.eye(P, dtype=np.float32))
    put("ones", np.ones((P, P), np.float32))
    sel = np.zeros((36, 8, P), np.float32)
    for d in range(2):
        for h in range(4):
            sel[32 * d + h, d * 4 + h] = 1
    put("sel", sel)
    s, t = np.arange(P)[:, None], np.arange(SEQ)[None, :]
    no = np.float32(-1e30)
    madd = np.zeros((P, 2, 2, SEQ), np.float32)
    for st in range(2):
        madd[:, 0, st] = np.where(s + P * st <= t, 0, no)
        madd[:, 1, st] = np.where(s + P * st >= t, 0, no)
    put("madd", madd)
    put("reset", np.broadcast_to((np.arange(SEQ) % CHUNK != 0).astype(np.float32), (P, SEQ)))
    i = np.arange(P)[None, :]
    causal = ((s <= i) & (s // CHUNK == i // CHUNK)).astype(np.float32)
    put("causal", np.concatenate([causal, causal], axis=1))
    put("amask", np.concatenate([np.where(i <= s, 0, no), np.zeros((P, P)), np.where(i <= s, 0, no)], axis=1))
    return con


def kernel(**inputs):
    import numpy as np
    import concourse.bacc as bacc
    from concourse.bass_utils import run_bass_kernel_spmd as run

    v = {k: np.asarray(a) for k, a in inputs.items()}
    w_in, w_gla = v["a_w_in"][0], v["gla_w_in_2"][0]
    gates = w_in[:, 3072:]
    wg = np.zeros((D, P), np.float32)
    b_gate = np.zeros((P, 1), np.float32)
    for n, row in enumerate((0, 32, 64, 96)):
        wg[:, row:row + HEADS] = gates[:, n * HEADS:(n + 1) * HEADS]
        b_gate[row:row + HEADS, 0] = v["a_b_gate"][0, n * HEADS:(n + 1) * HEADS]
    kv_a, kv_b = v["mla_w_kv_a_2"], v["mla_w_kv_b_2"].reshape(256, MLA_HEADS, 2, P)
    pe = [kv_a[:, 256 + 32 * n:288 + 32 * n] for n in range(2)]
    uq = v["mla_w_uq_2"][0].reshape(Q_LORA, MLA_HEADS, P + ROPE)
    uq = np.concatenate([uq[:, :, :P].reshape(Q_LORA, -1), uq[:, :, P:P + 32].reshape(Q_LORA, -1),
                         uq[:, :, P + 32:].reshape(Q_LORA, -1)], axis=1)
    uq = _tiles(uq).reshape(P, 12, 3 * P)
    dq = _tiles(v["mla_w_dq_2"][0]).reshape(P, 3, DT * P)
    gu, dn = v["ffn_w_gu_2"], v["ffn_w_down_2"]

    def ffn(up, down):
        return [_up_pairs(up), _by_input(down)]

    w_mod = v["w_mod"][0]
    stream = [w_mod[:, :FIRST_MODS * P].reshape(DT, P, CW), _by_output(w_in[:, :512]),
              _padded(_tiles(wg).reshape(P, -1), CW)[None], _by_output(w_in[:, 512:1024]),
              _wide(w_in[:, 1024:2048]), _by_output(w_in[:, 2048:3072]), _by_input(v["a_w_out"][0]),
              *ffn(v["f_w_up"][0], v["f_w_down"][0]), *ffn(gu[0, 0], dn[0, 0]),
              _padded(_tiles(_padded(w_gla[:, 2048:2064], P)).reshape(P, -1), CW)[None],
              _by_output(w_gla[:, :1024]), _wide(w_gla[:, 1024:2048]), _by_output(w_gla[:, 2064:]),
              _by_input(v["gla_w_out_2"][0]), *ffn(gu[0, 1], dn[0, 1]), *ffn(gu[1, 0], dn[1, 0]),
              _by_output(np.concatenate([kv_a[:, :256]] + [pe[0]] * 4 + [pe[1]] * 4, axis=1)),
              _by_output(kv_b[:, :, 0].reshape(256, -1)),
              kv_b[:, :, 1].reshape(2, P, D).transpose(1, 0, 2).reshape(1, P, CW),
              dq[:, :2].reshape(1, P, CW),
              _padded(np.concatenate([dq[:, 2], uq[:, :2].reshape(P, -1)], axis=1), CW)[None],
              _padded(uq[:, 2:7].reshape(P, -1), CW)[None], _padded(uq[:, 7:].reshape(P, -1), CW)[None],
              _by_input(v["mla_w_out_2"][0]), *ffn(gu[1, 1], dn[1, 1])]
    w_stream = np.ascontiguousarray(np.concatenate(stream, axis=0))
    assert w_stream.shape == (N_CHUNKS, P, CW)
    rows = np.concatenate([w_mod[:, FIRST_MODS * P:].T, v["cond_w_2"][0].T, v["kv_cond_w_2"].T, v["cond_w_2"][1].T])
    invf = (10000.0 ** (-np.arange(0, ROPE, 2, dtype=np.float32) / np.float32(ROPE))).astype(np.float32)
    cw = v["f_w_conv"][0]
    cols = np.concatenate([_feature_cols(a) for a in (
        v["b_mod"][0], v["cond_b_2"][0], v["kv_cond_b_2"], v["cond_b_2"][1], v["g_mix"][0], v["g_ffn"][0],
        v["g_final"], v["a_head_gain"][0], cw[0], cw[1], cw[2], v["f_b_conv"][0], v["norm_g_2"].reshape(-1),
        v["kv_g_in_2"], v["gla_g_out_2"][0], v["gla_b_gate_2"][0], v["mla_g_kv_2"], v["mla_g_q_2"][0], b_gate,
        np.tile(invf, 4))], axis=1)

    def features(x):
        return x.reshape(SEQ, DT, P).transpose(2, 1, 0)

    data = {
        "w_stream": w_stream, "m_stream": rows.reshape(-1, P, D), "w_gup": v["gla_w_gate_up_2"][0],
        "xT": features(v["x"]), "ctxT": features(v["ctx"]),
        "c_cols": np.stack([_feature_cols(v["c"]), _feature_cols(v["c_ctx"])], axis=2),
        "c_row": v["c"].reshape(D), "c2_row": v["c_2"].reshape(D), "cols_d": cols, "const_d": _constants(),
        "pos_d": v["positions_2"].reshape(SEQ),
    }
    nc = bacc.Bacc("TRN2", target_bir_lowering=False, num_devices=1)
    dt, arrays, args = mybir.dt, {}, {}
    for name, a in data.items():
        a = np.ascontiguousarray(a)
        arrays[name] = a
        args[name] = nc.dram_tensor(name, a.shape, dt.int32 if a.dtype.kind == "i" else dt.float32,
                                    kind="ExternalInput").ap()
    out = nc.dram_tensor("y", (P, DT, SEQ), dt.float32, kind="ExternalOutput").ap()
    build(nc, **args, out_d=out)
    y = run(nc, [arrays], core_ids=[0]).results[0]["y"]
    return np.ascontiguousarray(np.asarray(y).transpose(2, 1, 0)).reshape(1, SEQ, D)
```

```python
import concourse.bass as bass
from concourse import mybir
from contextlib import ExitStack
import numpy as np

D, SEQ, FF = 1024, 256, 2816
P = 128
DT = D // P
FT = FF // P
HEADS, DK, DV, CHUNK = 4, 128, 256, 64
MLA_HEADS, ROPE, Q_LORA = 8, 64, 384
EPS = 1e-6
TILES = 16
CW = TILES * P

FFN_CHUNKS = FT + FT // 2
C_LSTM = DT
C_FFN = [25, 58, 108, 141, 186]
C_GLA = 91
C_KV = 174
C_MLA = 178
N_CHUNKS = C_FFN[-1] + FFN_CHUNKS
M_COND = [48, 136]
M_KV = 120
N_MOD = 208
FIRST_MODS = 16
N_UNITS = N_MOD - FIRST_MODS
_names = [("g_mix", 8), ("g_ffn", 8), ("g_final", 8), ("gain", 8), ("cw0", FT), ("cw1", FT), ("cw2", FT),
          ("cb", FT), ("norm_g", 96), ("kv_g", 8), ("g_out", 2), ("b_gla", 4), ("g_kv", 2), ("g_q", 3),
          ("b_gate", 1), ("invf", 1)]
COL, _at = {}, N_MOD
for _n, _w in _names:
    COL[_n] = (_at, _w)
    _at += _w
N_COLS = _at
_names = [("ident", P), ("ones", P), ("sel", 8 * P), ("madd", 4 * SEQ), ("reset", SEQ),
          ("causal", SEQ), ("amask", 3 * P)]
CON, _at = {}, 0
for _n, _w in _names:
    CON[_n] = (_at, _w)
    _at += _w
N_CONST = _at


def build(nc, w_stream, m_stream, w_gup, xT, ctxT, c_cols, c_row, c2_row, cols_d, const_d,
          pos_d, out_d):
    f32, f32r, i32 = mybir.dt.float32, mybir.dt.float32r, mybir.dt.int32
    ALU, ACT, AX = mybir.AluOpType, mybir.ActivationFunctionType, mybir.AxisListType
    LN_EXP = "natural_log_exp_and_others"

    ctx = ExitStack()
    with ctx:
        def sb(name, shape, dt=f32):
            return ctx.enter_context(nc.sbuf_tensor(name, shape, dt))

        sems = {}

        def sem(name):
            if name not in sems:
                sems[name] = ctx.enter_context(nc.semaphore(name))
            return sems[name]

        raw = sb("raw", [P, 3, CW])
        whi = sb("whi", [P, 3, CW], f32r)
        wlo = sb("wlo", [P, 3, CW], f32r)
        mring = sb("mring", [P, 2, D])
        X = sb("X", [P, DT, SEQ])
        hhi = sb("hhi", [P, DT, SEQ], f32r)
        hlo = sb("hlo", [P, DT, SEQ], f32r)
        cb = sb("cb", [P, D])
        cols = sb("cols", [P, N_COLS])
        con = sb("con", [P, N_CONST])
        mod = sb("mod", [P, N_MOD])
        modc = sb("modc", [P, FIRST_MODS])
        ccol = sb("ccol", [P, DT, 2])
        scol = sb("scol", [P, DT, 2])
        coef = sb("coef", [P, 16, DT])
        eps = sb("eps", [P, 1])
        lnt = sb("lnt", [P, SEQ])
        rstd = sb("rstd", [P, 2, SEQ])
        T = sb("T", [P, 3, SEQ])
        SG = sb("SG", [P, 3, SEQ])
        CG = sb("CG", [P, SEQ])
        rd = sb("rd", [P, 2, SEQ])
        uc = sb("uc", [P, 4, 36])
        arena = sb("arena", [P, 68 * 256])
        base = nc.sbuf_base - 68 * 1024

        def at(name, kb, shape, dt=f32):
            return nc.alloc_sbuf_tensor_at(name, shape, dt, offset=base + int(kb * 1024))

        c4 = at("c4", 0, [P, DT, P], f32r)
        mrow = at("mrow", 4, [4, FIRST_MODS * P])
        hid_hi = at("hid_hi", 8, [P, FT, SEQ], f32r)
        hid_lo = at("hid_lo", 8 + FT, [P, FT, SEQ], f32r)
        XC = at("XC", 44, [P, DT, SEQ])
        thb = at("thb", 0, [P, HEADS, 2, SEQ])
        chi = at("chi", 8, [P, DT, SEQ], f32r)
        OS = at("OS", 8, [P, DT, SEQ])
        clo = at("clo", 16, [P, DT, SEQ], f32r)
        EF = [at("EF0", 54, [P, 2, 4, SEQ]), at("EF1", 16, [P, 2, 4, SEQ])]
        Q = at("Q", 24, [P, HEADS, SEQ])
        K = at("K", 28, [P, HEADS, 2 * SEQ])
        V = at("V", 36, [P, 4, D])
        GQ = at("GQ", 0, [P, HEADS, SEQ])
        GK = at("GK", 4, [P, HEADS, SEQ])
        LA = at("LA", 8, [P, HEADS, SEQ])
        LB = at("LB", 12, [P, HEADS, SEQ])
        EB = at("EB", 16, [P, HEADS, SEQ])
        EN = at("EN", 20, [P, HEADS, SEQ])
        GV = at("GV", 24, [P, 2, D])
        SR = at("SR", 32, [P, DT, SEQ])
        GKU = at("GKU", 40, [P, HEADS, SEQ])
        wgu = at("wgu", 44, [16, HEADS * DK])
        glow = at("glow", 46, [16, SEQ])
        ST = [at("ST0", 47, [P, 3, DV]), at("ST1", 60, [P, 3, DV])]
        att = [at("att0", 50, [P, 2, P]), at("att1", 63, [P, 2, P])]
        kut = [at("kut0", 51, [P, 2, P]), rd[:, 0].rearrange("p (a b) -> p a b", a=2)]
        KN = at("KN", 0, [P, MLA_HEADS, SEQ])
        VM = at("VM", 8, [P, 2, D])
        KR = at("KR", 16, [P, 2, SEQ])
        QN = at("QN", 18, [P, MLA_HEADS, SEQ])
        QR = at("QR", 26, [P, 2, 2, SEQ])
        KRM = at("KRM", 30, [P, 4, 2, SEQ])
        lhi = at("lhi", 38, [P, 3, SEQ], f32r)
        llo = at("llo", 41, [P, 3, SEQ], f32r)
        SC = at("SC", 44, [P, 2, 3 * P])
        PT = at("PT", 47, [P, 2, 3 * P])
        cb2 = at("cb2", 64, [P, D])
        SQ = at("SQ", 52, [P, DT, SEQ])
        gf = at("gf", 54, [36, 512])
        ga = at("ga", 56, [36, 512])
        gb = at("gb", 58, [36, 512])
        g_all = at("g_all", 60, [P, 512])
        gi = at("gi", 62, [36, 512])
        ut = at("ut", 64, [36, 512])
        mt = at("mt", 66, [36, SEQ])
        th = at("th", 67, [36, SEQ])
        mx = sb("mx", [P, 2, 2])
        sm = sb("sm", [P, 2, 2])

        bank = [ctx.enter_context(nc.psum_tensor(f"bank{b}", [P, 512], f32)) for b in range(8)]
        block = ctx.enter_context(nc.Block())

        def col(name, j=0, n=None):
            a, w = COL[name]
            return cols[:, a + j:a + j + (n or 1)]

        def cst(name):
            a, w = CON[name]
            return con[:, a:a + w]

        ident, ones = cst("ident"), cst("ones")

        s_raw = [sem(f"raw_loaded{j}") for j in range(3)]
        s_hi, s_lo, s_pe = sem("chunk_rounded"), sem("chunk_rest"), sem("chunk_used")
        s_mod = [sem(f"mod_loaded{j}") for j in range(2)]
        s_mused = sem("mod_used")

        def run(i, per):
            return 0 if i is None else i * per

        def act_split(act, c, i=None):
            if c >= N_CHUNKS:
                return
            act.wait_ge(s_raw[c % 3], 16 * (c // 3 + 1) + run(i, 16))
            if c >= 3:
                act.wait_ge(s_pe, c - 2 + run(i, 3))
            nc.scalar.activation(whi[:, c % 3], raw[:, c % 3], ACT.Copy).then_inc(s_hi, 1)

        def dve_split(dve, c, i=None):
            if c >= N_CHUNKS:
                return
            dve.wait_ge(s_hi, c + 1 + run(i, 3))
            nc.vector.tensor_tensor(wlo[:, c % 3], raw[:, c % 3], whi[:, c % 3].bitcast(f32),
                                    ALU.subtract).then_inc(s_lo, 1)

        def mm3(out, c, s, rhi, rlo, start):
            wh, wl = whi[:, c % 3, s * P:(s + 1) * P], wlo[:, c % 3, s * P:(s + 1) * P]
            nc.tensor.matmul(out, wh, rhi, start=start, stop=True, skip_group_check=True)
            nc.tensor.matmul(out, wh, rlo, start=False, stop=True, skip_group_check=True)
            return nc.tensor.matmul(out, wl, rhi, start=False, stop=True, skip_group_check=True)

        def mm(out, lhsT, rhs, start):
            return nc.tensor.matmul(out, lhsT, rhs, start=start, stop=True, skip_group_check=True)

        s_h = sem("input_tile_split")
        s_hhi = sem("input_tile_rounded")

        def pe_pair(pe, c, bk, hi=hhi, lo=hlo, last=True, wait=None, between=None):
            pe.wait_ge(s_lo, c + 1)
            for m in range(2):
                if m and between:
                    between()
                for k in range(DT):
                    if m == 0 and wait is not None:
                        pe.wait_ge(s_h, wait + k + 1)
                    ins = mm3(bank[bk][:, m * SEQ:(m + 1) * SEQ], c, m * DT + k, hi[:, k], lo[:, k], k == 0)
            if last:
                ins.then_inc(s_pe, 1)

        def pe_first_chunks(pe, u0, parts):
            for k in range(DT):
                pe.wait_ge(s_h, u0 + k + 1)
                for c, b, tiles in parts:
                    for m in range(tiles):
                        ins = mm3(b[:, m * SEQ:(m + 1) * SEQ], c, m * DT + k, hhi[:, k], hlo[:, k],
                                  k == 0 and m == 0)
                    if k == DT - 1:
                        ins.then_inc(s_pe, 1)

        def pe_wide(pe, c, k0, outs, his, los):
            pe.wait_ge(s_lo, c + 1)
            for n, o in enumerate(outs):
                for g in range(4):
                    k = k0 + g
                    wh, wl = whi[:, c % 3, g * 512:(g + 1) * 512], wlo[:, c % 3, g * 512:(g + 1) * 512]
                    mm(o, his[n](k), wh, k == 0)
                    mm(o, his[n](k), wl, False)
                    ins = mm(o, los[n](k), wh, False)
            ins.then_inc(s_pe, 1)

        s_down = sem("output_bank_ready")

        def pe_down_chunk(pe, c, khi, klo, first, last=False):
            order = [(g, m + n) for m in range(0, DT, 2) for g in range(2) for n in range(2)] if last else \
                [(g, m) for g in range(2) for m in range(DT)]
            for g, m in order:
                ins = mm3(down(m), c, g * DT + m, khi[g], klo[g], first and g == 0 and m % 2 == 0)
                if last and g and m % 2 and m < DT - 1:
                    ins.then_inc(s_down, 1)
            ins.then_inc(s_pe, 1)

        def down(m):
            return bank[m // 2][:, (m % 2) * SEQ:(m % 2 + 1) * SEQ]

        s_sq, s_stat, s_rstd, s_ln = sem("squares"), sem("mean_square"), sem("rstd"), sem("log_mean_square")
        NORMS = ([8, 8] + [2] * 4 + [8, 8] + [8, 8] + [8] + [2] * 4 + [8] + [8, 8]
                 + [8, 8, 8] + [2, 8] + [3, 8] + [8, 8])
        N_X1, N_CTX, N_LSTM, N_F0, N_FIN, N_F1, N_GLA, N_GHEAD, N_GPOST, N_F2 = 0, 1, 2, 6, 7, 8, 10, 11, 15, 16
        N_F3, N_KV, N_F3P, N_KVL, N_MLA, N_QL, N_MPOST, N_F4 = 18, 19, 20, 21, 22, 23, 24, 25

        def act_squares(act, n, src, wait=None, table=True):
            if table:
                act.preload_act_table_set(LN_EXP)
            for j in range(NORMS[n]):
                if wait is not None:
                    act.wait_ge(*wait(j))
                if n and j == 0:
                    act.wait_ge(s_stat, n)
                nc.scalar.activation(SQ[:, j], src(j), ACT.Square).then_inc(s_sq, 1)

        def pe_stat(pe, n):
            before = sum(NORMS[:n])
            if n:
                pe.wait_ge(s_ln, n)
            for j in range(NORMS[n]):
                pe.wait_ge(s_sq, before + j + 1)
                ins = mm(bank[7][:, (n % 2) * SEQ:(n % 2 + 1) * SEQ], ones, SQ[:, j], j == 0)
            ins.then_inc(s_stat, 1)

        def act_rstd(act, n, dim):
            act.wait_ge(s_stat, n + 1)
            if n:
                act.wait_ge(s_rstd, n)
            nc.scalar.activation(lnt[:], bank[7][:, (n % 2) * SEQ:(n % 2 + 1) * SEQ], ACT.Ln, bias=eps[:, 0:1],
                                 scale=1.0 / dim).then_inc(s_ln, 1)
            act.wait_ge(s_ln, n + 1)
            nc.scalar.activation(rstd[:, n % 2], lnt[:], ACT.Exp, scale=-0.5).then_inc(s_rstd, 1)

        def rs(n):
            return rstd[:, n % 2]

        s_vstep = sem("vector_step")
        vsteps = [0]

        def link(dve, ins):
            vsteps[0] += 1
            ins.then_inc(s_vstep, 1)
            dve.wait_ge(s_vstep, vsteps[0])

        s_astep = sem("scalar_step")
        asteps = [0]

        def alink(act, ins):
            asteps[0] += 1
            ins.then_inc(s_astep, 1)
            act.wait_ge(s_astep, asteps[0])

        s_t = sem("input_tile_scaled")

        MODULATED = ["x1", "ctx", "f0", "f1", "gla", "f2", "f3", "kv", "mla", "f4"]

        def dve_modulate(dve, n, A, sh, stage, src=None, hi=hhi, lo=hlo):
            u0 = U[stage]
            dve.wait_ge(s_rstd, n + 1)
            for j in range(DT + 1):
                if j < DT:
                    if u0 or j >= 3:
                        dve.wait_ge(s_h, u0 + max(j - 2, 0))
                    nc.vector.scalar_tensor_tensor(out=T[:, j % 3], in0=(src or X)[:, j], scalar=A(j), in1=rs(n),
                                                   op0=ALU.mult, op1=ALU.mult).then_inc(s_t, 1)
                if j:
                    k = j - 1
                    dve.wait_ge(s_hhi, u0 + k + 1)
                    nc.vector.scalar_tensor_tensor(out=lo[:, k], in0=T[:, k % 3], scalar=sh(k),
                                                   in1=hi[:, k].bitcast(f32), op0=ALU.add,
                                                   op1=ALU.subtract).then_inc(s_h, 1)

        def act_modulate(act, sh, stage, hi=hhi):
            t0 = 8 * MODULATED.index(stage)
            for j in range(DT):
                act.wait_ge(s_t, t0 + j + 1)
                nc.scalar.activation(hi[:, j], T[:, j % 3], ACT.Identity, bias=sh(j)).then_inc(s_hhi, 1)

        U = {n: 8 * i for i, n in enumerate(
            ["x1", "ctx", "lstm_y", "f0", "f1", "gla", "gla_y", "f2", "f3", "kv", "mla", "mla_y", "f4"])}

        COND_UNITS = M_COND[0] - FIRST_MODS

        def dve_mod_unit(dve, u, i=None, per=0):
            dve.wait_ge(s_mod[u % 2], 16 * (u // 2 + 1) + run(i, 8 * per))
            a = FIRST_MODS + u
            dst = mod[:, a:a + 1] if i is None else mod[:, bass.ds(i * per + a, 1)]
            nc.vector.scalar_tensor_tensor(out=mring[:, u % 2], in0=mring[:, u % 2], scalar=1.0,
                                           in1=(cb if u < COND_UNITS else cb2)[:],
                                           op0=ALU.mult, op1=ALU.mult, accum_out=dst).then_inc(s_mused, 1)

        def dve_mod_bias(dve, a, b, units):
            dve.wait_ge(s_mused, units)
            link(dve, nc.vector.tensor_tensor(mod[:, a:b], mod[:, a:b], cols[:, a:b], ALU.add))

        def dve_coef_pre(dve, q, scale_at, g, src=None):
            src = mod if src is None else src
            link(dve, nc.vector.scalar_tensor_tensor(out=coef[:, q], in0=src[:, scale_at:scale_at + DT], scalar=1.0,
                                                     in1=g, op0=ALU.add, op1=ALU.mult))

        def dve_coef_post(dve, q, gate_at, g, w):
            link(dve, nc.vector.scalar_tensor_tensor(out=coef[:, q], in0=mod[:, gate_at:gate_at + DT], scalar=w,
                                                     in1=g, op0=ALU.mult, op1=ALU.mult))

        def mcol(a):
            return lambda j: mod[:, a + j:a + j + 1]

        def cq(q):
            return lambda j: coef[:, q, j:j + 1]

        s_x = sem("x_tile_updated")
        XU = {n: 8 * i for i, n in enumerate(["lstm", "f0", "fin", "f1", "gla", "f2", "f3", "mla", "f4"])}

        def down_done(d, m, c):
            return (s_pe, c + 1) if m >= DT - 2 else (s_down, 3 * d + m // 2 + 1)

        def dve_add_plain(dve, gate_at, d, c):
            for m in range(DT):
                if m % 2 == 0:
                    dve.wait_ge(*down_done(d, m, c))
                nc.vector.scalar_tensor_tensor(out=X[:, m], in0=down(m), scalar=mod[:, gate_at + m:gate_at + m + 1],
                                               in1=X[:, m], op0=ALU.mult, op1=ALU.add).then_inc(s_x, 1)

        s_tp = sem("post_tile_scaled")
        tposts = [0]

        def dve_add_post(dve, n, q, x0):
            dve.wait_ge(s_rstd, n + 1)
            for m in range(DT + 1):
                if m < DT:
                    if m >= 3:
                        dve.wait_ge(s_x, x0 + m - 2)
                    nc.vector.scalar_tensor_tensor(out=T[:, m % 3], in0=down(m), scalar=coef[:, q, m:m + 1],
                                                   in1=rs(n), op0=ALU.mult, op1=ALU.mult).then_inc(s_tp, 1)
                if m:
                    tposts[0] += 1
                    dve.wait_ge(s_tp, tposts[0])
                    nc.vector.tensor_tensor(X[:, m - 1], X[:, m - 1], T[:, (m - 1) % 3], ALU.add).then_inc(s_x, 1)

        s_silu, s_prod = sem("hidden_silu"), sem("hidden_product")
        s_hidhi, s_hid, s_conv, s_cstep = sem("hidden_rounded"), sem("hidden_split"), sem("gate_conv"), sem("conv_step")
        DOWN_TURNS = 2

        UNITS, GLA_UNITS = [28, 58, 112, 152, 192], 98

        def after_units(dve, a, b):
            dve_mod_bias(dve, FIRST_MODS + a, FIRST_MODS + b, b)

        def hid(t, i, buf):
            return buf[:, t] if i is None else buf[:, bass.ds(i * 3 + t, 1), :].rearrange("p a b -> p (a b)")

        def up_parts(body, eng, f):
            peeled = 1 if f else 4
            for t in range(peeled):
                body(t, None)
            with eng.Fori(0, (FT - peeled) // 3) as i:
                for t in range(peeled, peeled + 3):
                    body(t, i)

        def down_parts(body, eng, after=()):
            after = dict(after)
            for d in range(2):
                body(d, None)
                if d in after:
                    after[d]()
            with eng.Fori(0, DOWN_TURNS) as i:
                for d in range(2, 5):
                    body(d, i)
            for d in range(2 + 3 * DOWN_TURNS, FT // 2):
                if d - 1 in after:
                    after[d - 1]()
                body(d, None)

        def pe_ffn(pe, f, u0, after=()):
            c0 = C_FFN[f]
            pe.wait_ge(s_lo, c0 + 2)
            if f:
                pe.wait_ge(s_prod, FT * f)
            pe_first_chunks(pe, u0, [(c0, bank[4], 2), (c0 + 1, bank[5], 2)])

            def up(t, i):
                pe.wait_ge(s_lo, c0 + t + 1 + run(i, 3))
                if f or t >= 3:
                    pe.wait_ge(s_prod, FT * f + t - 2 + run(i, 3))
                b = bank[4 + t % 3]
                for m in range(2):
                    for k in range(DT):
                        ins = mm3(b[:, m * SEQ:(m + 1) * SEQ], c0 + t, m * DT + k, hhi[:, k], hlo[:, k], k == 0)
                ins.then_inc(s_pe, 1)

            first = 2 if f else 5
            for t in range(2, first):
                up(t, None)
            with pe.Fori(0, (FT - 2 - first) // 3) as i:
                for t in range(first, first + 3):
                    up(t, i)
            for t in range(FT - 2, FT):
                up(t, None)

            def dn(d, i):
                c = c0 + FT + d
                pe.wait_ge(s_lo, c + 1 + run(i, 3))
                pe.wait_ge(s_hid, FT * f + 2 * d + 2 + run(i, 6))
                hi = [hid_hi[:, 2 * d + g] if i is None else
                      hid_hi[:, bass.ds(i * 6 + 2 * d + g, 1), :].rearrange("p a b -> p (a b)") for g in range(2)]
                lo = [hid_lo[:, 2 * d + g] if i is None else
                      hid_lo[:, bass.ds(i * 6 + 2 * d + g, 1), :].rearrange("p a b -> p (a b)") for g in range(2)]
                pe_down_chunk(pe, c, hi, lo, d == 0, d == FT // 2 - 1)

            down_parts(dn, pe, after)

        def conv_columns(t, i):
            return [cols[:, COL[n][0] + t:COL[n][0] + t + 1] if i is None else
                    cols[:, bass.ds(i * 3 + COL[n][0] + t, 1)] for n in ("cw0", "cw1", "cw2", "cb")]

        def act_ffn(act, f, after=()):
            c0 = C_FFN[f]
            act_split(act, c0 + 2)

            def up(t, i):
                act.wait_ge(s_pe, c0 + t + 1 + run(i, 3))
                gate = bank[4 + t % 3][:, 0:SEQ]
                if f == 0:
                    w = conv_columns(t, i)
                    nc.scalar.activation(CG[:], gate, ACT.Identity, bias=w[3], scale=w[1]).then_inc(s_cstep, 1)
                    act.wait_ge(s_conv, t + 1 + run(i, 3))
                    gate = CG[:]
                nc.scalar.activation(SG[:, t % 3], gate, ACT.Silu).then_inc(s_silu, 1)
                act_split(act, c0 + t + 3, i)
                act.wait_ge(s_prod, FT * f + t + 1 + run(i, 3))
                nc.scalar.activation(hid(t, i, hid_hi), T[:, t % 3], ACT.Copy).then_inc(s_hidhi, 1)

            up_parts(up, act, f)
            down_parts(lambda d, i: d < FT // 2 - 1 and act_split(act, c0 + FT + d + 3, i),
                       act, after)

        def dve_ffn(dve, f, after=()):
            c0, u0 = C_FFN[f], UNITS[f]

            def rest(t, i):
                dve.wait_ge(s_hidhi, FT * f + t + 1 + run(i, 3))
                nc.vector.tensor_tensor(hid(t, i, hid_lo), T[:, t % 3], hid(t, i, hid_hi).bitcast(f32),
                                        ALU.subtract).then_inc(s_hid, 1)

            def mods(t, i, at):
                if f == 4 or t == 0:
                    return
                if f or i is None:
                    units, base, per = ((0,), (1,), (2, 3)), u0 + 4 * ((t - 1) // 3), 4
                else:
                    units, base, per = ((0,), (), (1,)), u0 + 4, 2
                for u in units[(t - 1) % 3][at:at + 1]:
                    dve_mod_unit(dve, base + u, i, per)

            def up(t, i):
                dve_split(dve, c0 + t + 2, i)
                b = bank[4 + t % 3]
                if f == 0:
                    w = conv_columns(t, i)
                    dve.wait_ge(s_cstep, 2 * t + 1 + run(i, 6))
                    nc.vector.scalar_tensor_tensor(out=CG[:, 64:256], in0=b[:, 0:192], scalar=w[0], in1=CG[:, 64:256],
                                                   op0=ALU.mult, op1=ALU.add).then_inc(s_cstep, 1)
                    dve.wait_ge(s_cstep, 2 * t + 2 + run(i, 6))
                    nc.vector.scalar_tensor_tensor(out=CG[:, 0:192], in0=b[:, 64:256], scalar=w[2], in1=CG[:, 0:192],
                                                   op0=ALU.mult, op1=ALU.add).then_inc(s_conv, 1)
                mods(t, i, 0)
                dve.wait_ge(s_silu, FT * f + t + 1 + run(i, 3))
                if FT * f + t > 2:
                    dve.wait_ge(s_hid, FT * f + t - 2 + run(i, 3))
                nc.vector.tensor_tensor(T[:, t % 3], SG[:, t % 3], b[:, SEQ:2 * SEQ], ALU.mult).then_inc(s_prod, 1)
                if t:
                    rest(t - 1, i)
                mods(t, i, 1)

            up_parts(up, dve, f)
            rest(FT - 1, None)

            def dn(d, i):
                dve_split(dve, c0 + FT + d + 2, i)
                if f == 0 and d < 2:
                    for u in range(2):
                        dve_mod_unit(dve, UNITS[1] - 14 + 2 * d + u)
                elif f < 4 and d >= 2 and (f or d < FT // 2 - 1):
                    last = UNITS[1] + 2 if f == 0 else UNITS[f] + 40
                    for u in ((0,), (1,), (2, 3))[(d - 2) % 3]:
                        dve_mod_unit(dve, last - 12 + 4 * ((d - 2) // 3) + u, i, 4)

            down_parts(dn, dve, after)

        s_in = [sem(f"inputs_loaded{j}") for j in range(8)]
        s_gup, s_c2 = sem("gla_gate_weights_loaded"), sem("second_c_loaded")
        s_out = sem("output_stored")
        s_bc = sem("decay_rows_broadcast")

        @block.sync
        def _(sp):
            sp.dma_start(ccol[:], c_cols).then_inc(s_in[0], 16)
            for c in range(3):
                sp.dma_start(raw[:, c], w_stream[c]).then_inc(s_raw[c], 16)
            sp.dma_start(X[:], xT).then_inc(s_in[3], 16)
            sp.dma_start(con[:, 0:2 * P], const_d[:, 0:2 * P]).then_inc(s_in[1], 16)

            def chunks(a, b):
                for c in range(a, b):
                    sp.wait_ge(s_lo, c - 2)
                    sp.dma_start(raw[:, c % 3], w_stream[c]).then_inc(s_raw[c % 3], 16)

            chunks(3, 5)
            sp.dma_start(cols[:], cols_d).then_inc(s_in[1], 16)
            sp.dma_start(XC[:], ctxT).then_inc(s_in[2], 16)
            chunks(5, 12)
            sp.dma_start(con[:, 2 * P:], const_d[:, 2 * P:]).then_inc(s_in[5], 16)
            turns = (N_CHUNKS - 12) // 3
            with sp.Fori(0, turns) as i:
                for j in range(3):
                    sp.wait_ge(s_lo, i * 3 + (j + 10))
                    sp.dma_start(raw[:, j], w_stream[bass.ds(i * 3 + (j + 12), 1)]
                                 .rearrange("a p n -> p (a n)")).then_inc(s_raw[j], 16)
            chunks(12 + 3 * turns, N_CHUNKS)
            sp.wait_ge(s_x, XU["f4"] + DT)
            sp.dma_start(out_d, X[:]).then_inc(s_out, 16)
            sp.wait_ge(s_out, 16)

        @block.gpsimd
        def _(pool):
            pool.wait_ge(s_lo, 6)
            pool.dma_start(cb[:], c_row.partition_broadcast(P)).then_inc(s_in[4], 16)
            for u in range(2):
                pool.dma_start(mring[:, u], m_stream[u]).then_inc(s_mod[u], 16)

            def mods(u0, turns):
                with pool.Fori(0, turns) as i:
                    for j in range(2):
                        pool.wait_ge(s_mused, i * 2 + (u0 + j - 1))
                        pool.dma_start(mring[:, j], m_stream[bass.ds(i * 2 + (u0 + j), 1)]
                                       .rearrange("a p n -> p (a n)")).then_inc(s_mod[j], 16)

            mods(2, 12)
            pool.wait_ge(s_bc, HEADS)
            pool.dma_start(cb2[:], c2_row.partition_broadcast(P)).then_inc(s_c2, 16)
            mods(26, (N_UNITS - 26) // 2)

        s_scol, s_c4h, s_c4 = sem("c_silu"), sem("c_rounded"), sem("c_split")
        s_mrow, s_mT, s_mm0 = sem("first_mods_rows"), sem("first_mods_columns"), sem("first_mods_read")
        s_cb = sem("c_rows_silu")
        s_eps = sem("eps_set")
        s_qk, s_vb = sem("qk_bank_read"), sem("v_bank_read")
        s_gr = sem("gates_read")
        s_ga, s_gd = sem("gate_exp_ln"), sem("gate_rows")
        s_uT, s_uc = sem("u_columns"), sem("u_columns_read")
        s_os, s_ad, s_sg = sem("o_bank_read"), sem("denominators_abs"), sem("o_sigmoid")
        s_s = sem("qk_scores")
        s_arg, s_e = sem("decay_exponents"), sem("decay_weights")
        s_p, s_den = sem("weighted_scores"), sem("denominators")
        s_th, s_gw2, s_num = sem("threshold_read"), sem("normalised_scores"), sem("numerators")
        s_y = sem("gated_tile")
        EXPS = 6

        def head_bank(h):
            return bank[(6, 4)[h % 2]]

        def pe_lstm(pe):
            c = C_LSTM
            pe.wait_ge(s_c4, 1)
            for k in range(DT):
                pe.wait_ge(s_lo, k + 1)
                for g in range(4):
                    mm(bank[g][:], c4[:, k], whi[:, k % 3, g * 512:(g + 1) * 512], k == 0)
                    ins = mm(bank[g][:], c4[:, k], wlo[:, k % 3, g * 512:(g + 1) * 512], False)
                ins.then_inc(s_pe, 1)
                if k == 4:
                    pe.wait_ge(s_in[1], 32)
                    pe_stat(pe, N_X1)
            pe_stat(pe, N_CTX)
            pe.wait_ge(s_mrow, 4)
            for m in range(FIRST_MODS):
                ins = nc.tensor.transpose(bank[4][:, 4 * m:4 * m + 4], mrow[:, m * P:(m + 1) * P], ident[0:4, 0:4])
            ins.then_inc(s_mT, 1)
            pe.wait_ge(s_mm0, 1)
            for j in range(2):
                pe_pair(pe, c + j, 4 + j, wait=U["x1"] if j == 0 else None)
            pe.wait_ge(s_lo, c + 3)
            pe.wait_ge(s_ln, 2)
            for n, hi, lo in ((1, hhi, hlo), (0, chi, clo)):
                for k in range(DT):
                    if n == 0:
                        pe.wait_ge(s_h, U["ctx"] + k + 1)
                    ins = mm3(bank[7][:, n * SEQ:(n + 1) * SEQ], c + 2, k, hi[:, k], lo[:, k], k == 0)
            ins.then_inc(s_pe, 1)
            for j in range(2):
                for n, (hi, lo) in enumerate(((hhi, hlo), (chi, clo))):
                    a = 2 + 2 * j + n
                    if a >= 3:
                        pe.wait_ge(s_qk, a - 2)
                    pe_pair(pe, c + 3 + j, 4 + a % 3, hi, lo, n == 1)
            tiles = [(chi, clo, 0), (chi, clo, 1), (hhi, hlo, 0), (hhi, hlo, 1)]
            his = [lambda k, b=b, t=t: b[:, k, t * P:(t + 1) * P] for b, _, t in tiles]
            los = [lambda k, b=b, t=t: b[:, k, t * P:(t + 1) * P] for _, b, t in tiles]
            def values(j):
                pe_wide(pe, c + 5 + j, 4 * (j % 2), [bank[b + 4 * (j // 2)][:] for b in range(4)], his, los)

            values(0)
            values(1)
            pe.wait_ge(s_qk, 6)
            values(2)

            def rows(h):
                if h:
                    pe.wait_ge(s_e, EXPS * h - 1)
                for d in range(2):
                    q = (d * 4 + h) * P
                    mm(bank[2 + d][:, 0:SEQ], cst("sel")[0:36, q:q + P], mt[:], True)
                    ins = mm(bank[2 + d][:, SEQ:], cst("sel")[0:36, q:q + P], th[:], True)
                ins.then_inc(s_bc, 1)

            def scores(h):
                if h:
                    pe.wait_ge(s_p, 2 * h)
                for st in range(4):
                    ins = mm(bank[st // 2][:, (st % 2) * SEQ:(st % 2 + 1) * SEQ], K[:, h, st * P:(st + 1) * P],
                             Q[:, h], True)
                ins.then_inc(s_s, 1)

            def denominators(h):
                for n, d in enumerate((1, 0)):
                    pe.wait_ge(s_p, 2 * h + n + 1)
                    if h and n == 0:
                        pe.wait_ge(s_ad, h)
                    for st in range(4):
                        ins = mm(bank[5][:, d * SEQ:(d + 1) * SEQ], ones, EF[h % 2][:, d, st], st == 0)
                ins.then_inc(s_den, 1)

            def numerators(h):
                pe.wait_ge(s_gw2, h + 1)
                if h >= 2:
                    pe.wait_ge(s_y, 2 * h - 2)
                for v in range(2):
                    for st in range(4):
                        ins = mm(head_bank(h)[:, v * SEQ:(v + 1) * SEQ], V[:, st, h * DV + v * P:h * DV + (v + 1) * P],
                                 EF[h % 2][:, 0, st], st == 0)
                ins.then_inc(s_num, 1)

            def output_gate(j):
                if j:
                    pe.wait_ge(s_os, j)
                pe_pair(pe, c + 9 + j, 4)

            def out_chunk(j):
                pe.wait_ge(s_lo, c + 14 + j)
                for g in range(2):
                    pe.wait_ge(s_h, U["lstm_y"] + 2 * j + g + 1)
                pe_down_chunk(pe, c + 13 + j, [hhi[:, 2 * j], hhi[:, 2 * j + 1]], [hlo[:, 2 * j], hlo[:, 2 * j + 1]],
                              j == 0, j == 3)

            pe.wait_ge(s_in[5], 16)
            pe.wait_ge(s_gd, 1)
            pe.wait_ge(s_vb, 4)
            rows(0)
            for st in range(4):
                ins = nc.tensor.transpose(bank[1][:, st * 36:(st + 1) * 36], ut[:, st * P:(st + 1) * P],
                                          ident[0:36, 0:36])
            ins.then_inc(s_uT, 1)
            values(3)
            pe.wait_ge(s_uc, 1)
            scores(0)
            pe.wait_ge(s_vb, 8)
            output_gate(0)
            rows(1)
            output_gate(1)
            denominators(0)
            scores(1)
            output_gate(2)
            denominators(1)
            scores(2)
            output_gate(3)
            pe.wait_ge(s_os, 4)
            for h in range(HEADS):
                if 1 <= h < HEADS - 1:
                    denominators(h + 1)
                if h == 1:
                    scores(3)
                if h >= 2:
                    out_chunk(h - 2)
                if h + 2 < HEADS:
                    rows(h + 2)
                numerators(h)
                pe_stat(pe, N_LSTM + h)
            out_chunk(2)
            out_chunk(3)

        def act_lstm(act):
            c = C_LSTM
            act.wait_ge(s_in[0], 16)
            nc.scalar.activation(scol[:], ccol[:], ACT.Silu).then_inc(s_scol, 1)
            act.wait_ge(s_scol, 1)
            act.wait_ge(s_eps, 1)
            for n in range(2):
                nc.scalar.activation(c4[:, :, 2 * n:2 * n + 1], scol[:, :, n:n + 1], ACT.Copy).then_inc(s_c4h, 1)
            act_split(act, 0)
            act_split(act, 1)
            act_split(act, 2)
            act_squares(act, N_X1, lambda j: X[:, j], lambda j: (s_in[3], 16))
            for j in range(3, 7):
                act_split(act, j)
            act_rstd(act, N_X1, D)
            act_split(act, 7)
            act_squares(act, N_CTX, lambda j: XC[:, j], lambda j: (s_in[2], 16), False)
            act_split(act, c)
            act.wait_ge(s_pe, 8)
            for g in range(2):
                nc.scalar.activation(mrow[:, g * 512:(g + 1) * 512], bank[g][0:4], ACT.Copy).then_inc(s_mrow, 1)
            act_rstd(act, N_CTX, D)
            act_modulate(act, mcol(0), "x1")
            act_split(act, c + 1)
            act_split(act, c + 2)
            act_modulate(act, lambda j: modc[:, j:j + 1], "ctx", chi)
            act_split(act, c + 3)
            act.wait_ge(s_in[4], 16)
            nc.scalar.activation(cb[:], cb[:], ACT.Silu).then_inc(s_cb, 1)
            act.preload_act_table_set(LN_EXP)

            def values_read(half):
                act.wait_ge(s_pe, c + 7 + 2 * half)
                for b in (1, 3):
                    nc.scalar.activation(V[:, b, half * 512:(half + 1) * 512], bank[b + 4 * half][:], ACT.Copy)\
                        .then_inc(s_vb, 1)

            for j in range(9):
                if j > 1:
                    act_split(act, c + j + 2)
                if j == 6:
                    values_read(0)
                if j == 4:
                    act.wait_ge(s_gr, 1)
                    alink(act, nc.scalar.activation(ga[:], gf[:], ACT.Abs))
                    alink(act, nc.scalar.activation(ga[:], ga[:], ACT.Exp, scale=-1.0))
                    nc.scalar.activation(ga[:], ga[:], ACT.Ln, bias=1.0).then_inc(s_ga, 1)
                if j == 6:
                    act.wait_ge(s_gr, 2)
                    nc.scalar.activation(gb[:], ga[:], ACT.Exp, scale=-1.0).then_inc(s_ga, 1)

            def decay(h, d):
                e, b = EF[h % 2], bank[2 + d]
                if d:
                    act.wait_ge(s_bc, h + 1)
                    nc.scalar.activation(thb[:, h, 0], bank[2][:, SEQ:], ACT.Copy).then_inc(s_th, 1)
                    act.wait_ge(s_arg, 4 * h + 2)
                    nc.scalar.activation(thb[:, h, 1], b[:, SEQ:], ACT.Copy).then_inc(s_th, 1)
                    if h >= 2:
                        act.wait_ge(s_gw2, h - 1)
                else:
                    act.wait_ge(s_arg, 4 * h + 4)
                    if h >= 2:
                        act.wait_ge(s_num, h - 1)
                for st in range(2):
                    nc.scalar.activation(e[:, d, st], b[:, 0:SEQ], ACT.Exp,
                                         bias=uc[:, st, 32 * d + h:32 * d + h + 1]).then_inc(s_e, 1)
                nc.scalar.activation(e[:, d, 2:4], e[:, d, 2:4], ACT.Exp).then_inc(s_e, 1)

            def gate_read(j):
                act_split(act, c + 9 + j + 2)
                act.wait_ge(s_pe, c + 9 + j + 1)
                nc.scalar.activation(flat(OS[:, 2 * j:2 * j + 2]), bank[4][:], ACT.Copy).then_inc(s_os, 1)

            def magnitudes(h):
                act.wait_ge(s_den, h + 1)
                if h:
                    act.wait_ge(s_gw2, h)
                nc.scalar.activation(flat(rd[:]), bank[5][:], ACT.Abs).then_inc(s_ad, 1)

            def round_head(h):
                for j in (2 * h, 2 * h + 1):
                    act.wait_ge(s_y, j + 1)
                    nc.scalar.activation(hhi[:, j], T[:, j % 2], ACT.Copy).then_inc(s_hhi, 1)

            act.wait_ge(s_uc, 1)
            decay(0, 1)
            decay(0, 0)
            values_read(1)
            gate_read(0)
            decay(1, 1)
            decay(1, 0)
            gate_read(1)
            magnitudes(0)
            gate_read(2)
            magnitudes(1)
            gate_read(3)
            act.wait_ge(s_os, 4)
            nc.scalar.activation(OS[:], OS[:], ACT.Sigmoid).then_inc(s_sg, 1)
            for h in range(HEADS):
                if 1 <= h < HEADS - 1:
                    magnitudes(h + 1)
                if h:
                    round_head(h - 1)
                    act_split(act, c + 14 + h)
                if h + 2 < HEADS:
                    decay(h + 2, 1)
                act_squares(act, N_LSTM + h, lambda j: head_bank(h)[:, j * SEQ:(j + 1) * SEQ],
                            lambda j: (s_num, h + 1), h == 0)
                if h + 2 < HEADS:
                    decay(h + 2, 0)
                act_rstd(act, N_LSTM + h, DV)
            round_head(HEADS - 1)
            act_split(act, c + 18)

        def dve_lstm(dve):
            c = C_LSTM
            nc.vector.memset(eps[:], EPS)
            nc.vector.memset(c4[:].bitcast(f32), 0.0).then_inc(s_eps, 1)
            nc.vector.memset(gi[:], 0.0)
            nc.vector.memset(ut[:], 0.0)
            nc.vector.memset(mt[:], 0.0)
            nc.vector.memset(th[:], 0.0)
            dve.wait_ge(s_c4h, 2)
            nc.vector.tensor_tensor(c4[:, :, 1:4:2], scol[:], c4[:, :, 0:4:2].bitcast(f32), ALU.subtract)\
                .then_inc(s_c4, 1)
            for j in range(9):
                dve_split(dve, j)
            dve.wait_ge(s_mrow, 2)
            for g in range(2, 4):
                nc.vector.tensor_copy(mrow[:, g * 512:(g + 1) * 512], bank[g][0:4]).then_inc(s_mrow, 1)
            dve.wait_ge(s_in[1], 32)
            dve.wait_ge(s_mT, 1)
            nc.vector.tensor_reduce(CG[:, 0:2 * FIRST_MODS],
                                    bank[4][:, 0:4 * FIRST_MODS].rearrange("p (m t) -> p m t", t=2), AX.X, ALU.add)\
                .then_inc(s_mm0, 1)
            dve.wait_ge(s_mm0, 1)
            pm = CG[:, 0:2 * FIRST_MODS].rearrange("p (m t) -> p t m", t=2)
            nc.vector.tensor_tensor(modc[:], pm[:, 1], cols[:, 0:FIRST_MODS], ALU.add)
            link(dve, nc.vector.tensor_tensor(mod[:, 0:FIRST_MODS], pm[:, 0], cols[:, 0:FIRST_MODS], ALU.add))
            dve_coef_pre(dve, 1, 8, col("g_mix", 0, 8))
            dve_modulate(dve, N_X1, cq(1), mcol(0), "x1")
            dve_coef_pre(dve, 0, 8, col("g_mix", 0, 8), modc)
            dve_split(dve, c + 1)
            dve_split(dve, c + 2)
            dve_modulate(dve, N_CTX, cq(0), lambda j: modc[:, j:j + 1], "ctx", XC, chi, clo)
            nc.vector.memset(gf[:], 0.0)
            dve.wait_ge(s_cb, 1)
            two = lambda x: x.rearrange("p (a b) -> p a b", a=2)

            def mods(u, n):
                for k in range(n):
                    dve_mod_unit(dve, u + k)

            dve_split(dve, c + 3)
            for j in range(2):
                dve.wait_ge(s_pe, c + j + 1)
                nc.vector.tensor_copy(flat(Q[:, 2 * j:2 * j + 2]), bank[4 + j][:]).then_inc(s_qk, 1)
                mods(2 * j, 2)
            dve_split(dve, c + 4)
            dve.wait_ge(s_pe, c + 3)
            link(dve, nc.vector.tensor_scalar(g_all[:], bank[7][:], col("b_gate"), None, ALU.add))
            nc.vector.tensor_copy(gi[0:4], g_all[0:4])
            nc.vector.tensor_copy(two(gi[32:36]), two(g_all[32:36])[:, :, ::-1])
            nc.vector.tensor_copy(gf[0:4], g_all[64:68])
            nc.vector.tensor_copy(two(gf[32:36]), two(g_all[96:100])[:, :, ::-1]).then_inc(s_gr, 1)
            mods(4, 2)
            for j in range(2):
                dve_split(dve, c + 3 + j + 2)
                dve.wait_ge(s_pe, c + 3 + j + 1)
                for n in range(2):
                    a = 2 + 2 * j + n
                    nc.vector.tensor_scalar(K[:, 2 * j:2 * j + 2, (1 - n) * SEQ:(2 - n) * SEQ],
                                            bank[4 + a % 3][:].rearrange("p (m t) -> p m t", m=2),
                                            DK ** -0.5, None, ALU.mult).then_inc(s_qk, 1)
                mods(6 + 2 * j, 2)
            dve.wait_ge(s_ga, 1)
            link(dve, nc.vector.scalar_tensor_tensor(out=gf[:], in0=gf[:], scalar=0.0, in1=ga[:], op0=ALU.min,
                                                     op1=ALU.subtract))
            link(dve, nc.vector.tensor_tensor_scan(g_all[0:36], ones[0:36, 0:1].to_broadcast([36, 512]), gf[:], 0.0,
                                                   ALU.mult, ALU.add))
            link(dve, nc.vector.tensor_tensor(gi[:], gi[:], g_all[0:36], ALU.subtract))
            link(dve, nc.vector.tensor_tensor_scan(gf[:], gi[:], gi[:], 0.0, ALU.max, ALU.max))
            nc.vector.tensor_tensor(ga[:], gf[:], g_all[0:36], ALU.add).then_inc(s_gr, 1)
            nc.vector.tensor_copy(ut[0:4], gi[0:4])
            nc.vector.tensor_copy(two(ut[32:36]), two(gi[32:36])[:, :, ::-1])
            nc.vector.tensor_scalar(mt[0:4], gf[0:4, SEQ:], -1.0, None, ALU.mult)
            nc.vector.tensor_scalar(mt[32:36], gf[32:36, SEQ:][:, ::-1], -1.0, None, ALU.mult)
            mods(10, 2)
            dve_split(dve, c + 7)
            mods(12, 2)
            dve_split(dve, c + 8)
            dve.wait_ge(s_ga, 2)
            nc.vector.tensor_copy(th[0:4], gb[0:4, SEQ:])
            nc.vector.tensor_copy(th[32:36], gb[32:36, SEQ:][:, ::-1]).then_inc(s_gd, 1)
            mods(14, 2)

            def values_read(half):
                dve.wait_ge(s_pe, c + 7 + 2 * half)
                for b in (0, 2):
                    nc.vector.tensor_copy(V[:, b, half * 512:(half + 1) * 512], bank[b + 4 * half][:])\
                        .then_inc(s_vb, 1)

            values_read(0)
            mods(16, 2)
            dve_split(dve, c + 9)
            dve.wait_ge(s_uT, 1)
            nc.vector.tensor_copy(flat(uc[:]), bank[1][:, 0:144]).then_inc(s_uc, 1)
            mods(18, 2)
            dve_split(dve, c + 10)
            dve.wait_ge(s_uc, 1)
            madd = cst("madd").rearrange("p (d s t) -> p d s t", d=2, s=2)

            def exponents(h):
                e = EF[h % 2]
                dve.wait_ge(s_bc, h + 1)
                for d in (1, 0):
                    if d == 0:
                        dve.wait_ge(s_th, 2 * h + 1)
                    if h >= 2:
                        dve.wait_ge(*((s_gw2, h - 1) if d else (s_num, h - 1)))
                    for st in range(2):
                        nc.vector.scalar_tensor_tensor(out=e[:, d, 2 + st], in0=bank[2 + d][:, 0:SEQ],
                                                       scalar=uc[:, 2 + st, 32 * d + h:32 * d + h + 1],
                                                       in1=madd[:, d, st], op0=ALU.add, op1=ALU.add)\
                            .then_inc(s_arg, 1)

            def weighted(h):
                dve.wait_ge(s_s, h + 1)
                for n, d in enumerate((1, 0)):
                    dve.wait_ge(s_e, EXPS * h + 3 * (n + 1))
                    for b in range(2):
                        e = flat(EF[h % 2][:, d, 2 * b:2 * b + 2])
                        ins = nc.vector.tensor_tensor(e, e, bank[b][:], ALU.mult)
                    ins.then_inc(s_p, 1)

            def normalise(h):
                e = EF[h % 2]
                dve.wait_ge(s_ad, h + 1)
                link(dve, nc.vector.tensor_tensor(flat(rd[:]), flat(rd[:]), flat(thb[:, h]), ALU.max))
                link(dve, nc.vector.reciprocal(flat(rd[:]), flat(rd[:])))
                for d in range(2):
                    ins = nc.vector.tensor_tensor(e[:, d], e[:, d], rd[:, d:d + 1].to_broadcast([P, 4, SEQ]),
                                                  ALU.mult)
                link(dve, ins)
                nc.vector.tensor_tensor(e[:, 0], e[:, 0], e[:, 1], ALU.add).then_inc(s_gw2, 1)

            def finish_head(h):
                dve.wait_ge(s_rstd, N_LSTM + h + 1)
                dve.wait_ge(s_sg, 1)
                dve.wait_ge(s_h, U["lstm_y"] + 2 * h)
                for v in range(2):
                    ins = nc.vector.scalar_tensor_tensor(out=T[:, v], in0=head_bank(h)[:, v * SEQ:(v + 1) * SEQ],
                                                         scalar=col("gain", 2 * h + v), in1=rs(N_LSTM + h),
                                                         op0=ALU.mult, op1=ALU.mult)
                link(dve, ins)
                for v in range(2):
                    nc.vector.tensor_tensor(T[:, v], T[:, v], OS[:, 2 * h + v], ALU.mult).then_inc(s_y, 1)
                for v in range(2):
                    j = 2 * h + v
                    dve.wait_ge(s_hhi, U["lstm_y"] + j + 1)
                    nc.vector.tensor_tensor(hlo[:, j], T[:, v], hhi[:, j].bitcast(f32), ALU.subtract)\
                        .then_inc(s_h, 1)

            dve.wait_ge(s_in[5], 16)
            exponents(0)
            mods(20, 2)
            values_read(1)
            dve_split(dve, c + 11)
            weighted(0)
            mods(22, 1)
            exponents(1)
            dve_split(dve, c + 12)
            weighted(1)
            for h in range(HEADS):
                normalise(h)
                if h == 0:
                    dve_split(dve, c + 13)
                    dve_split(dve, c + 14)
                else:
                    finish_head(h - 1)
                    if h > 1:
                        dve_split(dve, c + 14 + h)
                if h + 2 < HEADS:
                    exponents(h + 2)
                    if h == 1:
                        dve_split(dve, c + 15)
                    else:
                        mods(23, 2)
                    weighted(h + 2)
                elif h == 2:
                    mods(25, 2)
            finish_head(HEADS - 1)
            mods(27, 1)
            dve_split(dve, c + 18)
            after_units(dve, 0, UNITS[0])
            dve_add_plain(dve, 16, 0, c + 16)

        def x_ready(u):
            return lambda j: (s_x, u + j + 1)

        def ng(layer, sub, post):
            return col("norm_g", ((layer * 3 + sub) * 2 + post) * DT, DT)

        SWIGLU = {1: (0, 0, N_F1, "f1", "fin"), 2: (0, 2, N_F2, "f2", "gla"), 3: (1, 0, N_F3, "f3", "f2"),
                  4: (1, 2, N_F4, "f4", "mla")}

        OUTS = {"f1": 2, "gla": 3, "f2": 4, "f3": 5, "mla": 6, "f4": 7}

        def pe_swiglu(pe, f):
            _, _, n, name, _ = SWIGLU[f]
            pe_stat(pe, n)
            if f == 3:
                pe_ffn(pe, f, U[name], {8: lambda: pe_stat(pe, N_KV)})
            else:
                pe_ffn(pe, f, U[name])
                pe_stat(pe, n + 1)

        def act_swiglu(act, f):
            layer, sub, n, name, before = SWIGLU[f]
            if f == 3:
                act.dma_start(CG[:].bitcast(i32), pos_d.partition_broadcast(P)).then_inc(s_pos, 16)
            act_squares(act, n, lambda j: X[:, j], x_ready(XU[before]))
            act_rstd(act, n, D)
            act_modulate(act, mcol(M_COND[layer] + 3 * sub * DT), name)
            post = N_F3P if f == 3 else n + 1
            act_ffn(act, f, {7: lambda: act_kv_norm(act), 8: lambda: act_kv_input(act)} if f == 3 else ())
            act_squares(act, post, down, lambda j: down_done(OUTS[name], j, C_FFN[f] + FFN_CHUNKS - 1))
            act_rstd(act, post, D)

        def dve_swiglu(dve, f):
            layer, sub, n, name, _ = SWIGLU[f]
            m0 = M_COND[layer] + 3 * sub * DT
            dve_coef_pre(dve, 3, m0 + DT, ng(layer, sub, 0))
            dve_coef_post(dve, 4, m0 + 2 * DT, ng(layer, sub, 1), 0.5)
            dve_modulate(dve, n, cq(3), mcol(m0), name)
            if f == 3:
                dve_ffn(dve, f, {0: lambda: dve_angles(dve, 0), 1: lambda: dve_angles(dve, 1),
                                 8: lambda: dve_kv_input(dve)})
            else:
                dve_ffn(dve, f)
            if f < 4:
                after_units(dve, UNITS[f], GLA_UNITS if f == 1 else UNITS[f + 1])
            dve_add_post(dve, N_F3P if f == 3 else n + 1, 4, XU[name])

        s_gb, s_z, s_zr = sem("gla_bank_read"), sem("gate_products"), sem("gate_products_read")
        s_gln, s_gsc, s_gex = sem("gla_gate_ln"), sem("gla_gate_scan"), sem("gla_gate_exp")
        s_qkd, s_gvb, s_r = sem("gla_qk_decayed"), sem("gla_v_bank_read"), sem("gla_r_bank_read")
        s_att, s_attr, s_kut = sem("gla_scores"), sem("gla_scores_read"), sem("gla_keys_transposed_read")
        s_upd, s_st, s_o = sem("gla_updates"), sem("gla_states"), sem("gla_head_output")

        def upd(n):
            return bank[2 + n % 2][:, (n // 2) * DV:(n // 2 + 1) * DV]

        def gla_bank(h):
            return bank[(5, 6)[h % 2]]

        def pe_gla(pe):
            c, n0 = C_GLA, N_GLA
            pe_stat(pe, n0)
            pe.wait_ge(s_lo, c + 2)
            pe_first_chunks(pe, U["gla"], [(c, bank[4], 1), (c + 1, bank[5], 2)])
            for j, b in enumerate((6, 4, 5), 1):
                if j >= 2:
                    pe.wait_ge(s_gb, j - 1)
                pe_pair(pe, c + 1 + j, b)
            pe.wait_ge(s_gb, 4)
            pe.wait_ge(s_gup, 16)
            for h in range(HEADS):
                ins = mm(bank[(6, 4)[h // 2]][:, (h % 2) * SEQ:(h % 2 + 1) * SEQ], wgu[:, h * DK:(h + 1) * DK], glow[:],
                         h % 2 == 0)
            ins.then_inc(s_z, 1)
            his = [lambda k, t=t: hhi[:, k, t * P:(t + 1) * P] for t in range(2)]
            los = [lambda k, t=t: hlo[:, k, t * P:(t + 1) * P] for t in range(2)]
            for j in range(4):
                b = 2 * (j // 2)
                pe_wide(pe, c + 5 + j, 4 * (j % 2), [bank[b][:], bank[b + 1][:]], his, los)

            def gate(j):
                if j >= 2:
                    pe.wait_ge(s_r, j - 1)
                pe_pair(pe, c + 9 + j, (6, 4)[j % 2])

            def scores(h):
                if h:
                    pe.wait_ge(s_attr, h)
                    pe.wait_ge(s_kut, h)
                for t in range(2):
                    tt = slice(t * P, (t + 1) * P)
                    mm(bank[0][:, tt], GK[:, h, tt], GQ[:, h, tt], t == 0)
                for t in range(2):
                    tt = slice(t * P, (t + 1) * P)
                    ins = nc.tensor.transpose(bank[1][:, tt], GKU[:, h, tt], ident)
                ins.then_inc(s_att, 1)

            def updates(h):
                pe.wait_ge(s_kut, h + 1)
                if h:
                    pe.wait_ge(s_st, 3 * h)
                for n in range(3):
                    half = slice(64 * (n % 2), 64 * (n % 2) + 64)
                    ins = mm(upd(n), kut[h % 2][half, n // 2], GV[half, n // 2, h * DV:(h + 1) * DV], n < 2)
                ins.then_inc(s_upd, 1)

            def output(h):
                pe.wait_ge(s_attr, h + 1)
                pe.wait_ge(s_st, 3 * h + 3)
                if h >= 2:
                    pe.wait_ge(s_y, 2 * HEADS + 2 * h - 2)
                o = gla_bank(h)
                for v in range(2):
                    for t in range(2):
                        mm(o[:, v * SEQ + t * P:v * SEQ + (t + 1) * P],
                           GV[:, t, h * DV + v * P:h * DV + (v + 1) * P], att[h % 2][:, t], v == 0 and t == 0)
                    for n in range(1, 4):
                        ins = mm(o[:, v * SEQ + n * CHUNK:v * SEQ + (n + 1) * CHUNK],
                                 ST[h % 2][:, n - 1, v * P:(v + 1) * P], GQ[:, h, n * CHUNK:(n + 1) * CHUNK], False)
                ins.then_inc(s_o, 1)

            def out_chunk(j):
                pe.wait_ge(s_lo, c + 14 + j)
                for g in range(2):
                    pe.wait_ge(s_h, U["gla_y"] + 2 * j + g + 1)
                pe_down_chunk(pe, c + 13 + j, [hhi[:, 2 * j], hhi[:, 2 * j + 1]], [hlo[:, 2 * j], hlo[:, 2 * j + 1]],
                              j == 0, j == 3)

            pe.wait_ge(s_gvb, 4)
            pe.wait_ge(s_qkd, 2)
            scores(0)
            pe.wait_ge(s_zr, 4)
            gate(0)
            updates(0)
            gate(1)
            scores(1)
            gate(2)
            updates(1)
            gate(3)
            pe.wait_ge(s_r, 4)
            output(0)
            scores(2)
            pe_stat(pe, N_GHEAD)
            updates(2)
            output(1)
            scores(3)
            pe_stat(pe, N_GHEAD + 1)
            updates(3)
            output(2)
            pe_stat(pe, N_GHEAD + 2)
            output(3)
            out_chunk(0)
            pe_stat(pe, N_GHEAD + 3)
            for j in range(1, 4):
                out_chunk(j)
            pe_stat(pe, N_GPOST)

        flat = lambda x: x.rearrange("p a b -> p (a b)")

        def act_gla(act):
            c = C_GLA
            act_squares(act, N_GLA, lambda j: X[:, j], x_ready(XU["f1"]))
            act.wait_ge(s_pe, c)
            act.dma_start(wgu[:], w_gup).then_inc(s_gup, 16)
            act_rstd(act, N_GLA, D)
            act_modulate(act, mcol(M_COND[0] + 3 * DT), "gla")
            for j in range(5):
                act_split(act, c + j + 2)
            act.preload_act_table_set(LN_EXP)
            act.wait_ge(s_z, 1)
            for h in range(HEADS):
                nc.scalar.activation(LA[:, h], bank[(6, 4)[h // 2]][:, (h % 2) * SEQ:(h % 2 + 1) * SEQ], ACT.Identity,
                                     bias=col("b_gla", h)).then_inc(s_zr, 1)
            act.wait_ge(s_zr, 4)
            alink(act, nc.scalar.activation(LB[:], LA[:], ACT.Abs))
            alink(act, nc.scalar.activation(LB[:], LB[:], ACT.Exp, scale=-1.0))
            nc.scalar.activation(LB[:], LB[:], ACT.Ln, bias=1.0).then_inc(s_gln, 1)
            for j in range(2):
                act_split(act, c + 5 + j + 2)
            act.wait_ge(s_gsc, 1)
            nc.scalar.activation(EB[:], LB[:], ACT.Exp, scale=1 / 16).then_inc(s_gex, 1)
            nc.scalar.activation(EN[:], LB[:], ACT.Exp, scale=-1 / 16).then_inc(s_gex, 1)
            act.wait_ge(s_gsc, 2)
            nc.scalar.activation(LA[:], LA[:], ACT.Exp, scale=1 / 16).then_inc(s_gex, 1)
            for j in range(2, 4):
                act_split(act, c + 5 + j + 2)

            def keys_read(h):
                act.wait_ge(s_att, h + 1)
                if h >= 2:
                    act.wait_ge(s_upd, h - 1)
                nc.scalar.activation(flat(kut[h % 2][:]), bank[1][:, 0:SEQ], ACT.Copy).then_inc(s_kut, 1)

            def gate_read(j):
                act.wait_ge(s_pe, c + 9 + j + 1)
                nc.scalar.activation(flat(SR[:, 2 * j:2 * j + 2]), bank[(6, 4)[j % 2]][:], ACT.Silu).then_inc(s_r, 1)

            def head_squares(h):
                act_squares(act, N_GHEAD + h, lambda j: gla_bank(h)[:, j * SEQ:(j + 1) * SEQ],
                            lambda j: (s_o, h + 1), h == 0)

            def round_head(h):
                for j in (2 * h, 2 * h + 1):
                    act.wait_ge(s_y, 2 * HEADS + j + 1)
                    nc.scalar.activation(hhi[:, j], T[:, j % 2], ACT.Copy).then_inc(s_hhi, 1)

            act_split(act, c + 11)
            keys_read(0)
            gate_read(0)
            act_split(act, c + 12)
            gate_read(1)
            keys_read(1)
            act_split(act, c + 13)
            gate_read(2)
            act_split(act, c + 14)
            gate_read(3)
            for h in range(HEADS):
                head_squares(h)
                if h < 2:
                    keys_read(h + 2)
                act_rstd(act, N_GHEAD + h, DV)
                if h == 1:
                    act_split(act, c + 15)
                round_head(h)
            for j in range(16, 19):
                act_split(act, c + j)
            act_squares(act, N_GPOST, down, lambda j: down_done(OUTS["gla"], j, c + 16))
            act_rstd(act, N_GPOST, D)

        def dve_gla(dve):
            c, m0 = C_GLA, M_COND[0] + 3 * DT
            dve_coef_pre(dve, 3, m0 + DT, ng(0, 1, 0))
            dve_coef_post(dve, 4, m0 + 2 * DT, ng(0, 1, 1), 1.0)
            dve_modulate(dve, N_GLA, cq(3), mcol(m0), "gla")
            for j in range(5):
                dve_split(dve, c + j + 2)
                dve.wait_ge(s_pe, c + j + 1)
                if j == 0:
                    nc.vector.tensor_copy(glow[:], bank[4][0:16, 0:SEQ]).then_inc(s_gb, 1)
                elif j < 3:
                    nc.vector.tensor_scalar(flat(GQ[:, 2 * j - 2:2 * j]), bank[4 + j][:], DK ** -0.5, None,
                                            ALU.mult).then_inc(s_gb, 1)
                else:
                    nc.vector.tensor_copy(flat(GK[:, 2 * j - 6:2 * j - 4]), bank[1 + j][:]).then_inc(s_gb, 1)
                if j:
                    dve_mod_unit(dve, GLA_UNITS + j - 1)
            dve.wait_ge(s_gln, 1)
            link(dve, nc.vector.scalar_tensor_tensor(out=flat(LA[:]), in0=flat(LA[:]), scalar=0.0, in1=flat(LB[:]),
                                                     op0=ALU.min, op1=ALU.subtract))
            for h in range(HEADS):
                ins = nc.vector.tensor_tensor_scan(LB[:, h], cst("reset"), LA[:, h], 0.0, ALU.mult, ALU.add)
            ins.then_inc(s_gsc, 1)
            dve.wait_ge(s_gsc, 1)
            b4 = flat(LB[:]).rearrange("p (n c) -> p n c", c=CHUNK)
            nc.vector.tensor_tensor(flat(LA[:]).rearrange("p (n c) -> p n c", c=CHUNK),
                                    b4[:, :, CHUNK - 1:CHUNK].to_broadcast([P, 16, CHUNK]), b4, ALU.subtract)\
                .then_inc(s_gsc, 1)
            for j in range(2):
                dve_split(dve, c + 5 + j + 2)
            dve.wait_ge(s_gex, 3)
            nc.vector.tensor_tensor(flat(GQ[:]), flat(GQ[:]), flat(EB[:]), ALU.mult).then_inc(s_qkd, 1)
            link(dve, nc.vector.tensor_tensor(flat(GKU[:]), flat(GK[:]), flat(LA[:]), ALU.mult))
            nc.vector.tensor_tensor(flat(GK[:]), flat(GK[:]), flat(EN[:]), ALU.mult).then_inc(s_qkd, 1)
            dve_split(dve, c + 9)
            for half in range(2):
                dve.wait_ge(s_pe, c + 7 + 2 * half)
                for t in range(2):
                    nc.vector.tensor_copy(GV[:, t, half * 512:(half + 1) * 512], bank[2 * half + t][:])\
                        .then_inc(s_gvb, 1)
                if half == 0:
                    for u in range(2):
                        dve_mod_unit(dve, GLA_UNITS + 4 + u)
            dve_split(dve, c + 10)
            eb4 = flat(EB[:]).rearrange("p (n c) -> p n c", c=CHUNK)

            def masked(h):
                a = flat(att[h % 2][:])
                dve.wait_ge(s_att, h + 1)
                if h >= 2:
                    dve.wait_ge(s_o, h - 1)
                link(dve, nc.vector.tensor_scalar(a, bank[0][:, 0:SEQ], 3e38, -3e38, ALU.min, ALU.max))
                nc.vector.tensor_tensor(a, a, cst("causal"), ALU.mult).then_inc(s_attr, 1)

            def states(h):
                dve.wait_ge(s_upd, h + 1)
                if h >= 2:
                    dve.wait_ge(s_o, h - 1)
                nc.vector.tensor_copy(ST[h % 2][:, 0], upd(0)).then_inc(s_st, 1)
                for n in range(1, 3):
                    dve.wait_ge(s_st, 3 * h + n)
                    nc.vector.scalar_tensor_tensor(out=ST[h % 2][:, n], in0=ST[h % 2][:, n - 1],
                                                   scalar=eb4[:, 4 * h + n, CHUNK - 1:CHUNK],
                                                   in1=upd(n), op0=ALU.mult, op1=ALU.add).then_inc(s_st, 1)

            def finish_head(h):
                dve.wait_ge(s_rstd, N_GHEAD + h + 1)
                dve.wait_ge(s_r, 4)
                dve.wait_ge(s_h, U["gla_y"] + 2 * h)
                for v in range(2):
                    ins = nc.vector.scalar_tensor_tensor(out=T[:, v], in0=gla_bank(h)[:, v * SEQ:(v + 1) * SEQ],
                                                         scalar=col("g_out", v), in1=rs(N_GHEAD + h),
                                                         op0=ALU.mult, op1=ALU.mult)
                link(dve, ins)
                for v in range(2):
                    nc.vector.tensor_tensor(T[:, v], T[:, v], SR[:, 2 * h + v], ALU.mult).then_inc(s_y, 1)
                for v in range(2):
                    j = 2 * h + v
                    dve.wait_ge(s_hhi, U["gla_y"] + j + 1)
                    nc.vector.tensor_tensor(hlo[:, j], T[:, v], hhi[:, j].bitcast(f32), ALU.subtract)\
                        .then_inc(s_h, 1)

            masked(0)
            dve_split(dve, c + 11)
            dve_mod_unit(dve, GLA_UNITS + 6)
            states(0)
            dve_split(dve, c + 12)
            dve_mod_unit(dve, GLA_UNITS + 7)
            masked(1)
            dve_split(dve, c + 13)
            dve_mod_unit(dve, GLA_UNITS + 8)
            states(1)
            dve_split(dve, c + 14)
            masked(2)
            finish_head(0)
            states(2)
            dve_mod_unit(dve, GLA_UNITS + 9)
            masked(3)
            finish_head(1)
            states(3)
            dve_split(dve, c + 15)
            dve_mod_unit(dve, GLA_UNITS + 10)
            dve_mod_unit(dve, GLA_UNITS + 11)
            finish_head(2)
            finish_head(3)
            dve_split(dve, c + 16)
            for u in range(12, 14):
                dve_mod_unit(dve, GLA_UNITS + u)
            after_units(dve, GLA_UNITS, UNITS[2])
            for j in range(17, 19):
                dve_split(dve, c + j)
            dve_add_post(dve, N_GPOST, 4, XU["gla"])

        s_lt, s_lhi, s_l = sem("latent_scaled"), sem("latent_rounded"), sem("latent_split")
        s_pos, s_ang, s_cs = sem("positions_loaded"), sem("angles"), sem("cos_sin")
        s_kr, s_kn, s_vm = sem("rotary_key"), sem("key_bank_read"), sem("value_bank_read")
        s_qn, s_qr, s_sc = sem("query_bank_read"), sem("rotary_query"), sem("mla_scores")
        s_scr, s_pexp, s_pn = sem("scores_masked"), sem("scores_exp"), sem("probabilities")
        s_pt, s_ptr, s_pv = sem("probabilities_transposed"), sem("transposes_read"), sem("mla_head")
        s_mxx = sem("scores_max")

        def act_latent(act, l0, n):
            for j in range(n):
                act.wait_ge(s_lt, l0 + j + 1)
                nc.scalar.activation(lhi[:, j], T[:, j], ACT.Copy).then_inc(s_lhi, 1)

        def dve_latent(dve, l0, n, norm, g, srcs):
            dve.wait_ge(s_rstd, norm + 1)
            for j in range(n):
                nc.vector.scalar_tensor_tensor(out=T[:, j], in0=srcs[j], scalar=col(g, j), in1=rs(norm),
                                               op0=ALU.mult, op1=ALU.mult).then_inc(s_lt, 1)
            for j in range(n):
                dve.wait_ge(s_lhi, l0 + j + 1)
                nc.vector.tensor_tensor(llo[:, j], T[:, j], lhi[:, j].bitcast(f32), ALU.subtract).then_inc(s_l, 1)

        def dve_rope(dve, first, second, x1, x2, s_done):
            pair = len(first.shape) == 3
            cos, sin = [rd[:, n:n + 1].to_broadcast([P, 2, SEQ]) if pair else rd[:, n] for n in range(2)]
            part = SG[:, 0:2] if pair else CG[:]
            for out, a, b, op in ((first, cos, sin, ALU.subtract), (second, sin, cos, ALU.add)):
                nc.vector.tensor_tensor(out, x1, a, ALU.mult)
                link(dve, nc.vector.tensor_tensor(part, x2, b, ALU.mult))
                ins = nc.vector.tensor_tensor(out, out, part, op)
                if out is first:
                    link(dve, ins)
            ins.then_inc(s_done, 1)

        def act_kv_norm(act):
            act.wait_ge(s_ang, 1)
            nc.scalar.activation(rd[:], SG[:, 0:2], ACT.Sin).then_inc(s_cs, 1)
            act_squares(act, N_KV, lambda j: X[:, j])

        def act_kv_input(act):
            act_rstd(act, N_KV, D)
            act_modulate(act, mcol(M_KV), "kv")

        def dve_kv_input(dve):
            dve_coef_pre(dve, 5, M_KV + DT, col("kv_g", 0, DT))
            dve.wait_ge(s_pe, C_FFN[3] + FT)
            dve_modulate(dve, N_KV, cq(5), mcol(M_KV), "kv")

        def dve_angles(dve, n):
            TURN = 2 * np.pi
            C1 = 6.28125
            C2 = float(np.float32(np.round((TURN - C1) * 2 ** 20) / 2 ** 20))
            C3 = TURN - C1 - C2
            if n == 0:
                dve.wait_ge(s_pos, 16)
                link(dve, nc.vector.tensor_copy(SG[:, 2], CG[:].bitcast(i32)))
                link(dve, nc.vector.tensor_scalar(SG[:, 2], SG[:, 2], col("invf"), None, ALU.mult))
            link(dve, nc.vector.tensor_scalar(CG[:], SG[:, 2], 1 / TURN, (0.25, 0.0)[n], ALU.mult, ALU.add))
            link(dve, nc.vector.tensor_scalar(CG[:], CG[:], 1.5 * 2 ** 23, None, ALU.add))
            link(dve, nc.vector.tensor_scalar(CG[:], CG[:], -1.5 * 2 ** 23, None, ALU.add))
            src = SG[:, 2]
            for part in (C1, C2, C3):
                link(dve, nc.vector.scalar_tensor_tensor(out=SG[:, n], in0=CG[:], scalar=-part, in1=src,
                                                         op0=ALU.mult, op1=ALU.add))
                src = SG[:, n]
            if n == 0:
                link(dve, nc.vector.tensor_scalar(SG[:, 0], SG[:, 0], TURN / 4, None, ALU.add))
            else:
                pi = float(np.nextafter(np.float32(np.pi), np.float32(0)))
                nc.vector.tensor_scalar(flat(SG[:, 0:2]), flat(SG[:, 0:2]), pi, -pi, ALU.min, ALU.max)\
                    .then_inc(s_ang, 1)

        VALUE_BANKS = ((0, 0, 4), (0, 1, 6), (1, 0, 7), (1, 1, 5))

        def pe_kv(pe):
            c = C_KV
            pe_pair(pe, c, 4, wait=U["kv"], between=lambda: pe_stat(pe, N_F3P))
            pe_pair(pe, c + 1, 5, between=lambda: pe_stat(pe, N_KVL))
            pe_stat(pe, N_MLA)
            pe.wait_ge(s_lo, c + 3)
            pe.wait_ge(s_l, 2)
            pe.wait_ge(s_x, XU["f3"] + DT)
            for m in range(MLA_HEADS):
                for k in range(2):
                    ins = mm3(down(m), c + 2, 2 * m + k, lhi[:, k], llo[:, k], m % 2 == 0 and k == 0)
            ins.then_inc(s_pe, 1)
            pe.wait_ge(s_lo, c + 4)
            sl = (c + 3) % 3
            for n, (t, half, b) in enumerate(VALUE_BANKS):
                if b == 5:
                    pe.wait_ge(s_kr, 1)
                if b == 7:
                    pe.wait_ge(s_ln, N_MLA + 1)
                for k in range(2):
                    w = slice(k * D + half * 512, k * D + half * 512 + 512)
                    tt = slice(t * P, (t + 1) * P)
                    mm(bank[b][:], lhi[:, k, tt], whi[:, sl, w], k == 0)
                    mm(bank[b][:], lhi[:, k, tt], wlo[:, sl, w], False)
                    ins = mm(bank[b][:], llo[:, k, tt], whi[:, sl, w], False)
            ins.then_inc(s_pe, 1)

        def act_kv(act):
            c = C_KV
            act_squares(act, N_KVL, lambda j: bank[4][:, j * SEQ:(j + 1) * SEQ], lambda j: (s_pe, c + 1), False)
            act_split(act, c + 2)
            act_rstd(act, N_KVL, 256)
            act_squares(act, N_MLA, lambda j: X[:, j], x_ready(XU["f3"]), False)
            act_latent(act, 0, 2)
            act_split(act, c + 3)
            act_rstd(act, N_MLA, D)
            act_split(act, c + 4)
            act_modulate(act, mcol(M_COND[1] + 3 * DT), "mla")
            act.wait_ge(s_pe, c + 3)
            for b in (1, 3):
                nc.scalar.activation(flat(KN[:, 2 * b:2 * b + 2]), bank[b][:], ACT.Copy).then_inc(s_kn, 1)
            act_split(act, c + 5)
            act.wait_ge(s_pe, c + 4)
            for t, half, b in VALUE_BANKS[1::2]:
                nc.scalar.activation(VM[:, t, half * 512:(half + 1) * 512], bank[b][:], ACT.Copy).then_inc(s_vm, 1)

        def dve_kv(dve):
            c, m0 = C_KV, M_COND[1] + 3 * DT
            dve.wait_ge(s_x, XU["f3"] + DT)
            dve_latent(dve, 0, 2, N_KVL, "g_kv", [bank[4][:, 0:SEQ], bank[4][:, SEQ:]])
            dve_split(dve, c + 2)
            dve_coef_pre(dve, 3, m0 + DT, ng(1, 1, 0))
            dve_coef_post(dve, 4, m0 + 2 * DT, ng(1, 1, 1), 1.0)
            dve.wait_ge(s_cs, 1)
            dve.wait_ge(s_pe, c + 2)
            dve_rope(dve, KR[:, 0], KR[:, 1], bank[5][:, 0:SEQ], bank[5][:, SEQ:], s_kr)
            dve_split(dve, c + 3)
            dve_split(dve, c + 4)
            dve.wait_ge(s_pe, c + 3)
            for b in (0, 2):
                nc.vector.tensor_copy(flat(KN[:, 2 * b:2 * b + 2]), bank[b][:]).then_inc(s_kn, 1)
            dve_modulate(dve, N_MLA, cq(3), mcol(m0), "mla")
            dve_split(dve, c + 5)
            dve.wait_ge(s_pe, c + 4)
            for t, half, b in VALUE_BANKS[0::2]:
                nc.vector.tensor_copy(VM[:, t, half * 512:(half + 1) * 512], bank[b][:]).then_inc(s_vm, 1)

        def mla_out(h):
            return bank[h % 4][:, (h // 4) * SEQ:(h // 4 + 1) * SEQ]

        def pe_mla(pe):
            c = C_MLA
            pe.wait_ge(s_kn, 2)
            pe_pair(pe, c, 0, wait=U["mla"])
            pe.wait_ge(s_lo, c + 2)
            for k in range(DT):
                ins = mm3(bank[2][:, 0:SEQ], c + 1, k, hhi[:, k], hlo[:, k], k == 0)
            ins.then_inc(s_q2, 1)
            pe.wait_ge(s_vm, 4)
            pe.wait_ge(s_kn, 4)
            pe_stat(pe, N_QL)
            pe.wait_ge(s_l, 5)
            outs = [bank[6][:, 0:SEQ], bank[6][:, SEQ:], bank[4][:, 0:SEQ], bank[4][:, SEQ:]] + \
                [down(m) for m in range(8)]
            m = 0
            for j, (s0, count) in enumerate(((8, 2), (0, 5), (0, 5))):
                pe.wait_ge(s_lo, c + 2 + j)
                for n in range(count):
                    for k in range(3):
                        ins = mm3(outs[m], c + 1 + j, s0 + 3 * n + k, lhi[:, k], llo[:, k], m % 2 == 0 and k == 0)
                    m += 1
                ins.then_inc(s_pe, 1)
            score_banks = (5, 4)

            def scores(h):
                b = bank[score_banks[h % 2]]
                pe.wait_ge(s_qn, h // 2 + 1)
                if h >= 2:
                    pe.wait_ge(s_scr, h - 1)
                for qb in range(2):
                    w = P * (qb + 1)
                    o = b[:, qb * P:qb * P + w]
                    qq = slice(qb * P, qb * P + P)
                    mm(o, QN[:, h, qq], KN[:, h, 0:w], qb == 0)
                    mm(o, QR[:, 0, h // 4, qq], KRM[:, h % 4, 0, 0:w], False)
                    ins = mm(o, QR[:, 1, h // 4, qq], KRM[:, h % 4, 1, 0:w], False)
                ins.then_inc(s_sc, 1)

            pe.wait_ge(s_qr, 1)

            def transposes(h):
                pe.wait_ge(s_pn, h + 1)
                if h:
                    pe.wait_ge(s_ptr, h)
                for n in range(3):
                    ins = nc.tensor.transpose(bank[6][:, n * P:(n + 1) * P], SC[:, h % 2, n * P:(n + 1) * P], ident)
                ins.then_inc(s_pt, 1)

            def values(h):
                pe.wait_ge(s_ptr, h + 1)
                pe.wait_ge(s_qn, h % 4 + 1)
                if h >= 4:
                    pe.wait_ge(s_h, U["mla_y"] + h - 3)
                o, v = mla_out(h), lambda t: VM[:, t, h * P:(h + 1) * P]
                mm(o[:, 0:P], v(0), PT[:, h % 2, 0:P], True)
                mm(o[:, P:], v(0), PT[:, h % 2, P:2 * P], False)
                mm(o[:, P:], v(1), PT[:, h % 2, 2 * P:], False).then_inc(s_pv, 1)

            scores(0)
            scores(1)
            for h in range(MLA_HEADS):
                transposes(h)
                if h + 2 < MLA_HEADS:
                    scores(h + 2)
                if h:
                    values(h - 1)
            values(MLA_HEADS - 1)
            pe.wait_ge(s_h, U["mla_y"] + MLA_HEADS)
            for j in range(4):
                pe.wait_ge(s_lo, c + 5 + j)
                pe_down_chunk(pe, c + 4 + j, [hhi[:, 2 * j], hhi[:, 2 * j + 1]], [hlo[:, 2 * j], hlo[:, 2 * j + 1]],
                              j == 0, j == 3)
            pe_stat(pe, N_MPOST)

        s_q2 = sem("query_latent_ready")

        def act_mla(act):
            c = C_MLA
            act_split(act, c + 2)
            act_squares(act, N_QL, lambda j: (bank[0][:, 0:SEQ], bank[0][:, SEQ:], bank[2][:, 0:SEQ])[j],
                        lambda j: (s_q2, 1))
            act_rstd(act, N_QL, Q_LORA)
            act_latent(act, 2, 3)
            act_split(act, c + 3)
            for b in range(4):
                if b < 2:
                    act_split(act, c + 4 + b)
                act.wait_ge(s_pe, c + 3 + (b > 0))
                nc.scalar.activation(flat(QN[:, 2 * b:2 * b + 2]), bank[b][:], ACT.Copy).then_inc(s_qn, 1)

            def round_head(h):
                act.wait_ge(s_pv, h + 1)
                nc.scalar.activation(hhi[:, h], mla_out(h), ACT.Copy).then_inc(s_hhi, 1)

            def exponentials(h):
                act.wait_ge(s_mxx, h + 1)
                for qb in range(2):
                    s = SC[:, h % 2, qb * P:qb * P + P * (qb + 1)]
                    ins = nc.scalar.activation(s, s, ACT.Exp, bias=mx[:, h % 2, qb:qb + 1],
                                               accum_out=sm[:, h % 2, qb:qb + 1])
                ins.then_inc(s_pexp, 1)

            exponentials(0)
            for h in range(MLA_HEADS):
                if h + 1 < MLA_HEADS:
                    exponentials(h + 1)
                act.wait_ge(s_pt, h + 1)
                if h >= 2:
                    act.wait_ge(s_pv, h - 1)
                nc.scalar.activation(PT[:, h % 2], bank[6][:, 0:3 * P], ACT.Copy).then_inc(s_ptr, 1)
                if h >= 2:
                    round_head(h - 2)
            for h in range(MLA_HEADS - 2, MLA_HEADS):
                round_head(h)
            for j in range(4, 8):
                act_split(act, c + j + 2)
            act_squares(act, N_MPOST, down, lambda j: down_done(OUTS["mla"], j, c + 7))
            act_rstd(act, N_MPOST, D)

        def dve_mla(dve):
            c = C_MLA
            dve_split(dve, c + 2)
            dve_latent(dve, 2, 3, N_QL, "g_q", [bank[0][:, 0:SEQ], bank[0][:, SEQ:], bank[2][:, 0:SEQ]])
            link(dve, nc.vector.memset(KRM[:], 0.0))
            for h in range(4):
                rows = slice(32 * h, 32 * h + 32)
                ins = nc.vector.tensor_copy(KRM[rows, h], KR[rows])
            ins.then_inc(s_kr, 1)
            for j in range(1, 4):
                dve_split(dve, c + j + 2)
                if j == 1:
                    dve.wait_ge(s_pe, c + 3)
                    halves = [bank[b][:].rearrange("p (g t) -> p g t", g=2) for b in (6, 4)]
                    dve_rope(dve, QR[:, 0], QR[:, 1], *halves, s_qr)

            def softmax(h):
                dve.wait_ge(s_sc, h + 1)
                if h >= 2:
                    dve.wait_ge(s_pt, h - 1)
                s = SC[:, h % 2]
                nc.vector.scalar_tensor_tensor(out=s, in0=bank[(5, 4)[h % 2]][:, 0:3 * P], scalar=(P + ROPE) ** -0.5,
                                               in1=cst("amask"), op0=ALU.mult, op1=ALU.add).then_inc(s_scr, 1)
                dve.wait_ge(s_scr, h + 1)
                for qb in range(2):
                    ins = nc.vector.tensor_reduce(mx[:, h % 2, qb:qb + 1], SC[:, h % 2, qb * P:qb * P + P * (qb + 1)],
                                                  AX.X, ALU.max)
                link(dve, ins)
                nc.vector.tensor_scalar(mx[:, h % 2], mx[:, h % 2], -1.0, None, ALU.mult).then_inc(s_mxx, 1)

            def rest_head(h):
                dve.wait_ge(s_hhi, U["mla_y"] + h + 1)
                nc.vector.tensor_tensor(hlo[:, h], mla_out(h), hhi[:, h].bitcast(f32), ALU.subtract).then_inc(s_h, 1)

            softmax(0)
            for h in range(MLA_HEADS):
                if h + 1 < MLA_HEADS:
                    softmax(h + 1)
                dve.wait_ge(s_pexp, h + 1)
                link(dve, nc.vector.reciprocal(sm[:, h % 2], sm[:, h % 2]))
                for qb in range(2):
                    s = SC[:, h % 2, qb * P:qb * P + P * (qb + 1)]
                    ins = nc.vector.tensor_scalar(s, s, sm[:, h % 2, qb:qb + 1], None, ALU.mult)
                ins.then_inc(s_pn, 1)
                if h >= 2:
                    rest_head(h - 2)
            for h in range(MLA_HEADS - 2, MLA_HEADS):
                rest_head(h)
            for j in range(4, 8):
                dve_split(dve, c + j + 2)
            dve_add_post(dve, N_MPOST, 4, XU["mla"])

        def pe_rest(pe):
            pe_swiglu(pe, 1)
            pe_gla(pe)
            pe_swiglu(pe, 2)
            pe_swiglu(pe, 3)
            pe_kv(pe)
            pe_mla(pe)
            pe_swiglu(pe, 4)

        def act_rest(act):
            act_swiglu(act, 1)
            act_gla(act)
            act_swiglu(act, 2)
            act_swiglu(act, 3)
            act_kv(act)
            act_mla(act)
            act_swiglu(act, 4)

        def dve_rest(dve):
            dve_swiglu(dve, 1)
            dve_gla(dve)
            dve_swiglu(dve, 2)
            dve_swiglu(dve, 3)
            dve_kv(dve)
            dve_mla(dve)
            dve_swiglu(dve, 4)

        @block.tensor
        def _(pe):
            pe_lstm(pe)
            pe_stat(pe, N_F0)
            pe_ffn(pe, 0, U["f0"])
            pe_stat(pe, N_FIN)
            pe_rest(pe)

        @block.scalar
        def _(act):
            act_lstm(act)
            act_squares(act, N_F0, lambda j: X[:, j], x_ready(XU["lstm"]))
            act_rstd(act, N_F0, D)
            act_modulate(act, mcol(24), "f0")
            act.wait_ge(s_c2, 16)
            nc.scalar.activation(cb2[:], cb2[:], ACT.Silu).then_inc(s_cb, 1)
            act_ffn(act, 0)
            act_squares(act, N_FIN, lambda j: X[:, j], x_ready(XU["f0"]))
            act_rstd(act, N_FIN, D)
            act_rest(act)

        @block.vector
        def _(dve):
            dve_lstm(dve)
            dve_coef_pre(dve, 2, 32, col("g_ffn", 0, 8))
            dve_modulate(dve, N_F0, cq(2), mcol(24), "f0")
            dve.wait_ge(s_cb, 2)
            dve_ffn(dve, 0)
            after_units(dve, UNITS[0], UNITS[1])
            dve_add_plain(dve, 40, 1, C_FFN[0] + FFN_CHUNKS - 1)
            dve.wait_ge(s_rstd, N_FIN + 1)
            for j in range(DT):
                nc.vector.scalar_tensor_tensor(out=X[:, j], in0=X[:, j], scalar=col("g_final", j), in1=rs(N_FIN),
                                               op0=ALU.mult, op1=ALU.mult).then_inc(s_x, 1)
            dve_rest(dve)


def _feature_cols(a):
    import numpy as np
    return np.asarray(a).reshape(-1, P).T


def _tiles(w):
    k, m = w.shape
    return w.reshape(k // P, P, m // P, P).transpose(1, 2, 0, 3)


def _by_output(w):
    return _tiles(w).reshape(P, -1, CW).transpose(1, 0, 2)


def _by_input(w):
    return _tiles(w).transpose(0, 2, 1, 3).reshape(P, -1, CW).transpose(1, 0, 2)


def _wide(w):
    k, m = w.shape
    return w.reshape(k // P, P, m // 512, 512).transpose(1, 2, 0, 3).reshape(P, -1, CW).transpose(1, 0, 2)


def _up_pairs(w):
    k = w.shape[0]
    t = _tiles(w).reshape(P, 2, FT, k // P, P)
    return t.transpose(0, 2, 1, 3, 4).reshape(P, FT, CW).transpose(1, 0, 2)


def _padded(a, width):
    import numpy as np
    out = np.zeros(a.shape[:-1] + (width,), a.dtype)
    out[..., :a.shape[-1]] = a
    return out


def _constants():
    import numpy as np
    con = np.zeros((P, N_CONST), np.float32)

    def put(name, a):
        at, w = CON[name]
        con[:a.shape[0], at:at + w] = a.reshape(a.shape[0], -1)

    put("ident", np.eye(P, dtype=np.float32))
    put("ones", np.ones((P, P), np.float32))
    sel = np.zeros((36, 8, P), np.float32)
    for d in range(2):
        for h in range(4):
            sel[32 * d + h, d * 4 + h] = 1
    put("sel", sel)
    s, t = np.arange(P)[:, None], np.arange(SEQ)[None, :]
    no = np.float32(-1e30)
    madd = np.zeros((P, 2, 2, SEQ), np.float32)
    for st in range(2):
        madd[:, 0, st] = np.where(s + P * st <= t, 0, no)
        madd[:, 1, st] = np.where(s + P * st >= t, 0, no)
    put("madd", madd)
    put("reset", np.broadcast_to((np.arange(SEQ) % CHUNK != 0).astype(np.float32), (P, SEQ)))
    i = np.arange(P)[None, :]
    causal = ((s <= i) & (s // CHUNK == i // CHUNK)).astype(np.float32)
    put("causal", np.concatenate([causal, causal], axis=1))
    put("amask", np.concatenate([np.where(i <= s, 0, no), np.zeros((P, P)), np.where(i <= s, 0, no)], axis=1))
    return con


def kernel(**inputs):
    import numpy as np
    import concourse.bacc as bacc
    from concourse.bass_utils import run_bass_kernel_spmd as run

    v = {k: np.asarray(a) for k, a in inputs.items()}
    w_in, w_gla = v["a_w_in"][0], v["gla_w_in_2"][0]
    gates = w_in[:, 3072:]
    wg = np.zeros((D, P), np.float32)
    b_gate = np.zeros((P, 1), np.float32)
    for n, row in enumerate((0, 32, 64, 96)):
        wg[:, row:row + HEADS] = gates[:, n * HEADS:(n + 1) * HEADS]
        b_gate[row:row + HEADS, 0] = v["a_b_gate"][0, n * HEADS:(n + 1) * HEADS]
    kv_a, kv_b = v["mla_w_kv_a_2"], v["mla_w_kv_b_2"].reshape(256, MLA_HEADS, 2, P)
    pe = [kv_a[:, 256 + 32 * n:288 + 32 * n] for n in range(2)]
    uq = v["mla_w_uq_2"][0].reshape(Q_LORA, MLA_HEADS, P + ROPE)
    uq = np.concatenate([uq[:, :, P:P + 32].reshape(Q_LORA, -1), uq[:, :, P + 32:].reshape(Q_LORA, -1),
                         uq[:, :, :P].reshape(Q_LORA, -1)], axis=1)
    uq = _tiles(uq).reshape(P, 12, 3 * P)
    dq = _tiles(v["mla_w_dq_2"][0]).reshape(P, 3, DT * P)
    gu, dn = v["ffn_w_gu_2"], v["ffn_w_down_2"]

    def ffn(up, down):
        return [_up_pairs(up), _by_input(down)]

    w_mod = v["w_mod"][0]
    stream = [w_mod[:, :FIRST_MODS * P].reshape(DT, P, CW), _by_output(w_in[:, :512]),
              _padded(_tiles(wg).reshape(P, -1), CW)[None], _by_output(w_in[:, 512:1024]),
              _wide(w_in[:, 1024:2048]), _by_output(w_in[:, 2048:3072]), _by_input(v["a_w_out"][0]),
              *ffn(v["f_w_up"][0], v["f_w_down"][0]), *ffn(gu[0, 0], dn[0, 0]),
              _padded(_tiles(_padded(w_gla[:, 2048:2064], P)).reshape(P, -1), CW)[None],
              _by_output(w_gla[:, :1024]), _wide(w_gla[:, 1024:2048]), _by_output(w_gla[:, 2064:]),
              _by_input(v["gla_w_out_2"][0]), *ffn(gu[0, 1], dn[0, 1]), *ffn(gu[1, 0], dn[1, 0]),
              _by_output(np.concatenate([kv_a[:, :256]] + [pe[0]] * 4 + [pe[1]] * 4, axis=1)),
              _by_output(kv_b[:, :, 0].reshape(256, -1)),
              kv_b[:, :, 1].reshape(2, P, D).transpose(1, 0, 2).reshape(1, P, CW),
              dq[:, :2].reshape(1, P, CW),
              _padded(np.concatenate([dq[:, 2], uq[:, :2].reshape(P, -1)], axis=1), CW)[None],
              _padded(uq[:, 2:7].reshape(P, -1), CW)[None], _padded(uq[:, 7:].reshape(P, -1), CW)[None],
              _by_input(v["mla_w_out_2"][0]), *ffn(gu[1, 1], dn[1, 1])]
    w_stream = np.ascontiguousarray(np.concatenate(stream, axis=0))
    assert w_stream.shape == (N_CHUNKS, P, CW)
    rows = np.concatenate([w_mod[:, FIRST_MODS * P:].T, v["cond_w_2"][0].T, v["kv_cond_w_2"].T, v["cond_w_2"][1].T])
    invf = (10000.0 ** (-np.arange(0, ROPE, 2, dtype=np.float32) / np.float32(ROPE))).astype(np.float32)
    cw = v["f_w_conv"][0]
    cols = np.concatenate([_feature_cols(a) for a in (
        v["b_mod"][0], v["cond_b_2"][0], v["kv_cond_b_2"], v["cond_b_2"][1], v["g_mix"][0], v["g_ffn"][0],
        v["g_final"], v["a_head_gain"][0], cw[0], cw[1], cw[2], v["f_b_conv"][0], v["norm_g_2"].reshape(-1),
        v["kv_g_in_2"], v["gla_g_out_2"][0], v["gla_b_gate_2"][0], v["mla_g_kv_2"], v["mla_g_q_2"][0], b_gate,
        np.tile(invf, 4))], axis=1)

    def features(x):
        return x.reshape(SEQ, DT, P).transpose(2, 1, 0)

    data = {
        "w_stream": w_stream, "m_stream": rows.reshape(-1, P, D), "w_gup": v["gla_w_gate_up_2"][0],
        "xT": features(v["x"]), "ctxT": features(v["ctx"]),
        "c_cols": np.stack([_feature_cols(v["c"]), _feature_cols(v["c_ctx"])], axis=2),
        "c_row": v["c"].reshape(D), "c2_row": v["c_2"].reshape(D), "cols_d": cols, "const_d": _constants(),
        "pos_d": v["positions_2"].reshape(SEQ),
    }
    nc = bacc.Bacc("TRN2", target_bir_lowering=False, num_devices=1)
    dt, arrays, args = mybir.dt, {}, {}
    for name, a in data.items():
        a = np.ascontiguousarray(a)
        arrays[name] = a
        args[name] = nc.dram_tensor(name, a.shape, dt.int32 if a.dtype.kind == "i" else dt.float32,
                                    kind="ExternalInput").ap()
    out = nc.dram_tensor("y", (P, DT, SEQ), dt.float32, kind="ExternalOutput").ap()
    build(nc, **args, out_d=out)
    y = run(nc, [arrays], core_ids=[0]).results[0]["y"]
    return np.ascontiguousarray(np.asarray(y).transpose(2, 1, 0)).reshape(1, SEQ, D)
```
